# Optimizing a Trainium2 kernel written in Bass

```python
import jax, jax.numpy as jnp
from jax import lax
import numpy as np
import math

D_MODEL = 1024
BATCH = 1
SEQ = 256
DEPTH = 2

CTX_LEN = 256
GRID_W = 64
D_FF = 2816
N_MOD = 9
EPS = 1e-6
ROPE_BASE = 10000.0
Q_BLOCK = 128
MLA_HEADS = 8
MLA_NOPE = 64
MLA_ROPE = 32
MLA_V = 64
MLA_Q_LORA = 384
MLA_KV_LORA = 256
CONV_CH = 512
CONV_WIDTH = 31
HEAD_DIM = 64
GQA_HEADS = 8
GQA_KV_HEADS = 2
NA_HEADS = 8
WIN_H = 8
WIN_W = 16

EVEN_KV_COLS = MLA_KV_LORA + MLA_ROPE
EVEN_CONV_OFF = EVEN_KV_COLS + MLA_Q_LORA
EVEN_COLS = EVEN_CONV_OFF + 2 * CONV_CH
GQA_KV_W = GQA_KV_HEADS * HEAD_DIM
GQA_Q_W = GQA_HEADS * HEAD_DIM
NA_W = NA_HEADS * HEAD_DIM
ODD_KV_COLS = 2 * GQA_KV_W + 2 * NA_W
ODD_COLS = ODD_KV_COLS + GQA_Q_W + NA_W
MIX_OUT = MLA_HEADS * MLA_V + CONV_CH


def rms_norm(x, g):
    xf = x.astype(jnp.float32)
    y = xf * lax.rsqrt(jnp.mean(xf * xf, axis=-1, keepdims=True) + EPS)
    return (y * g.astype(jnp.float32)).astype(x.dtype)

def layer_norm(x, g, b):
    xf = x.astype(jnp.float32)
    mu = jnp.mean(xf, axis=-1, keepdims=True)
    var = jnp.mean(jnp.square(xf - mu), axis=-1, keepdims=True)
    y = (xf - mu) * lax.rsqrt(var + EPS)
    return (y * g.astype(jnp.float32) + b.astype(jnp.float32)).astype(x.dtype)

def axial_rope_table(n_tokens, dim):
    t = jnp.arange(n_tokens)
    row = (t // GRID_W).astype(jnp.float32)
    col = (t % GRID_W).astype(jnp.float32)
    n_pairs = dim // 4
    inv = ROPE_BASE ** (-jnp.arange(n_pairs, dtype=jnp.float32) / n_pairs)
    ang = jnp.concatenate([row[:, None] * inv, col[:, None] * inv], axis=-1)
    return jnp.cos(ang), jnp.sin(ang)

def apply_rope(x, cos, sin):
    xp = x.reshape(*x.shape[:-1], x.shape[-1] // 2, 2)
    x1, x2 = xp[..., 0], xp[..., 1]
    cs = cos[None, :, None, :].astype(x.dtype)
    sn = sin[None, :, None, :].astype(x.dtype)
    return jnp.stack([x1 * cs - x2 * sn, x1 * sn + x2 * cs], axis=-1).reshape(x.shape)

def _attend(q, k, v):
    scale = q.shape[-1] ** -0.5
    s = jnp.einsum('bqhgd,bkhd->bhgqk', q, k).astype(jnp.float32) * scale
    p = jax.nn.softmax(s, axis=-1).astype(v.dtype)
    return jnp.einsum('bhgqk,bkhd->bqhgd', p, v)

def context_attention(q, k, v):
    B, L, Hk, G, _ = q.shape
    return _attend(q, k, v).reshape(B, L, Hk * G, v.shape[-1])

def latent_attention(q, k, v, k_ctx, v_ctx):
    B, S, Hk, G, d = q.shape
    k_all = jnp.concatenate([k_ctx, k], axis=1)
    v_all = jnp.concatenate([v_ctx, v], axis=1)
    qb = q.reshape(B, S // Q_BLOCK, Q_BLOCK, Hk, G, d).transpose(1, 0, 2, 3, 4, 5)
    o = lax.map(lambda qi: _attend(qi, k_all, v_all), qb)
    return o.transpose(1, 0, 2, 3, 4, 5).reshape(B, S, Hk * G, v.shape[-1])

def neighbourhood_attention(q, k, v, k_ctx, v_ctx, rpb):
    B, S, H, d = q.shape
    rows = S // GRID_W
    kh = min(WIN_H, rows)
    scale = d ** -0.5
    qg = q.reshape(B, rows, GRID_W, H, d).transpose(1, 0, 2, 3, 4)
    kg = k.reshape(B, rows, GRID_W, H, d)
    vg = v.reshape(B, rows, GRID_W, H, d)
    col = jnp.arange(GRID_W)
    cs = jnp.clip(col - WIN_W // 2, 0, GRID_W - WIN_W)
    col_idx = cs[:, None] + jnp.arange(WIN_W)[None, :]
    dc = col_idx - col[:, None] + (WIN_W - 1)
    n_ctx = k_ctx.shape[1]

    def row_block(args):
        r, q_r = args
        rs = jnp.clip(r - kh // 2, 0, rows - kh)
        k_rows = lax.dynamic_slice_in_dim(kg, rs, kh, axis=1)
        v_rows = lax.dynamic_slice_in_dim(vg, rs, kh, axis=1)
        k_nb = k_rows[:, :, col_idx]
        v_nb = v_rows[:, :, col_idx]
        s_nb = jnp.einsum('bqhd,bjqwhd->bhqjw', q_r, k_nb).astype(jnp.float32) * scale
        dr = rs + jnp.arange(kh) - r + (WIN_H - 1)
        bias = rpb[:, dr[None, :, None], dc[:, None, :]]
        s_nb = (s_nb + bias[None].astype(jnp.float32)).reshape(B, H, GRID_W, kh * WIN_W)
        s_ctx = jnp.einsum('bqhd,bkhd->bhqk', q_r, k_ctx).astype(jnp.float32) * scale
        p = jax.nn.softmax(jnp.concatenate([s_ctx, s_nb], axis=-1), axis=-1).astype(v.dtype)
        p_ctx = p[..., :n_ctx]
        p_nb = p[..., n_ctx:].reshape(B, H, GRID_W, kh, WIN_W)
        return (jnp.einsum('bhqk,bkhd->bqhd', p_ctx, v_ctx)
                + jnp.einsum('bhqjw,bjqwhd->bqhd', p_nb, v_nb))

    o = lax.map(row_block, (jnp.arange(rows), qg))
    return o.transpose(1, 0, 2, 3, 4).reshape(B, S, H, d)

def swiglu(h, w_in, w_out):
    g, u = jnp.split(h @ w_in, 2, axis=-1)
    return (jax.nn.silu(g) * u) @ w_out

def conv_module(u, prm):
    u = u + prm["conv_glu_b"]
    a, g = jnp.split(u, 2, axis=-1)
    y = a * jax.nn.sigmoid(g)
    y = lax.conv_general_dilated(
        y, prm["conv_dw_w"][:, None, :].astype(y.dtype), window_strides=(1,),
        padding=[(CONV_WIDTH // 2, CONV_WIDTH // 2)],
        dimension_numbers=("NWC", "WIO", "NWC"), feature_group_count=CONV_CH) + prm["conv_dw_b"]
    y = layer_norm(y, prm["conv_ln_g"], prm["conv_ln_b"])
    return jax.nn.silu(y)

def mla_kv(pp, prm, rope):
    B, L, _ = pp.shape
    ckv = rms_norm(pp[..., :MLA_KV_LORA], prm["mla_kv_norm"])
    kvu = (ckv @ prm["mla_w_ukv"]).reshape(B, L, MLA_HEADS, MLA_NOPE + MLA_V)
    k_nope = rms_norm(kvu[..., :MLA_NOPE], prm["mla_k_gain"][:MLA_NOPE])
    v = kvu[..., MLA_NOPE:]
    k_rope = rms_norm(pp[..., MLA_KV_LORA:EVEN_KV_COLS], prm["mla_k_gain"][MLA_NOPE:])[:, :, None, :]
    if rope is not None:
        k_rope = apply_rope(k_rope, *rope)
    k = jnp.concatenate([k_nope, jnp.broadcast_to(k_rope, (B, L, MLA_HEADS, MLA_ROPE))], axis=-1)
    return k, v

def mla_q(pp, prm, rope):
    B, L, _ = pp.shape
    cq = rms_norm(pp[..., EVEN_KV_COLS:EVEN_CONV_OFF], prm["mla_q_norm"])
    q = (cq @ prm["mla_w_uq"]).reshape(B, L, MLA_HEADS, MLA_NOPE + MLA_ROPE)
    q_nope = rms_norm(q[..., :MLA_NOPE], prm["mla_q_gain"][:MLA_NOPE])
    q_rope = rms_norm(q[..., MLA_NOPE:], prm["mla_q_gain"][MLA_NOPE:])
    if rope is not None:
        q_rope = apply_rope(q_rope, *rope)
    return jnp.concatenate([q_nope, q_rope], axis=-1)[:, :, :, None, :]

def even_mixer(hl, hc, prm, ctx_out, ropes):
    rope_mla, _ = ropes
    B, S, _ = hl.shape
    pl = hl @ prm["w_in"]
    pc = hc @ (prm["w_in"] if ctx_out else prm["w_in"][:, :EVEN_KV_COLS])
    k_l, v_l = mla_kv(pl, prm, rope_mla)
    k_c, v_c = mla_kv(pc, prm, None)
    att_l = latent_attention(mla_q(pl, prm, rope_mla), k_l, v_l, k_c, v_c).reshape(B, S, -1)
    conv_l = conv_module(pl[..., EVEN_CONV_OFF:], prm)
    ol = jnp.concatenate([att_l, conv_l], axis=-1) @ prm["w_out"]
    oc = None
    if ctx_out:
        Bc, Lc, _ = hc.shape
        att_c = context_attention(mla_q(pc, prm, None), k_c, v_c).reshape(Bc, Lc, -1)
        conv_c = conv_module(pc[..., EVEN_CONV_OFF:], prm)
        oc = jnp.concatenate([att_c, conv_c], axis=-1) @ prm["w_out"]
    return ol, oc

def odd_kv(pp, prm, rope):
    B, L, _ = pp.shape
    o1, o2, o3 = GQA_KV_W, 2 * GQA_KV_W, 2 * GQA_KV_W + NA_W
    ck = rms_norm(pp[..., :o1].reshape(B, L, GQA_KV_HEADS, HEAD_DIM), prm["gqa_k_gain"])
    if rope is not None:
        ck = apply_rope(ck, *rope)
    cv = pp[..., o1:o2].reshape(B, L, GQA_KV_HEADS, HEAD_DIM)
    nk = rms_norm(pp[..., o2:o3].reshape(B, L, NA_HEADS, HEAD_DIM), prm["na_k_gain"])
    nv = pp[..., o3:ODD_KV_COLS].reshape(B, L, NA_HEADS, HEAD_DIM)
    return ck, cv, nk, nv

def odd_q(pp, prm, rope):
    B, L, _ = pp.shape
    cq = rms_norm(pp[..., ODD_KV_COLS:ODD_KV_COLS + GQA_Q_W].reshape(B, L, GQA_HEADS, HEAD_DIM), prm["gqa_q_gain"])
    if rope is not None:
        cq = apply_rope(cq, *rope)
    cq = cq.reshape(B, L, GQA_KV_HEADS, GQA_HEADS // GQA_KV_HEADS, HEAD_DIM)
    nq = rms_norm(pp[..., ODD_KV_COLS + GQA_Q_W:].reshape(B, L, NA_HEADS, HEAD_DIM), prm["na_q_gain"])
    return cq, nq

def odd_mixer(hl, hc, prm, ctx_out, ropes):
    _, rope_hd = ropes
    B, S, _ = hl.shape
    pl = hl @ prm["w_in"]
    pc = hc @ (prm["w_in"] if ctx_out else prm["w_in"][:, :ODD_KV_COLS])
    ck_l, cv_l, nk_l, nv_l = odd_kv(pl, prm, rope_hd)
    ck_c, cv_c, nk_c, nv_c = odd_kv(pc, prm, None)
    cq_l, nq_l = odd_q(pl, prm, rope_hd)
    gqa_l = latent_attention(cq_l, ck_l, cv_l, ck_c, cv_c).reshape(B, S, -1)
    na_l = neighbourhood_attention(nq_l, nk_l, nv_l, nk_c, nv_c, prm["na_rpb"]).reshape(B, S, -1)
    ol = jnp.concatenate([gqa_l, na_l], axis=-1) @ prm["w_out"]
    oc = None
    if ctx_out:
        Bc, Lc, _ = hc.shape
        cq_c, nq_c = odd_q(pc, prm, None)
        gqa_c = context_attention(cq_c, ck_c, cv_c).reshape(Bc, Lc, -1)
        na_c = context_attention(nq_c[:, :, :, None, :], nk_c, nv_c).reshape(Bc, Lc, -1)
        oc = jnp.concatenate([gqa_c, na_c], axis=-1) @ prm["w_out"]
    return ol, oc

def adaln(cond, prm):
    mod = jax.nn.silu(cond) @ prm["mod_w"] + prm["mod_b"]
    return jnp.split(mod, N_MOD, axis=-1)

def modulate(h, shift, scale):
    return h * (1.0 + scale) + shift

def trunk_layer(xl, xc, c, c_ctx, prm, even, ctx_out, ropes):
    mod_l = adaln(c[:, None, :], prm)
    mod_c = adaln(c_ctx[None, None, :], prm)

    def half_ffn(x, m, name):
        sh, sc, g = m
        h = modulate(rms_norm(x, prm[name + "_norm"]), sh, sc)
        return x + 0.5 * g * swiglu(h, prm[name + "_w_in"], prm[name + "_w_out"])

    xl = half_ffn(xl, mod_l[0:3], "ffn1")
    xc = half_ffn(xc, mod_c[0:3], "ffn1")
    hl = modulate(rms_norm(xl, prm["mix_norm"]), mod_l[3], mod_l[4])
    hc = modulate(rms_norm(xc, prm["mix_norm"]), mod_c[3], mod_c[4])
    mixer = even_mixer if even else odd_mixer
    ol, oc = mixer(hl, hc, prm, ctx_out, ropes)
    xl = xl + mod_l[5] * ol
    xl = half_ffn(xl, mod_l[6:9], "ffn2")
    if ctx_out:
        xc = xc + mod_c[5] * oc
        xc = half_ffn(xc, mod_c[6:9], "ffn2")
    return xl, xc

def _layer_params(key, i):
    ks = iter(jax.random.split(key, 32))

    def nrm(shape, scale):
        return jax.random.normal(next(ks), shape, jnp.float32) * scale

    def gain(n):
        return 1.0 + 0.02 * jax.random.normal(next(ks), (n,), jnp.float32)

    D = D_MODEL
    pre = f"l{i}_"
    p = {}
    p[pre + "mod_w"] = nrm((D, N_MOD * D), 0.5 * D ** -0.5)
    p[pre + "mod_b"] = nrm((N_MOD * D,), 0.02)
    p[pre + "ffn1_norm"] = gain(D)
    p[pre + "ffn1_w_in"] = nrm((D, 2 * D_FF), D ** -0.5)
    p[pre + "ffn1_w_out"] = nrm((D_FF, D), D_FF ** -0.5)
    p[pre + "mix_norm"] = gain(D)
    if i % 2 == 0:
        p[pre + "w_in"] = nrm((D, EVEN_COLS), D ** -0.5)
        p[pre + "mla_q_norm"] = gain(MLA_Q_LORA)
        p[pre + "mla_w_uq"] = nrm((MLA_Q_LORA, MLA_HEADS * (MLA_NOPE + MLA_ROPE)), MLA_Q_LORA ** -0.5)
        p[pre + "mla_kv_norm"] = gain(MLA_KV_LORA)
        p[pre + "mla_w_ukv"] = nrm((MLA_KV_LORA, MLA_HEADS * (MLA_NOPE + MLA_V)), MLA_KV_LORA ** -0.5)
        p[pre + "mla_q_gain"] = gain(MLA_NOPE + MLA_ROPE)
        p[pre + "mla_k_gain"] = gain(MLA_NOPE + MLA_ROPE)
        p[pre + "conv_glu_b"] = nrm((2 * CONV_CH,), 0.02)
        p[pre + "conv_dw_w"] = nrm((CONV_WIDTH, CONV_CH), CONV_WIDTH ** -0.5)
        p[pre + "conv_dw_b"] = nrm((CONV_CH,), 0.02)
        p[pre + "conv_ln_g"] = gain(CONV_CH)
        p[pre + "conv_ln_b"] = nrm((CONV_CH,), 0.02)
    else:
        p[pre + "w_in"] = nrm((D, ODD_COLS), D ** -0.5)
        p[pre + "gqa_q_gain"] = gain(HEAD_DIM)
        p[pre + "gqa_k_gain"] = gain(HEAD_DIM)
        p[pre + "na_q_gain"] = gain(HEAD_DIM)
        p[pre + "na_k_gain"] = gain(HEAD_DIM)
        p[pre + "na_rpb"] = nrm((NA_HEADS, 2 * WIN_H - 1, 2 * WIN_W - 1), 0.1)
    p[pre + "w_out"] = nrm((MIX_OUT, D), MIX_OUT ** -0.5)
    p[pre + "ffn2_norm"] = gain(D)
    p[pre + "ffn2_w_in"] = nrm((D, 2 * D_FF), D ** -0.5)
    p[pre + "ffn2_w_out"] = nrm((D_FF, D), D_FF ** -0.5)
    return p

def first_inputs(seed: int = 0) -> dict:
    key = jax.random.key(seed)
    k_x, k_c, k_ctx, k_cc, k_layers = jax.random.split(key, 5)
    inputs = {
        "x": jax.random.normal(k_x, (BATCH, SEQ, D_MODEL), jnp.float32),
        "c": jax.random.normal(k_c, (BATCH, D_MODEL), jnp.float32),
        "ctx": jax.random.normal(k_ctx, (BATCH, CTX_LEN, D_MODEL), jnp.float32),
        "c_ctx": jax.random.normal(k_cc, (D_MODEL,), jnp.float32),
    }
    layer_keys = jax.random.split(k_layers, DEPTH)
    for i in range(DEPTH):
        inputs.update(_layer_params(layer_keys[i], i))
    return inputs

def first_block(x, c, ctx, c_ctx,
              l0_mod_w, l0_mod_b, l0_ffn1_norm, l0_ffn1_w_in, l0_ffn1_w_out, l0_mix_norm, l0_w_in,
              l0_mla_q_norm, l0_mla_w_uq, l0_mla_kv_norm, l0_mla_w_ukv, l0_mla_q_gain, l0_mla_k_gain,
              l0_conv_glu_b, l0_conv_dw_w, l0_conv_dw_b, l0_conv_ln_g, l0_conv_ln_b,
              l0_w_out, l0_ffn2_norm, l0_ffn2_w_in, l0_ffn2_w_out,
              l1_mod_w, l1_mod_b, l1_ffn1_norm, l1_ffn1_w_in, l1_ffn1_w_out, l1_mix_norm, l1_w_in,
              l1_gqa_q_gain, l1_gqa_k_gain, l1_na_q_gain, l1_na_k_gain, l1_na_rpb,
              l1_w_out, l1_ffn2_norm, l1_ffn2_w_in, l1_ffn2_w_out):
    layers = (
        dict(mod_w=l0_mod_w, mod_b=l0_mod_b, ffn1_norm=l0_ffn1_norm, ffn1_w_in=l0_ffn1_w_in,
             ffn1_w_out=l0_ffn1_w_out, mix_norm=l0_mix_norm, w_in=l0_w_in,
             mla_q_norm=l0_mla_q_norm, mla_w_uq=l0_mla_w_uq, mla_kv_norm=l0_mla_kv_norm,
             mla_w_ukv=l0_mla_w_ukv, mla_q_gain=l0_mla_q_gain, mla_k_gain=l0_mla_k_gain,
             conv_glu_b=l0_conv_glu_b, conv_dw_w=l0_conv_dw_w, conv_dw_b=l0_conv_dw_b,
             conv_ln_g=l0_conv_ln_g, conv_ln_b=l0_conv_ln_b, w_out=l0_w_out,
             ffn2_norm=l0_ffn2_norm, ffn2_w_in=l0_ffn2_w_in, ffn2_w_out=l0_ffn2_w_out),
        dict(mod_w=l1_mod_w, mod_b=l1_mod_b, ffn1_norm=l1_ffn1_norm, ffn1_w_in=l1_ffn1_w_in,
             ffn1_w_out=l1_ffn1_w_out, mix_norm=l1_mix_norm, w_in=l1_w_in,
             gqa_q_gain=l1_gqa_q_gain, gqa_k_gain=l1_gqa_k_gain, na_q_gain=l1_na_q_gain,
             na_k_gain=l1_na_k_gain, na_rpb=l1_na_rpb, w_out=l1_w_out,
             ffn2_norm=l1_ffn2_norm, ffn2_w_in=l1_ffn2_w_in, ffn2_w_out=l1_ffn2_w_out),
    )
    S = x.shape[1]
    ropes = (axial_rope_table(S, MLA_ROPE), axial_rope_table(S, HEAD_DIM))
    xl, xc = x, ctx
    for i in range(DEPTH):
        xl, xc = trunk_layer(xl, xc, c, c_ctx, layers[i], even=(i % 2 == 0),
                             ctx_out=(i < DEPTH - 1), ropes=ropes)
    return xl


N_HEADS_DIFF = 4
N_HEADS_FOX = 4
N_HEADS_SB = 4
N_HEADS_DSA = 4
N_IDX_HEADS = 8
IDX_DIM = 64
TOPK_MAX = 256
ROPE_THETA = 500000.0
ROPE_DIM = HEAD_DIM // 4
N_BRANCH = 4
NORM_EPS = 1e-6
SUBLN_EPS = 1e-5

W_DIFF = N_HEADS_DIFF * 2 * HEAD_DIM
W_FOX = N_HEADS_FOX * HEAD_DIM
W_SB = N_HEADS_SB * HEAD_DIM
W_DSA = N_HEADS_DSA * HEAD_DIM
IN_SPLITS = (
    W_DIFF, W_DIFF, W_DIFF,
    W_FOX, W_FOX, W_FOX, N_HEADS_FOX,
    W_SB, W_SB, W_SB,
    W_DSA, W_DSA, W_DSA, N_IDX_HEADS * IDX_DIM, IDX_DIM, N_IDX_HEADS,
)
IN_WIDTH = sum(IN_SPLITS)


def rms_norm_2(x, g, eps=NORM_EPS):
    xf = x.astype(jnp.float32)
    y = xf * lax.rsqrt(jnp.mean(xf * xf, axis=-1, keepdims=True) + eps)
    return (y * g.astype(jnp.float32)).astype(x.dtype)

def swiglu_2(x, w_gu, w_down):
    g, u = jnp.split(x @ w_gu, 2, axis=-1)
    return (jax.nn.silu(g) * u) @ w_down

def rope_tables(positions):
    freqs = ROPE_THETA ** (-jnp.arange(0, ROPE_DIM, 2, dtype=jnp.float32) / ROPE_DIM)
    ang = positions.astype(jnp.float32)[:, None] * freqs[None, :]
    return jnp.cos(ang), jnp.sin(ang)

def partial_rope(x, cos, sin):
    shape = (1, cos.shape[0]) + (1,) * (x.ndim - 3) + (cos.shape[1],)
    c = cos.reshape(shape).astype(x.dtype)
    s = sin.reshape(shape).astype(x.dtype)
    half = ROPE_DIM // 2
    x1, x2, xp = x[..., :half], x[..., half:ROPE_DIM], x[..., ROPE_DIM:]
    return jnp.concatenate([x1 * c - x2 * s, x2 * c + x1 * s, xp], axis=-1)

def sweep_query_blocks(block_fn, seq_len):
    n_blocks = seq_len // Q_BLOCK
    out = lax.map(block_fn, jnp.arange(n_blocks, dtype=jnp.int32) * Q_BLOCK)
    nb, b, blk, h, e = out.shape
    return jnp.moveaxis(out, 0, 1).reshape(b, nb * blk, h, e)

def diff_attention(q, k, v, lam):
    S = q.shape[1]
    scale = HEAD_DIM ** -0.5
    kpos = jnp.arange(S)

    def block(start):
        qb = lax.dynamic_slice_in_dim(q, start, Q_BLOCK, axis=1)
        qpos = start + jnp.arange(Q_BLOCK)
        causal = kpos[None, :] <= qpos[:, None]
        logits = jnp.einsum('bqhcd,bkhcd->bchqk', qb, k).astype(jnp.float32) * scale
        p = jax.nn.softmax(jnp.where(causal, logits, -jnp.inf), axis=-1)
        p = p[:, 0] - lam * p[:, 1]
        return jnp.einsum('bhqk,bkhe->bqhe', p.astype(v.dtype), v)

    return sweep_query_blocks(block, S)

def forgetting_attention(q, k, v, f_logits):
    S = q.shape[1]
    scale = HEAD_DIM ** -0.5
    kpos = jnp.arange(S)
    cum = jnp.transpose(jnp.cumsum(jax.nn.log_sigmoid(f_logits.astype(jnp.float32)), axis=1), (0, 2, 1))

    def block(start):
        qb = lax.dynamic_slice_in_dim(q, start, Q_BLOCK, axis=1)
        cq = lax.dynamic_slice_in_dim(cum, start, Q_BLOCK, axis=2)
        qpos = start + jnp.arange(Q_BLOCK)
        causal = kpos[None, :] <= qpos[:, None]
        logits = (jnp.einsum('bqhd,bkhd->bhqk', qb, k).astype(jnp.float32) * scale
                  + cq[..., :, None] - cum[:, :, None, :])
        p = jax.nn.softmax(jnp.where(causal, logits, -jnp.inf), axis=-1)
        return jnp.einsum('bhqk,bkhd->bqhd', p.astype(v.dtype), v)

    return sweep_query_blocks(block, S)

def stick_breaking_attention(q, k, v):
    S = q.shape[1]
    scale = HEAD_DIM ** -0.5
    kpos = jnp.arange(S)

    def block(start):
        qb = lax.dynamic_slice_in_dim(q, start, Q_BLOCK, axis=1)
        qpos = start + jnp.arange(Q_BLOCK)
        strict = kpos[None, :] < qpos[:, None]
        z = jnp.einsum('bqhd,bkhd->bhqk', qb, k).astype(jnp.float32) * scale
        log_1m = jnp.where(strict, jax.nn.log_sigmoid(-z), 0.0)
        after = lax.cumsum(log_1m, axis=3, reverse=True) - log_1m
        a = jnp.where(strict, jnp.exp(jax.nn.log_sigmoid(z) + after), 0.0)
        return jnp.einsum('bhqk,bkhd->bqhd', a.astype(v.dtype), v)

    return sweep_query_blocks(block, S)

def indexed_sparse_attention(q, k, v, iq, ik, iw, topk):
    B, S = q.shape[0], q.shape[1]
    scale = HEAD_DIM ** -0.5
    kpos = jnp.arange(S)
    bidx = jnp.arange(B)[:, None, None]

    def block(start):
        qb = lax.dynamic_slice_in_dim(q, start, Q_BLOCK, axis=1)
        iqb = lax.dynamic_slice_in_dim(iq, start, Q_BLOCK, axis=1)
        iwb = lax.dynamic_slice_in_dim(iw, start, Q_BLOCK, axis=1)
        qpos = start + jnp.arange(Q_BLOCK)
        causal = kpos[None, :] <= qpos[:, None]
        rel = jax.nn.relu(jnp.einsum('bqhd,bkd->bqhk', iqb, ik).astype(jnp.float32))
        score = jnp.einsum('bqhk,bqh->bqk', rel, iwb.astype(jnp.float32))
        score = jnp.where(causal[None], score, -jnp.inf)
        _, idx = lax.top_k(score, topk)
        valid = idx <= qpos[None, :, None]
        k_sel = k[bidx, idx]
        v_sel = v[bidx, idx]
        logits = jnp.einsum('bqhd,bqjhd->bhqj', qb, k_sel).astype(jnp.float32) * scale
        p = jax.nn.softmax(jnp.where(valid[:, None], logits, -jnp.inf), axis=-1)
        return jnp.einsum('bhqj,bqjhd->bqhd', p.astype(v.dtype), v_sel)

    return sweep_query_blocks(block, S)

def hybrid_mixer(h, cos, sin, layer_idx, w_in, b_fgt, lam_q1, lam_k1, lam_q2, lam_k2, diff_gain,
                 w_gate, b_gate, w_br_a, w_br_b, w_br_c, w_br_d, w_out):
    B, S, D = h.shape
    points = np.cumsum(IN_SPLITS)[:-1].tolist()
    (aq, ak, av, bq, bk, bv, bf, cq, ck, cv,
     dq, dk, dv, diq, dik, diw) = jnp.split(h @ w_in, points, axis=-1)

    lam_init = 0.8 - 0.6 * math.exp(-0.3 * layer_idx)
    lam = (jnp.exp(jnp.sum(lam_q1.astype(jnp.float32) * lam_k1.astype(jnp.float32)))
           - jnp.exp(jnp.sum(lam_q2.astype(jnp.float32) * lam_k2.astype(jnp.float32))) + lam_init)
    qa = partial_rope(aq.reshape(B, S, N_HEADS_DIFF, 2, HEAD_DIM), cos, sin)
    ka = partial_rope(ak.reshape(B, S, N_HEADS_DIFF, 2, HEAD_DIM), cos, sin)
    ya = diff_attention(qa, ka, av.reshape(B, S, N_HEADS_DIFF, 2 * HEAD_DIM), lam)
    ya = (rms_norm_2(ya, diff_gain, SUBLN_EPS) * (1.0 - lam_init)).reshape(B, S, W_DIFF)

    yb = forgetting_attention(bq.reshape(B, S, N_HEADS_FOX, HEAD_DIM),
                              bk.reshape(B, S, N_HEADS_FOX, HEAD_DIM),
                              bv.reshape(B, S, N_HEADS_FOX, HEAD_DIM),
                              bf + b_fgt).reshape(B, S, W_FOX)

    yc = stick_breaking_attention(cq.reshape(B, S, N_HEADS_SB, HEAD_DIM),
                                  ck.reshape(B, S, N_HEADS_SB, HEAD_DIM),
                                  cv.reshape(B, S, N_HEADS_SB, HEAD_DIM)).reshape(B, S, W_SB)

    topk = min(TOPK_MAX, S // 4)
    qd = partial_rope(dq.reshape(B, S, N_HEADS_DSA, HEAD_DIM), cos, sin)
    kd = partial_rope(dk.reshape(B, S, N_HEADS_DSA, HEAD_DIM), cos, sin)
    iq = partial_rope(diq.reshape(B, S, N_IDX_HEADS, IDX_DIM), cos, sin)
    ik = partial_rope(dik, cos, sin)
    yd = indexed_sparse_attention(qd, kd, dv.reshape(B, S, N_HEADS_DSA, HEAD_DIM),
                                  iq, ik, diw, topk).reshape(B, S, W_DSA)

    g = jax.nn.sigmoid(h @ w_gate + b_gate).reshape(B, S, N_BRANCH, D)
    merged = (g[:, :, 0] * (ya @ w_br_a) + g[:, :, 1] * (yb @ w_br_b)
              + g[:, :, 2] * (yc @ w_br_c) + g[:, :, 3] * (yd @ w_br_d))
    return merged @ w_out

def second_inputs(seed: int = 0) -> dict:
    key = jax.random.key(seed)
    ks = iter(jax.random.split(key, 32))
    f32 = jnp.float32

    def nrm(shape, scale):
        return jax.random.normal(next(ks), shape, f32) * scale

    def gain(shape):
        return 1.0 + 0.02 * jax.random.normal(next(ks), shape, f32)

    L, D, F = DEPTH, D_MODEL, D_FF
    return {
        "x": jax.random.normal(next(ks), (BATCH, SEQ, D), f32),
        "positions": jnp.arange(SEQ, dtype=jnp.int32),
        "ffn1_norm": gain((L, D)),
        "ffn1_w_gu": nrm((L, D, 2 * F), D ** -0.5),
        "ffn1_w_down": nrm((L, F, D), F ** -0.5),
        "mix_norm": gain((L, D)),
        "w_in": nrm((L, D, IN_WIDTH), D ** -0.5),
        "b_fgt": 2.0 + 0.5 * jax.random.normal(next(ks), (L, N_HEADS_FOX), f32),
        "lam_q1": nrm((L, HEAD_DIM), 0.1),
        "lam_k1": nrm((L, HEAD_DIM), 0.1),
        "lam_q2": nrm((L, HEAD_DIM), 0.1),
        "lam_k2": nrm((L, HEAD_DIM), 0.1),
        "diff_gain": gain((L, 2 * HEAD_DIM)),
        "w_gate": nrm((L, D, N_BRANCH * D), D ** -0.5),
        "b_gate": nrm((L, N_BRANCH * D), 0.01),
        "w_br_a": nrm((L, W_DIFF, D), W_DIFF ** -0.5),
        "w_br_b": nrm((L, W_FOX, D), W_FOX ** -0.5),
        "w_br_c": nrm((L, W_SB, D), W_SB ** -0.5),
        "w_br_d": nrm((L, W_DSA, D), W_DSA ** -0.5),
        "w_out": nrm((L, D, D), 0.5 * D ** -0.5),
        "ffn2_norm": gain((L, D)),
        "ffn2_w_gu": nrm((L, D, 2 * F), D ** -0.5),
        "ffn2_w_down": nrm((L, F, D), F ** -0.5),
        "final_norm": gain((D,)),
    }

def second_block(x, positions, ffn1_norm, ffn1_w_gu, ffn1_w_down, mix_norm, w_in, b_fgt,
              lam_q1, lam_k1, lam_q2, lam_k2, diff_gain, w_gate, b_gate,
              w_br_a, w_br_b, w_br_c, w_br_d, w_out, ffn2_norm, ffn2_w_gu, ffn2_w_down,
              final_norm):
    cos, sin = rope_tables(positions)
    for l in range(DEPTH):
        x = x + 0.5 * swiglu_2(rms_norm_2(x, ffn1_norm[l]), ffn1_w_gu[l], ffn1_w_down[l])
        x = x + hybrid_mixer(rms_norm_2(x, mix_norm[l]), cos, sin, l, w_in[l], b_fgt[l],
                             lam_q1[l], lam_k1[l], lam_q2[l], lam_k2[l], diff_gain[l],
                             w_gate[l], b_gate[l], w_br_a[l], w_br_b[l], w_br_c[l], w_br_d[l],
                             w_out[l])
        x = x + 0.5 * swiglu_2(rms_norm_2(x, ffn2_norm[l]), ffn2_w_gu[l], ffn2_w_down[l])
    return rms_norm_2(x, final_norm)


def setup_inputs(seed=0):
    out = dict(first_inputs(seed))
    for name, value in second_inputs(seed + 1).items():
        if name != "x":
            out[name + "_2"] = value
    return out


def reference(
    x, c, ctx, c_ctx, l0_mod_w, l0_mod_b, l0_ffn1_norm, l0_ffn1_w_in, l0_ffn1_w_out,
    l0_mix_norm, l0_w_in, l0_mla_q_norm, l0_mla_w_uq, l0_mla_kv_norm, l0_mla_w_ukv,
    l0_mla_q_gain, l0_mla_k_gain, l0_conv_glu_b, l0_conv_dw_w, l0_conv_dw_b, l0_conv_ln_g,
    l0_conv_ln_b, l0_w_out, l0_ffn2_norm, l0_ffn2_w_in, l0_ffn2_w_out, l1_mod_w, l1_mod_b,
    l1_ffn1_norm, l1_ffn1_w_in, l1_ffn1_w_out, l1_mix_norm, l1_w_in, l1_gqa_q_gain,
    l1_gqa_k_gain, l1_na_q_gain, l1_na_k_gain, l1_na_rpb, l1_w_out, l1_ffn2_norm, l1_ffn2_w_in,
    l1_ffn2_w_out, positions_2, ffn1_norm_2, ffn1_w_gu_2, ffn1_w_down_2, mix_norm_2, w_in_2,
    b_fgt_2, lam_q1_2, lam_k1_2, lam_q2_2, lam_k2_2, diff_gain_2, w_gate_2, b_gate_2, w_br_a_2,
    w_br_b_2, w_br_c_2, w_br_d_2, w_out_2, ffn2_norm_2, ffn2_w_gu_2, ffn2_w_down_2,
    final_norm_2,
):
    x = first_block(
        x, c, ctx, c_ctx, l0_mod_w, l0_mod_b, l0_ffn1_norm, l0_ffn1_w_in, l0_ffn1_w_out,
        l0_mix_norm, l0_w_in, l0_mla_q_norm, l0_mla_w_uq, l0_mla_kv_norm, l0_mla_w_ukv,
        l0_mla_q_gain, l0_mla_k_gain, l0_conv_glu_b, l0_conv_dw_w, l0_conv_dw_b, l0_conv_ln_g,
        l0_conv_ln_b, l0_w_out, l0_ffn2_norm, l0_ffn2_w_in, l0_ffn2_w_out, l1_mod_w, l1_mod_b,
        l1_ffn1_norm, l1_ffn1_w_in, l1_ffn1_w_out, l1_mix_norm, l1_w_in, l1_gqa_q_gain,
        l1_gqa_k_gain, l1_na_q_gain, l1_na_k_gain, l1_na_rpb, l1_w_out, l1_ffn2_norm,
        l1_ffn2_w_in, l1_ffn2_w_out,
    )
    return second_block(
        x, positions_2, ffn1_norm_2, ffn1_w_gu_2, ffn1_w_down_2, mix_norm_2, w_in_2, b_fgt_2,
        lam_q1_2, lam_k1_2, lam_q2_2, lam_k2_2, diff_gain_2, w_gate_2, b_gate_2, w_br_a_2,
        w_br_b_2, w_br_c_2, w_br_d_2, w_out_2, ffn2_norm_2, ffn2_w_gu_2, ffn2_w_down_2,
        final_norm_2,
    )


_drawn_inputs = setup_inputs


def setup_inputs(seed=0):
    import zlib

    import numpy as np

    out = dict(_drawn_inputs(seed))
    spreads = {}
    factors = {'l0_ffn1_norm': 8.0,
     'l0_mix_norm': 8.0,
     'l0_mla_q_norm': 8.0,
     'l0_mla_kv_norm': 8.0,
     'l0_mla_q_gain': 8.0,
     'l0_mla_k_gain': 8.0,
     'l0_conv_glu_b': 8.0,
     'l0_conv_dw_b': 6.041,
     'l0_conv_ln_g': 8.0,
     'l0_conv_ln_b': 8.0,
     'l0_ffn2_norm': 8.0,
     'l1_ffn1_norm': 8.0,
     'l1_mix_norm': 8.0,
     'l1_gqa_q_gain': 8.0,
     'l1_gqa_k_gain': 8.0,
     'l1_na_q_gain': 8.0,
     'l1_na_k_gain': 8.0,
     'l1_na_rpb': 26.644,
     'l1_ffn2_norm': 8.0,
     'ffn1_norm_2': 4.103,
     'mix_norm_2': 3.796,
     'lam_q1_2': 24.467,
     'lam_q2_2': 2.931,
     'lam_k2_2': 5.419,
     'diff_gain_2': 64.0,
     'b_gate_2': 64.0,
     'ffn2_norm_2': 5.024,
     'final_norm_2': 8.673}
    for name, (base, spread) in spreads.items():
        noise = np.random.default_rng([zlib.crc32(name.encode()), seed]).standard_normal(out[name].shape)
        drawn = base * np.exp(spread * noise) if base else spread * noise
        out[name] = __import__('jax').numpy.asarray(drawn.astype(out[name].dtype))
    for name, factor in factors.items():
        out[name] = (out[name] * factor).astype(out[name].dtype)
    return out
```

```python
from contextlib import ExitStack

import numpy as np

import concourse.bass as bass
from concourse import mybir

F32 = mybir.dt.float32
ACT = mybir.ActivationFunctionType
ALU = mybir.AluOpType
AX = mybir.AxisListType

P = 128
D = 1024
KD = D // P
LAT, CTX = 256, 256
TOK = LAT + CTX
FF = 2816
KF = FF // P
N_MOD = 9
EPS = 1e-6
HD = 64
HEADS = 8
MLA_ROPE = 32
GRID_W = 64
WIN_W = 16
RPB_H, RPB_W = 15, 31
CONV_W = 31
PAD = CONV_W // 2
ROPE2 = 16
TOPK = 64
BANK = 512

QK_COLUMNS = (0, 256, 512, 768, 3076, 3332, 3844, 4100, 1536, 1792, 2308, 2564)
V_COLUMNS = (1024, 1280, 2048, 2820, 3588)

RING = 4
SLOT = KF * P
MASKED = -1.0e30
TAKEN = -3.0e38


class Tally:

    def __init__(self, sem):
        self.sem, self.base = sem, 0

    def close(self, n):
        self.base += n


class Product:

    def __init__(self, name, n, load, looped, dmas):
        self.name, self.n, self.load, self.looped, self.dmas = name, n, load, looped, dmas
        self.start, self.ready = 0, []


class Shared:
    pass



def constant_table():
    parts, rows = {}, {}

    def put(name, a):
        full = np.zeros((P, a.shape[1]), np.float32)
        full[: a.shape[0]] = a
        parts[name] = full
        rows[name] = a.shape[0]

    put("ident", np.eye(P, dtype=np.float32))
    for n in (512, 64, 32):
        put(f"mean{n}", np.full((min(n, P), P), 1.0 / n, np.float32))
    put("ones", np.ones((P, P), np.float32))
    put("later", np.tril(np.ones((P, P), np.float32), -1))

    def pairs(n):
        r = np.zeros((n, P), np.float32)
        for i in range(0, n, 2):
            r[i + 1, i] = -1.0
            r[i, i + 1] = 1.0
        return r

    put("turn64", pairs(64))
    put("turn32", pairs(32))
    r = np.zeros((ROPE2, P), np.float32)
    for i in range(ROPE2 // 2):
        r[ROPE2 // 2 + i, i] = -1.0
        r[i, ROPE2 // 2 + i] = 1.0
    put("turn16", r)
    t = np.arange(LAT)
    for n in (64, 32):
        q = n // 4
        inv = (np.float32(10000.0) ** (-np.arange(q, dtype=np.float32) / np.float32(q))).astype(np.float32)
        ang = np.concatenate([(t // GRID_W).astype(np.float32)[:, None] * inv,
                              (t % GRID_W).astype(np.float32)[:, None] * inv], axis=1)
        put(f"cos{n}", np.repeat(np.cos(ang), 2, axis=1).T.astype(np.float32))
        put(f"sin{n}", np.repeat(np.sin(ang), 2, axis=1).T.astype(np.float32))
    f = (np.float32(500000.0) ** (-np.arange(0, ROPE2, 2, dtype=np.float32) / np.float32(ROPE2))).astype(np.float32)
    put("freq", np.concatenate([f, f])[:, None])
    q, key = np.arange(P)[:, None], np.arange(LAT)[None, :]
    put("causal", np.concatenate([np.where(key <= q + P * i, 0.0, MASKED) for i in range(2)], 1).astype(np.float32))
    put("strict", np.concatenate([(q + P * i < key) for i in range(2)], 1).astype(np.float32))
    qc, kc = GRID_W - 1 - np.arange(P)[:, None] % GRID_W, np.arange(LAT)[None, :] % GRID_W
    start = np.clip(qc - WIN_W // 2, 0, GRID_W - WIN_W)
    put("window", np.where((kc >= start) & (kc < start + WIN_W), 0.0, MASKED).astype(np.float32))
    put("flip", np.kron(np.eye(P // GRID_W), np.eye(GRID_W)[::-1]).astype(np.float32))
    at, col = {}, 0
    for name, a in parts.items():
        at[name] = (rows[name], col, a.shape[1])
        col += a.shape[1]
    return np.ascontiguousarray(np.concatenate(list(parts.values()), axis=1)), at


def selector():
    return np.repeat(np.eye(4, dtype=np.float32), LAT, axis=1)


def vector_rows():
    rows, at = [], {}

    def put(name, source, n, width=P, layer=None, off=0):
        at[name] = sum(r[2] for r in rows)
        rows.append((source, layer, n, width, off))

    put("c", "c", 8)
    put("c_ctx", "c_ctx", 8)
    for l in (0, 1):
        put(f"mod_b{l}", f"l{l}_mod_b", 72)
        for m in ("ffn1", "mix", "ffn2"):
            put(f"{m}_{l}", f"l{l}_{m}_norm", 8)
    put("q_norm", "l0_mla_q_norm", 3)
    put("kv_norm", "l0_mla_kv_norm", 2)
    put("qg_nope", "l0_mla_q_gain", 1, 64)
    put("qg_rope", "l0_mla_q_gain", 1, 32, off=64)
    put("kg_nope", "l0_mla_k_gain", 1, 64)
    put("kg_rope", "l0_mla_k_gain", 1, 32, off=64)
    put("glu_b", "l0_conv_glu_b", 8)
    put("dw_b", "l0_conv_dw_b", 4)
    put("ln_g", "l0_conv_ln_g", 4)
    put("ln_b", "l0_conv_ln_b", 4)
    put("dw_w", "l0_conv_dw_w", CONV_W * 4)
    for g in ("gqa_q", "gqa_k", "na_q", "na_k"):
        put(g, f"l1_{g}_gain", 1, 64)
    for l in (0, 1):
        for m in ("ffn1", "mix", "ffn2"):
            put(f"{m}_b{l}", f"{m}_norm_2", 8, layer=l)
        put(f"gate_b{l}", "b_gate_2", 32, layer=l)
        put(f"diff{l}", "diff_gain_2", 1, layer=l)
        put(f"fgt{l}", "b_fgt_2", 1, 4, layer=l)
    put("final", "final_norm_2", 8)
    return rows, at



def by_chunk(w):
    return w.rearrange("(k p) n -> p k n", p=P)


def pair_tiles(slot):
    return slot[:, 0:2 * KD * P].rearrange("p (t k c) -> p t k c", t=2, k=KD)


def wide_tile(slot):
    return slot[:, 0:KD * 2 * P].rearrange("p (k c) -> p k c", k=KD)


def tall_tile(slot):
    return slot[:, 0:SLOT].rearrange("p (k c) -> p k c", k=KF)


def cols(start, n):
    return slice(start, start + n) if isinstance(start, int) else bass.ds(start, n)


def weight_plan(w):
    plan = []

    def add(name, n, load, dmas=1, looped=True):
        plan.append(Product(name, n, load, looped, dmas if isinstance(dmas, list) else [dmas] * n))

    def wide(name, mat, n, first=0):
        m = by_chunk(mat)
        add(name, n, lambda slot, i, c: [(wide_tile(slot), m[:, :, cols(i * (RING * 256) + (first + c * 256), 256)])])

    def gate_up(name, mat):
        m = by_chunk(mat)
        add(name, KF, lambda slot, i, c: [(pair_tiles(slot)[:, t], m[:, :, cols(i * (RING * P) + (t * FF + c * P), P)])
                                          for t in (0, 1)], 2)

    def tall(name, mat):
        m = by_chunk(mat)
        add(name, KD, lambda slot, i, c: [(tall_tile(slot), m[:, :, cols(i * (RING * P) + c * P, P)])])

    def listed(name, mat, units):
        m = by_chunk(mat)
        add(name, len(units), lambda slot, i, c: [(dst(slot), m[:, :, at:at + n]) for dst, at, n in units[c]],
            [len(u) for u in units], looped=False)

    def whole(slot, n=256):
        return wide_tile(slot)[:, :, 0:n]

    def tile(t, n=P):
        return lambda slot: pair_tiles(slot)[:, t, :, 0:n]

    for l in (0, 1):
        wide(f"mod{l}", w[f"l{l}_mod_w"], N_MOD * D // 256)
        gate_up(f"ffn1_in{l}", w[f"l{l}_ffn1_w_in"])
        tall(f"ffn1_out{l}", w[f"l{l}_ffn1_w_out"])
        if l == 0:
            units = [[(whole, 0, 256)], [(whole, 288, 256)], [(tile(0), 544, 128), (tile(1, 32), 256, 32)]]
            units += [[(tile(0), 672 + P * c, P), (tile(1), 1184 + P * c, P)] for c in range(4)]
            listed("in0", w["l0_w_in"], units)
            uq = by_chunk(w["l0_mla_w_uq"])
            heads = w["l0_mla_w_ukv"].rearrange("(k p) (h e) -> p k h e", p=P, h=HEADS)

            def latents_out(slot, i, c):
                if c == 1:
                    return [(slot[:, 0:2304].rearrange("p (k n) -> p k n", k=3), uq)]
                return [(slot[:, (2 * part + kc) * 512:(2 * part + kc + 1) * 512].rearrange("p (h e) -> p h e", h=HEADS),
                         heads[:, kc, :, part * HD:(part + 1) * HD]) for part in range(2) for kc in range(2)]

            add("heads0", 2, latents_out, [4, 1], looped=False)
        else:
            wide("in1", w["l1_w_in"], 9)
        wide(f"out{l}", w[f"l{l}_w_out"], 4)
        gate_up(f"ffn2_in{l}", w[f"l{l}_ffn2_w_in"])
        tall(f"ffn2_out{l}", w[f"l{l}_ffn2_w_out"])
    for l in (0, 1):
        gate_up(f"ffn1_in_b{l}", w["ffn1_w_gu_2"][l])
        tall(f"ffn1_out_b{l}", w["ffn1_w_down_2"][l])
        order = list(QK_COLUMNS) + list(V_COLUMNS)
        units = [[(whole, c, 256)] for c in order]
        units += [[(lambda slot: whole(slot, 72), 4356, 72), (lambda slot: wide_tile(slot)[:, :, 72:76], 2304, 4)]]
        listed(f"in_b{l}", w["w_in_2"][l], units)
        gates = w["w_gate_2"][l].rearrange("(k p) (b n) -> p b k n", p=P, b=4)
        br = {n: by_chunk(w[f"w_br_{n}_2"][l]) for n in "abcd"}

        def merge(slot, i, c, gates=gates, br=br):
            n = cols(i * (RING // 2 * P) + c // 2 * P, P)
            two = ((0, "a", 16, 4), (3, "d", 20, 2)) if c % 2 == 0 else ((1, "b", 16, 2), (2, "c", 18, 2))
            out = []
            for t, (gate, name, row, rows) in enumerate(two):
                out.append((tall_tile(slot)[:, t * KD:(t + 1) * KD, :], gates[:, gate, :, n]))
                out.append((tall_tile(slot)[:, row:row + rows, :], br[name][:, :, n]))
            return out

        add(f"merge_b{l}", 16, merge, 4)
        wide(f"out_b{l}", w["w_out_2"][l], 4)
        gate_up(f"ffn2_in_b{l}", w["ffn2_w_gu_2"][l])
        tall(f"ffn2_out_b{l}", w["ffn2_w_down_2"][l])
    start = 0
    raised = [0] * RING
    for spec in plan:
        spec.start = start
        spec.ready = []
        for j in range(spec.n):
            slot = (start + j) % RING
            raised[slot] += 16 * spec.dmas[j]
            spec.ready.append(raised[slot])
        start += spec.n
    return plan


def each_unit(engine, first, last, body, looped=True):
    full = (last - first) // RING if looped else 0
    if full > 1:
        with engine.Fori(0, full) as i:
            for s in range(RING):
                body(i, first + s)
    elif full == 1:
        for s in range(RING):
            body(0, first + s)
    for c in range(first + full * RING, last):
        body(0, c)


def load_weights(k, sp, first, last):
    for spec in k.plan:
        a, b = max(first, spec.start) - spec.start, min(last, spec.start + spec.n) - spec.start
        if a >= b:
            continue

        def unit(i, c, spec=spec):
            slot = (spec.start + c) % RING
            if first > 0:
                sp.wait_ge(k.unit_done, i * RING + (spec.start + c - RING + 1))
            for dst, src in spec.load(k.slots[slot], i, c):
                sp.dma_start(dst, src).then_inc(k.weights_ready[slot], 16)

        each_unit(sp, a, b, unit, spec.looped)


def wait_weights(k, pe, spec, i, c):
    slot = (spec.start + c) % RING
    pe.wait_ge(k.weights_ready[slot], i * (16 * spec.dmas[c]) + spec.ready[c])
    pe.wait_ge(k.banks_free, i * RING + (spec.start + c + 1))
    return slot


def wait_product(k, engine, spec, i, c):
    engine.wait_ge(k.unit_done, i * RING + (spec.start + c + 1))
    return (spec.start + c) % RING


def stream_ahead(k, block, spec):
    total = k.plan[-1].start + k.plan[-1].n

    @block.sync
    def _(sp):
        load_weights(k, sp, spec.start + RING, min(spec.start + spec.n + RING, total))



def halves(tokens):
    return [(0, slice(0, LAT)), (1, slice(LAT, TOK))][: tokens // LAT]


def one(t, h, rows=slice(None), col=slice(None)):
    if isinstance(h, int):
        return t[rows, h, col]
    return t[rows, bass.ds(h, 1), col].rearrange("p o n -> p (o n)")


def column(t, n, rows=slice(None)):
    return t[rows, cols(n, 1)]


def norm_tokens(k, tokens, gain, shift=None, dst=None):
    x, dst = k.x, k.h if dst is None else dst
    squared, mean, root, scaled = (k.tally(n) for n in ("squared", "mean_done", "root_done", "scaled"))
    T = slice(0, tokens)
    with k.nc.Block() as block:
        @block.scalar
        def _(act):
            for c in range(KD):
                k.nc.scalar.activation(k.mix[:, c, T], x[:, c, T], ACT.Square).then_inc(squared.sem, 1)
            act.wait_ge(mean.sem, mean.base + 1)
            k.nc.scalar.activation(k.root[:, T], k.psum[:, 0, T], ACT.Sqrt, bias=k.eps[:, 0:1],
                                   scale=1.0 / D).then_inc(root.sem, 1)
            if shift is not None:
                for c in range(KD):
                    for cond, part in halves(tokens):
                        act.wait_ge(scaled.sem, scaled.base + 2 + c)
                        k.nc.scalar.activation(dst[:, c, part], dst[:, c, part], ACT.Identity,
                                               bias=shift(c, cond), scale=gain(c, cond))

        @block.tensor
        def _(pe):
            for c in range(KD):
                pe.wait_ge(squared.sem, squared.base + c + 1)
                mm = k.nc.tensor.matmul(k.psum[:, 0, T], k.const("ones"), k.mix[:, c, T], start=c == 0, stop=c == KD - 1)
            mm.then_inc(mean.sem, 1)

        @block.vector
        def _(dve):
            dve.wait_ge(root.sem, root.base + 1)
            k.nc.vector.reciprocal(k.rinv[:, T], k.root[:, T]).then_inc(scaled.sem, 1)
            dve.wait_ge(scaled.sem, scaled.base + 1)
            for c in range(KD):
                if shift is None:
                    k.nc.vector.scalar_tensor_tensor(dst[:, c, T], x[:, c, T], gain(c, 0), k.rinv[:, T],
                                                     ALU.mult, ALU.mult).then_inc(scaled.sem, 1)
                else:
                    k.nc.vector.tensor_tensor(dst[:, c, T], x[:, c, T], k.rinv[:, T], ALU.mult).then_inc(scaled.sem, 1)
    for t, n in ((squared, KD), (mean, 1), (root, 1), (scaled, 1 + KD)):
        t.close(n)


def ffn_in(k, spec, tokens):
    T = slice(0, tokens)
    hidden = k.arena[:, 0:KF * TOK].rearrange("p (f t) -> p f t", f=KF)
    silu = k.tally("silu_done")
    with k.nc.Block() as block:
        stream_ahead(k, block, spec)

        @block.tensor
        def _(pe):
            def unit(i, c):
                slot = wait_weights(k, pe, spec, i, c)
                w = pair_tiles(k.slots[slot])
                for t in range(2):
                    for kc in range(KD):
                        mm = k.nc.tensor.matmul(k.psum[:, 2 * slot + t, T], w[:, t, kc], k.h[:, kc, T],
                                                start=kc == 0, stop=kc == KD - 1)
                mm.then_inc(k.unit_done, 1)
            each_unit(pe, 0, spec.n, unit)

        @block.scalar
        def _(act):
            def unit(i, c):
                slot = wait_product(k, act, spec, i, c)
                k.nc.scalar.activation(one(hidden, i * RING + c, col=T), k.psum[:, 2 * slot, T], ACT.Silu)\
                    .then_inc(silu.sem, 1)
            each_unit(act, 0, spec.n, unit)

        @block.vector
        def _(dve):
            def unit(i, c):
                slot = wait_product(k, dve, spec, i, c)
                dve.wait_ge(silu.sem, i * RING + (silu.base + c + 1))
                row = one(hidden, i * RING + c, col=T)
                k.nc.vector.tensor_tensor(row, row, k.psum[:, 2 * slot + 1, T], ALU.mult).then_inc(k.banks_free, 1)
            each_unit(dve, 0, spec.n, unit)
    silu.close(spec.n)


def add_product(k, spec, tokens, source, chunks, tile_of, tiles, gate):
    T = slice(0, tokens)
    with k.nc.Block() as block:
        stream_ahead(k, block, spec)

        @block.tensor
        def _(pe):
            def unit(i, c):
                slot = wait_weights(k, pe, spec, i, c)
                for t in range(tiles):
                    for kc in range(chunks):
                        mm = k.nc.tensor.matmul(k.psum[:, 2 * slot + t, T], tile_of(k.slots[slot], kc, t),
                                                source[:, kc, T], start=kc == 0, stop=kc == chunks - 1)
                mm.then_inc(k.unit_done, 1)
            each_unit(pe, 0, spec.n, unit)

        @block.vector
        def _(dve):
            def unit(i, c):
                slot = wait_product(k, dve, spec, i, c)
                for t in range(tiles):
                    chunk = i * (RING * tiles) + (c * tiles + t)
                    for cond, part in (halves(tokens) if callable(gate) else [(0, T)]):
                        row = one(k.x, chunk, col=part)
                        last = k.nc.vector.scalar_tensor_tensor(row, k.psum[:, 2 * slot + t, part],
                                                                gate(chunk, cond) if callable(gate) else gate, row,
                                                                ALU.mult, ALU.add)
                last.then_inc(k.banks_free, 1)
            each_unit(dve, 0, spec.n, unit)


def half_ffn(k, tokens, name, gain, shift, gate):
    norm_tokens(k, tokens, gain, shift)
    ffn_in(k, k.spec(name[0]), tokens)
    hidden = k.arena[:, 0:KF * TOK].rearrange("p (f t) -> p f t", f=KF)
    add_product(k, k.spec(name[1]), tokens, hidden, KF, lambda slot, kc, t: tall_tile(slot)[:, kc, :], 1, gate)


def wide_lhs(slot, kc, t):
    return wide_tile(slot)[:, kc, t * P:(t + 1) * P]


def norm_heads(k, src, rows, groups, n, mean, gain, scale=1.0, eps=None):
    squared, mean_done, root, inv, normed = (k.tally(t) for t in ("squared", "mean_done", "root_done", "inverse_done", "normed"))
    R, N = slice(0, rows), slice(0, n)
    eps = k.eps if eps is None else eps
    with k.nc.Block() as block:
        @block.scalar
        def _(act):
            act.sem_inc(inv.sem, 2)
            with act.Fori(0, groups // 2) as i:
                for u in range(2):
                    k.nc.scalar.activation(k.square[R, u, N], one(src, i * 2 + u, R, N), ACT.Square).then_inc(squared.sem, 1)
                for u in range(2):
                    act.wait_ge(mean_done.sem, i * 2 + (mean_done.base + u + 1))
                    act.wait_ge(inv.sem, i * 2 + (inv.base + u + 1))
                    k.nc.scalar.activation(k.roots[R, u, N], k.psum[R, u, N], ACT.Sqrt, bias=eps[R, 0:1], scale=scale)\
                        .then_inc(root.sem, 1)

        @block.tensor
        def _(pe):
            with pe.Fori(0, groups // 2) as i:
                for u in range(2):
                    pe.wait_ge(squared.sem, i * 2 + (squared.base + u + 1))
                    k.nc.tensor.matmul(k.psum[:, u, N], mean, k.square[R, u, N], start=True, stop=True)\
                        .then_inc(mean_done.sem, 1)

        @block.vector
        def _(dve):
            with dve.Fori(0, groups // 2) as i:
                for u in range(2):
                    dve.wait_ge(root.sem, i * 2 + (root.base + u + 1))
                    k.nc.vector.reciprocal(k.rinvs[R, u, N], k.roots[R, u, N]).then_inc(inv.sem, 1)
                    dve.wait_ge(inv.sem, i * 2 + (inv.base + 2 + u + 1))
                    row = one(src, i * 2 + u, R, N)
                    k.nc.vector.scalar_tensor_tensor(row, row, gain, k.rinvs[R, u, N], ALU.mult, ALU.mult)\
                        .then_inc(normed.sem, 1)
    for t, n in ((squared, groups), (mean_done, groups), (root, groups), (inv, groups + 2), (normed, groups)):
        t.close(n)


def rotate_heads(k, src, rows, groups, turn, cos, sin):
    turned, by_cos, by_sin, rotated = (k.tally(t) for t in ("turned", "by_cos", "by_sin", "rotated"))
    R, N = slice(0, rows), slice(0, LAT)
    with k.nc.Block() as block:
        @block.tensor
        def _(pe):
            pe.sem_inc(by_sin.sem, 2)
            def group(g, u):
                pe.wait_ge(by_sin.sem, g + (by_sin.base + 1))
                k.nc.tensor.matmul(k.psum[:, u, N], turn, one(src, g, R, N), start=True, stop=True).then_inc(turned.sem, 1)
            with pe.Fori(0, groups // 2) as i:
                for u in range(2):
                    group(i * 2 + u, u)
            if groups % 2:
                group(groups - 1, (groups - 1) % 2)

        @block.vector
        def _(dve):
            def group(g, u):
                row = one(src, g, R, N)
                dve.wait_ge(turned.sem, g + (turned.base + 1))
                k.nc.vector.tensor_tensor(k.square[R, u, N], k.psum[R, u, N], sin, ALU.mult).then_inc(by_sin.sem, 1)
                k.nc.vector.tensor_tensor(row, row, cos, ALU.mult).then_inc(by_cos.sem, 1)
                dve.wait_ge(by_cos.sem, g + (by_cos.base + 1))
                k.nc.vector.tensor_tensor(row, row, k.square[R, u, N], ALU.add).then_inc(rotated.sem, 1)
            with dve.Fori(0, groups // 2) as i:
                for u in range(2):
                    group(i * 2 + u, u)
            if groups % 2:
                group(groups - 1, (groups - 1) % 2)
    for t, n in ((turned, groups), (by_cos, groups), (by_sin, groups + 2), (rotated, groups)):
        t.close(n)


def attention(k, pairs, key_tiles, staging, score, value, width, dst, difference=None):
    nc, J = k.nc, 4
    keys = key_tiles * P
    steps = 1 if difference is None else 2
    t = {n: k.tally(n) for n in (
        "staged", "scored", "maxed", "exp_done", "probs_turned", "even_copied", "odd_copied", "weighted",
        "sums_inverted", "out_normed", "out_turned", "out_placed")}
    S = [k.psum[:, j, 0:keys] for j in range(J)]
    PT = [k.psum[:, 4 + u, 0:keys] for u in range(2)]
    O = [k.psum[:, 6, j * width:(j + 1) * width] for j in range(J)]
    OT = k.psum[:, 7, 0:2 * P]
    jobs = [(j, j // 2, j % 2) for j in range(J)]
    prob = [k.prob(j, keys) for j in range(J)]
    prob_t = [k.prob_t(u, keys) for u in range(2)]
    with nc.Block() as block:
        @block.gpsimd
        def _(pool):
            with pool.Fori(0, pairs) as b:
                copies = staging(b)
                for n, (to, of) in enumerate(copies):
                    last = nc.gpsimd.tensor_copy(to, of)
                last.then_inc(t["staged"].sem, 1)
                pool.wait_ge(t["scored"].sem, b * J + (t["scored"].base + J))

        @block.tensor
        def _(pe):
            pe.sem_inc(t["out_placed"].sem, 1)

            def weigh(b, j, hh):
                copied = t["even_copied"] if j % 2 == 0 else t["odd_copied"]
                pe.wait_ge(copied.sem, b * (J // 2) + (copied.base + j // 2 + 1))
                for kt in range(key_tiles):
                    mm = nc.tensor.matmul(O[j], prob_t[j % 2][:, kt * P:(kt + 1) * P], value(b, hh, kt),
                                          start=kt == 0, stop=kt == key_tiles - 1)
                mm.then_inc(t["weighted"].sem, 1)

            with pe.Fori(0, pairs) as b:
                pe.wait_ge(t["staged"].sem, b + (t["staged"].base + 1))
                for j, hh, qt in jobs:
                    score(S[j], b, hh, qt).then_inc(t["scored"].sem, 1)
                for j, hh, qt in jobs:
                    pe.wait_ge(t["exp_done"].sem, b * J + (t["exp_done"].base + j + 1))
                    for kt in range(key_tiles):
                        mm = nc.tensor.transpose(PT[j % 2][:, kt * P:(kt + 1) * P], prob[j][:, kt * P:(kt + 1) * P],
                                                 k.const("ident"))
                    mm.then_inc(t["probs_turned"].sem, 1)
                    if j >= 1:
                        weigh(b, j - 1, (j - 1) // 2)
                weigh(b, J - 1, 1)
                pe.wait_ge(t["out_normed"].sem, b * J + (t["out_normed"].base + J))
                pe.wait_ge(t["out_placed"].sem, b + (t["out_placed"].base + 1))
                for qt in range(2):
                    mm = nc.tensor.transpose(OT[:, qt * P:(qt + 1) * P], k.out_rows[:, qt, :], k.const("ident"))
                mm.then_inc(t["out_turned"].sem, 1)

        @block.vector
        def _(dve):
            dve.sem_inc(t["out_turned"].sem, 1)
            with dve.Fori(0, pairs) as b:
                for j, hh, qt in jobs:
                    dve.wait_ge(t["scored"].sem, b * J + (t["scored"].base + j + 1))
                    nc.vector.tensor_reduce(k.negmax[:, j:j + 1], S[j], AX.X, ALU.max, negate=True).then_inc(t["maxed"].sem, 1)
                for j in (0, 2):
                    dve.wait_ge(t["probs_turned"].sem, b * J + (t["probs_turned"].base + j + 1))
                    if j == 2:
                        dve.wait_ge(t["weighted"].sem, b * J + (t["weighted"].base + 1))
                    nc.vector.tensor_copy(prob_t[0], PT[0]).then_inc(t["even_copied"].sem, 1)
                dve.wait_ge(t["exp_done"].sem, b * J + (t["exp_done"].base + J))
                inverse = nc.vector.reciprocal(k.inverse[:, 0:J], k.rowsum[:, 0:J])
                inverse.then_inc(t["sums_inverted"].sem, 1)
                dve.wait_ge(t["sums_inverted"].sem, b * steps + (t["sums_inverted"].base + 1))
                if difference is not None:
                    nc.vector.tensor_scalar(k.inverse[:, J:J + 2], k.inverse[:, 2:4], difference, None, ALU.mult)\
                        .then_inc(t["sums_inverted"].sem, 1)
                    dve.wait_ge(t["sums_inverted"].sem, b * steps + (t["sums_inverted"].base + 2))
                dve.wait_ge(t["out_turned"].sem, b + (t["out_turned"].base + 1))
                dve.wait_ge(t["weighted"].sem, b * J + (t["weighted"].base + J))
                for j, hh, qt in jobs:
                    if difference is None:
                        nc.vector.tensor_scalar(k.out_rows[:, qt, hh * width:(hh + 1) * width], O[j],
                                                k.inverse[:, j:j + 1], None, ALU.mult).then_inc(t["out_normed"].sem, 1)
                    elif hh == 0:
                        nc.vector.tensor_scalar(k.out_rows[:, qt, :], O[j], k.inverse[:, j:j + 1], None, ALU.mult)\
                            .then_inc(t["out_normed"].sem, 1)
                    else:
                        dve.wait_ge(t["out_normed"].sem, b * J + (t["out_normed"].base + j - 1))
                        nc.vector.scalar_tensor_tensor(k.out_rows[:, qt, :], O[j], k.inverse[:, J + qt:J + qt + 1],
                                                       k.out_rows[:, qt, :], ALU.mult, ALU.add).then_inc(t["out_normed"].sem, 1)

        @block.scalar
        def _(act):
            with act.Fori(0, pairs) as b:
                for j, hh, qt in jobs:
                    act.wait_ge(t["maxed"].sem, b * J + (t["maxed"].base + j + 1))
                    nc.scalar.activation(prob[j], S[j], ACT.Exp, bias=k.negmax[:, j:j + 1],
                                         accum_out=k.rowsum[:, j:j + 1]).then_inc(t["exp_done"].sem, 1)
                for j in (1, 3):
                    act.wait_ge(t["probs_turned"].sem, b * J + (t["probs_turned"].base + j + 1))
                    if j == 3:
                        act.wait_ge(t["weighted"].sem, b * J + (t["weighted"].base + 2))
                    nc.scalar.activation(prob_t[1], PT[1], ACT.Copy).then_inc(t["odd_copied"].sem, 1)
                act.wait_ge(t["out_turned"].sem, b + (t["out_turned"].base + 2))
                nc.scalar.activation(dst(b), OT, ACT.Copy).then_inc(t["out_placed"].sem, 1)
    for name, n in dict(staged=1, scored=J, maxed=J, exp_done=J, probs_turned=J, even_copied=2, odd_copied=2, weighted=J,
                        sums_inverted=steps, out_normed=J, out_turned=1, out_placed=1).items():
        t[name].close(n * pairs)
    t["out_turned"].close(1)
    t["out_placed"].close(1)



def opening(k, w):
    nc = k.nc
    t = {n: k.tally(n) for n in ("cleared", "consts_landed", "tokens_landed", "vectors_landed",
                                                   "tokens_turned", "tokens_placed", "vectors_turned", "vectors_placed")}
    tokens = k.arena[:, 0:4 * D].rearrange("p (t n) -> p t n", t=4)
    tiles = (k.n_rows + P - 1) // P
    rows = k.arena[:, 4 * D:4 * D + tiles * P].rearrange("p (t n) -> p t n", t=tiles)
    loads = []
    for name, (source, layer, n, width, off) in zip(k.vec_at, k.vec_rows):
        src = w[source] if layer is None else w[source][layer:layer + 1]
        if len(src.shape) == 1:
            src = src.unsqueeze(0)
        flat = src.rearrange("a b -> (a b)")
        flat = flat[off:off + n * width].rearrange("(r c) -> r c", c=width)
        r, done = k.vec_at[name], 0
        while done < n:
            m = min(n - done, P - (r + done) % P)
            at = (r + done) % P
            loads.append((rows[at:at + m, (r + done) // P, 0:width], flat[done:done + m, :]))
            done += m
    lams = [(k.lam[:, l, v, :], w[f"lam_{n}_2"][l:l + 1, :].partition_broadcast(P))
            for l in (0, 1) for v, n in enumerate(("q1", "k1", "q2", "k2"))]
    with nc.Block() as block:
        @block.vector
        def _(dve):
            dve.sem_inc(k.banks_free, RING)
            nc.vector.memset(rows, 0.0).then_inc(t["cleared"].sem, 1)
            nc.vector.memset(k.eps[:, :], EPS).then_inc(t["cleared"].sem, 1)
            nc.vector.memset(k.eps5[:, :], 1e-5).then_inc(t["cleared"].sem, 1)
            nc.vector.memset(k.half_pi[:, :], float(np.pi / 2)).then_inc(t["cleared"].sem, 1)
            for c in range(KD):
                dve.wait_ge(t["tokens_turned"].sem, c + 1)
                nc.vector.tensor_copy(k.x[:, c, :], k.psum[:, c, :]).then_inc(t["tokens_placed"].sem, 1)
            dve.wait_ge(t["vectors_turned"].sem, 1)
            nc.vector.tensor_copy(k.vec[:, 0:tiles * P], k.psum[:, 0, 0:tiles * P]).then_inc(t["vectors_placed"].sem, 1)

        @block.sync
        def _(sp):
            sp.dma_start(tokens[:, 0:2, :], w["x"][0].rearrange("(t p) n -> p t n", p=P)).then_inc(t["tokens_landed"].sem, 16)
            sp.dma_start(tokens[:, 2:4, :], w["ctx"][0].rearrange("(t p) n -> p t n", p=P)).then_inc(t["tokens_landed"].sem, 16)
            sp.dma_start(k.consts[:, :], w["constants"]).then_inc(t["consts_landed"].sem, 16)
            load_weights(k, sp, 0, RING)

        @block.scalar
        def _(act):
            act.wait_ge(t["cleared"].sem, 1)
            for to, of in loads:
                act.dma_start(to, of).then_inc(t["vectors_landed"].sem, 16)
            for to, of in lams:
                act.dma_start(to, of).then_inc(t["vectors_landed"].sem, 16)
            act.dma_start(k.positions[:, :], w["positions_2"].unsqueeze(0).partition_broadcast(ROPE2))\
                .then_inc(t["vectors_landed"].sem, 16)
            act.wait_ge(t["vectors_placed"].sem, 1)
            for cond, name in enumerate(("c", "c_ctx")):
                at = k.vec_at[name]
                last = nc.scalar.activation(k.cond[:, :, cond], k.vec[:, at:at + KD], ACT.Silu)

        @block.tensor
        def _(pe):
            pe.wait_ge(t["consts_landed"].sem, 16)
            pe.wait_ge(t["tokens_landed"].sem, 32)
            for c in range(KD):
                for tt in range(4):
                    mm = nc.tensor.transpose(k.psum[:, c, tt * P:(tt + 1) * P], tokens[:, tt, c * P:(c + 1) * P],
                                             k.const("ident"))
                mm.then_inc(t["tokens_turned"].sem, 1)
            pe.wait_ge(t["vectors_landed"].sem, 16 * (len(loads) + len(lams) + 1))
            pe.wait_ge(t["tokens_placed"].sem, 1)
            for tt in range(tiles):
                mm = nc.tensor.transpose(k.psum[:, 0, tt * P:(tt + 1) * P], rows[:, tt, :], k.const("ident"))
            mm.then_inc(t["vectors_turned"].sem, 1)
    for name, n in dict(cleared=4, tokens_turned=KD, tokens_placed=KD, vectors_turned=1, vectors_placed=1).items():
        t[name].close(n)


def conditioning(k, l):
    nc, spec = k.nc, k.spec(f"mod{l}")
    derived = k.tally("derived")
    bias = k.vec_at[f"mod_b{l}"]
    with nc.Block() as block:
        stream_ahead(k, block, spec)

        @block.tensor
        def _(pe):
            def unit(i, c):
                slot = wait_weights(k, pe, spec, i, c)
                for t in range(2):
                    for kc in range(KD):
                        mm = nc.tensor.matmul(k.psum[:, 2 * slot, 2 * t:2 * t + 2], wide_lhs(k.slots[slot], kc, t),
                                              k.cond[:, kc, :], start=kc == 0, stop=kc == KD - 1)
                mm.then_inc(k.unit_done, 1)
            each_unit(pe, 0, spec.n, unit)

        @block.vector
        def _(dve):
            def unit(i, c):
                slot = wait_product(k, dve, spec, i, c)
                for t in range(2):
                    chunk = i * (RING * 2) + (c * 2 + t)
                    last = nc.vector.tensor_scalar(one(k.mod, chunk), k.psum[:, 2 * slot, 2 * t:2 * t + 2],
                                                   column(k.vec, chunk + bias), None, ALU.add)
                last.then_inc(k.banks_free, 1)
            each_unit(dve, 0, spec.n, unit)
            dve.wait_ge(k.banks_free, spec.start + spec.n + RING)
            for m, name in enumerate(("ffn1", "mix", "ffn2")):
                gain = k.vec_at[f"{name}_{l}"]
                for cond in range(2):
                    nc.vector.scalar_tensor_tensor(k.gain[:, m, :, cond], k.mod[:, (3 * m + 1) * KD:(3 * m + 2) * KD, cond],
                                                   1.0, k.vec[:, gain:gain + KD], ALU.add, ALU.mult).then_inc(derived.sem, 1)
            for m, at in ((0, 2), (1, 8)):
                nc.vector.tensor_scalar(k.gate[:, m], k.mod[:, at * KD:(at + 1) * KD, :], 0.5, None, ALU.mult)\
                    .then_inc(derived.sem, 1)
    derived.close(8)


def modulated(k, m):
    return (lambda c, cond: k.gain[:, m, c, cond:cond + 1],
            lambda c, cond: k.mod[:, 3 * m * KD + c, cond:cond + 1])


def half_gate(k, m):
    def gate(chunk, cond):
        if isinstance(chunk, int):
            return k.gate[:, m, chunk, cond:cond + 1]
        return k.gate[:, m, bass.ds(chunk, 1), cond]
    return gate


def mix_gate(k):
    def gate(chunk, cond):
        if isinstance(chunk, int):
            return k.mod[:, 5 * KD + chunk, cond:cond + 1]
        return k.mod[:, bass.ds(chunk + 5 * KD, 1), cond]
    return gate


def ending(k, out):
    nc = k.nc
    turned, placed, stored = (k.tally(n) for n in ("tokens_turned", "tokens_placed", "stored"))
    rows = k.arena[:, 0:2 * D].rearrange("p (t n) -> p t n", t=2)
    with nc.Block() as block:
        @block.tensor
        def _(pe):
            for tt in range(2):
                for c in range(KD):
                    mm = nc.tensor.transpose(k.psum[:, 2 * tt + c // 4, (c % 4) * P:(c % 4 + 1) * P],
                                             k.h[:, c, tt * P:(tt + 1) * P], k.const("ident"))
                    if c % 4 == 3:
                        mm.then_inc(turned.sem, 1)

        @block.vector
        def _(dve):
            for n in range(4):
                dve.wait_ge(turned.sem, turned.base + n + 1)
                nc.vector.tensor_copy(rows[:, n // 2, (n % 2) * BANK:(n % 2 + 1) * BANK], k.psum[:, n, :])\
                    .then_inc(placed.sem, 1)

        @block.sync
        def _(sp):
            for n in range(4):
                sp.wait_ge(placed.sem, placed.base + n + 1)
                sp.dma_start(out[0][(n // 2) * P:(n // 2 + 1) * P, (n % 2) * BANK:(n % 2 + 1) * BANK],
                             rows[:, n // 2, (n % 2) * BANK:(n % 2 + 1) * BANK]).then_inc(stored.sem, 16)
            sp.wait_ge(stored.sem, 64)



def even_mixer(k):
    nc = k.nc
    qn = k.arena[0:HD, 0:HEADS * TOK].rearrange("p (h t) -> p h t", h=HEADS)
    kn = k.arena[0:HD, HEADS * TOK:2 * HEADS * TOK].rearrange("p (h t) -> p h t", h=HEADS)
    qr = k.arena[0:MLA_ROPE, 2 * HEADS * TOK:2 * HEADS * TOK + 9 * TOK].rearrange("p (h t) -> p h t", h=9)
    ypad = k.side[:, 0:4 * 2 * (LAT + 2 * PAD)].rearrange("p (c s t) -> p c s t", c=4, s=2)

    spec = k.spec("in0")
    first = k.tally("first_bank_out")
    cleared = k.tally("cleared")
    with nc.Block() as block:
        stream_ahead(k, block, spec)

        @block.gpsimd
        def _(pool):
            nc.gpsimd.memset(ypad[:, :, :, 0:PAD], 0.0).then_inc(cleared.sem, 1)
            nc.gpsimd.memset(ypad[:, :, :, PAD + LAT:], 0.0).then_inc(cleared.sem, 1)

        @block.tensor
        def _(pe):
            for c in range(spec.n):
                slot = wait_weights(k, pe, spec, 0, c)
                for t in range(2):
                    m = MLA_ROPE if (c, t) == (2, 1) else P
                    for kc in range(KD):
                        lhs = wide_lhs(k.slots[slot], kc, t) if c < 2 else pair_tiles(k.slots[slot])[:, t, kc, 0:m]
                        mm = nc.tensor.matmul(k.psum[0:m, 2 * slot + t, :], lhs, k.h[:, kc, :], start=kc == 0, stop=kc == KD - 1)
                mm.then_inc(k.unit_done, 1)

        @block.scalar
        def _(act):
            for c in range(spec.n):
                slot = wait_product(k, act, spec, 0, c)
                if c < 3:
                    last = nc.scalar.activation(k.mix[:, 2 * c, :], k.psum[:, 2 * slot, :], ACT.Copy)
                else:
                    if c >= 5:
                        act.wait_ge(k.banks_free, RING + spec.start + c - 1)
                    last = nc.scalar.activation(k.square[:, c % 2, :], k.psum[:, 2 * slot + 1, :], ACT.Sigmoid,
                                                bias=column(k.vec, k.vec_at["glu_b"] + 4 + c - 3))
                last.then_inc(first.sem, 1)

        @block.vector
        def _(dve):
            for c in range(spec.n):
                slot = wait_product(k, dve, spec, 0, c)
                dve.wait_ge(first.sem, first.base + c + 1)
                if c < 3:
                    m = MLA_ROPE if c == 2 else P
                    last = nc.vector.tensor_copy(k.mix[0:m, 2 * c + 1, :], k.psum[0:m, 2 * slot + 1, :])
                else:
                    last = nc.vector.scalar_tensor_tensor(
                        ypad[:, c - 3, :, PAD:PAD + LAT], k.psum[:, 2 * slot, :].rearrange("p (s t) -> p s t", s=2),
                        column(k.vec, k.vec_at["glu_b"] + c - 3), k.square[:, c % 2, :].rearrange("p (s t) -> p s t", s=2),
                        ALU.add, ALU.mult)
                last.then_inc(k.banks_free, 1)
    first.close(spec.n)
    cleared.close(2)

    squared, mean, root, inv = (k.tally(n) for n in ("squared", "mean_done", "root_done", "inverse_done"))
    groups = [([0, 1], P, "kv_norm"), ([2, 3, 4], P, "q_norm"), ([5], MLA_ROPE, "kg_rope")]
    with nc.Block() as block:
        @block.scalar
        def _(act):
            for chunks, rows, _ in groups:
                for c in chunks:
                    nc.scalar.activation(k.h[0:rows, c, :], k.mix[0:rows, c, :], ACT.Square).then_inc(squared.sem, 1)
            for g, (chunks, rows, _) in enumerate(groups):
                act.wait_ge(mean.sem, mean.base + g + 1)
                if g == 2:
                    act.wait_ge(inv.sem, inv.base + 1)
                nc.scalar.activation(k.roots[0:rows, g % 2, :], k.psum[0:rows, g, :], ACT.Sqrt, bias=k.eps[0:rows, 0:1],
                                     scale=1.0 / (rows * len(chunks)))\
                    .then_inc(root.sem, 1)

        @block.tensor
        def _(pe):
            done = 0
            for g, (chunks, rows, _) in enumerate(groups):
                for n, c in enumerate(chunks):
                    done += 1
                    pe.wait_ge(squared.sem, squared.base + done)
                    mm = nc.tensor.matmul(k.psum[0:rows, g, :], k.const("ones")[0:rows, 0:rows], k.h[0:rows, c, :],
                                          start=n == 0, stop=n == len(chunks) - 1)
                mm.then_inc(mean.sem, 1)

        @block.vector
        def _(dve):
            for g, (chunks, rows, gain) in enumerate(groups):
                dve.wait_ge(root.sem, root.base + g + 1)
                nc.vector.reciprocal(k.rinvs[0:rows, g % 2, :], k.roots[0:rows, g % 2, :]).then_inc(inv.sem, 1)
                dve.wait_ge(inv.sem, inv.base + g + 1)
                for n, c in enumerate(chunks):
                    dst = qr[:, 8, :] if g == 2 else k.mix[0:rows, c, :]
                    nc.vector.scalar_tensor_tensor(dst, k.mix[0:rows, c, :], column(k.vec, k.vec_at[gain] + n, slice(0, rows)),
                                                   k.rinvs[0:rows, g % 2, :], ALU.mult, ALU.mult)
    squared.close(6), mean.close(3), root.close(3), inv.close(3)

    spec = k.spec("heads0")
    item, out = k.tally("item_done"), k.tally("item_out")
    with nc.Block() as block:
        stream_ahead(k, block, spec)
        slots = [(spec.start + c) % RING for c in range(2)]
        uk, uv = (k.slots[slots[0]][:, n * 1024:(n + 1) * 1024].rearrange("p (k n) -> p k n", k=2) for n in range(2))
        uq = k.slots[slots[1]][:, 0:2304].rearrange("p (k h e) -> p k h e", k=3, h=HEADS)

        @block.tensor
        def _(pe):
            n = 0

            def free_bank():
                if n >= 8:
                    pe.wait_ge(out.sem, out.base + n - 7)
                return n % 8

            wait_weights(k, pe, spec, 0, 0)
            for pair in range(HEADS // 2):
                bank = free_bank()
                for kc in range(2):
                    mm = nc.tensor.matmul(k.psum[:, bank, :], uk[:, kc, pair * P:(pair + 1) * P], k.mix[:, kc, :],
                                          start=kc == 0, stop=kc == 1)
                mm.then_inc(item.sem, 1)
                n += 1
            for tt in range(4):
                bank = free_bank()
                for kc in range(2):
                    mm = nc.tensor.matmul(k.psum[:, bank, :], k.mix[:, kc, tt * P:(tt + 1) * P], uv[:, kc, :],
                                          start=kc == 0, stop=kc == 1)
                mm.then_inc(item.sem, 1)
                n += 1
            wait_weights(k, pe, spec, 0, 1)
            for h in range(HEADS):
                bank = free_bank()
                for kc in range(3):
                    mm = nc.tensor.matmul(k.psum[0:HD + MLA_ROPE, bank, :], uq[:, kc, h, :], k.mix[:, 2 + kc, :],
                                          start=kc == 0, stop=kc == 2)
                mm.then_inc(item.sem, 1)
                n += 1

        @block.vector
        def _(dve):
            for n in range(HEADS // 2 + 4 + HEADS):
                dve.wait_ge(item.sem, item.base + n + 1)
                bank = k.psum[:, n % 8, :]
                if n < 4:
                    for hh in range(2):
                        last = nc.vector.tensor_copy(kn[:, 2 * n + hh, :], bank[hh * HD:(hh + 1) * HD])
                elif n < 8:
                    last = nc.vector.tensor_copy(k.v[:, n - 4, :], bank)
                else:
                    nc.vector.tensor_copy(qn[:, n - 8, :], bank[0:HD])
                    last = nc.vector.tensor_copy(qr[:, n - 8, :], bank[HD:HD + MLA_ROPE])
                last.then_inc(out.sem, 1)
            dve.sem_inc(k.unit_done, 2)
            dve.sem_inc(k.banks_free, 2)
    item.close(16), out.close(16)

    scaled_gains(k, (HD + MLA_ROPE) ** -0.5, ["qg_nope", "qg_rope"])
    norm_heads(k, kn, HD, HEADS, TOK, k.const("mean64"), column(k.vec, k.vec_at["kg_nope"], slice(0, HD)))
    norm_heads(k, qn, HD, HEADS, TOK, k.const("mean64"), column(k.vec, k.vec_at["qg_nope"], slice(0, HD)))
    norm_heads(k, qr, MLA_ROPE, HEADS, TOK, k.const("mean32"), column(k.vec, k.vec_at["qg_rope"], slice(0, MLA_ROPE)))
    rotate_heads(k, qr, MLA_ROPE, 9, k.const("turn32"), k.const("cos32"), k.const("sin32"))

    convolution(k, ypad)
    for queries, keys, tile0, tiles in ((slice(0, LAT), slice(0, TOK), 0, 4), (slice(LAT, TOK), slice(LAT, TOK), 2, 2)):
        def score(ps, b, hh, qt, keys=keys):
            tile = slice(qt * P, (qt + 1) * P)
            nc.tensor.matmul(ps, k.q_stage[0:HD, hh, tile], one(kn, b * 2 + hh, col=keys), start=True, stop=False)
            return nc.tensor.matmul(ps, k.r_stage[0:MLA_ROPE, hh, tile], qr[:, 8, keys], start=False, stop=True)

        attention(k, HEADS // 2, tiles,
                  lambda b: [(k.q_stage[0:HD], qn[:, bass.ds(b * 2, 2), queries]),
                             (k.r_stage[0:MLA_ROPE], qr[:, bass.ds(b * 2, 2), queries])],
                  score, lambda b, hh, kt: k.v[:, tile0 + kt, bass.ds(b * P + hh * HD, HD)], HD,
                  lambda b: one(k.mix, b, col=queries))


def scaled_gains(k, scale, names):
    done = k.tally("derived")
    with k.nc.Block() as block:
        @block.vector
        def _(dve):
            for name in names:
                c = column(k.vec, k.vec_at[name])
                k.nc.vector.tensor_scalar(c, c, scale, None, ALU.mult).then_inc(done.sem, 1)
    done.close(len(names))


def convolution(k, ypad):
    nc, C = k.nc, 4
    t = {n: k.tally(n) for n in ("tap_done", "mean_done", "centred", "squared", "root_done", "inverse_done", "normed")}
    acc = [k.mix[:, 4 + c, :] for c in range(C)]
    with nc.Block() as block:
        @block.vector
        def _(dve):
            for c in range(C):
                w, b = k.vec_at["dw_w"] + c, k.vec_at["dw_b"] + c
                nc.vector.tensor_scalar(acc[c].rearrange("p (s t) -> p s t", s=2), ypad[:, c, :, 0:LAT], column(k.vec, w),
                                        column(k.vec, b), ALU.mult, ALU.add).then_inc(t["tap_done"].sem, 1)
            with dve.Fori(1, CONV_W) as tap:
                for c in range(C):
                    out = acc[c].rearrange("p (s t) -> p s t", s=2)
                    dve.wait_ge(t["tap_done"].sem, tap * C + (t["tap_done"].base + c + 1 - C))
                    nc.vector.scalar_tensor_tensor(out, ypad[:, c, :, bass.ds(tap, LAT)],
                                                   column(k.vec, tap * C + (k.vec_at["dw_w"] + c)), out,
                                                   ALU.mult, ALU.add).then_inc(t["tap_done"].sem, 1)
            dve.wait_ge(t["mean_done"].sem, t["mean_done"].base + 1)
            for c in range(C):
                nc.vector.tensor_tensor(acc[c], acc[c], k.psum[:, 0, :], ALU.subtract).then_inc(t["centred"].sem, 1)
            dve.wait_ge(t["root_done"].sem, t["root_done"].base + 1)
            nc.vector.reciprocal(k.rinv[:, :], k.root[:, :]).then_inc(t["inverse_done"].sem, 1)
            dve.wait_ge(t["inverse_done"].sem, t["inverse_done"].base + 1)
            for c in range(C):
                nc.vector.scalar_tensor_tensor(acc[c], acc[c], column(k.vec, k.vec_at["ln_g"] + c), k.rinv[:, :],
                                               ALU.mult, ALU.mult).then_inc(t["normed"].sem, 1)

        @block.tensor
        def _(pe):
            pe.wait_ge(t["tap_done"].sem, t["tap_done"].base + C * CONV_W)
            for c in range(C):
                mm = nc.tensor.matmul(k.psum[:, 0, :], k.const("mean512"), acc[c], start=c == 0, stop=c == C - 1)
            mm.then_inc(t["mean_done"].sem, 1)
            for c in range(C):
                pe.wait_ge(t["squared"].sem, t["squared"].base + c + 1)
                mm = nc.tensor.matmul(k.psum[:, 1, :], k.const("mean512"), k.h[:, c, :], start=c == 0, stop=c == C - 1)
            mm.then_inc(t["mean_done"].sem, 1)

        @block.scalar
        def _(act):
            for c in range(C):
                act.wait_ge(t["centred"].sem, t["centred"].base + c + 1)
                nc.scalar.activation(k.h[:, c, :], acc[c], ACT.Square).then_inc(t["squared"].sem, 1)
            act.wait_ge(t["mean_done"].sem, t["mean_done"].base + 2)
            nc.scalar.activation(k.root[:, :], k.psum[:, 1, :], ACT.Sqrt, bias=k.eps[:, 0:1]).then_inc(t["root_done"].sem, 1)
            for c in range(C):
                act.wait_ge(t["normed"].sem, t["normed"].base + c + 1)
                nc.scalar.activation(acc[c], acc[c], ACT.Silu, bias=column(k.vec, k.vec_at["ln_b"] + c))
    for name, n in dict(tap_done=C * CONV_W, mean_done=2, centred=C, squared=C, root_done=1, inverse_done=1, normed=C).items():
        t[name].close(n)



def odd_mixer(k, w):
    nc = k.nc
    A = k.arena

    def heads(at, n, t):
        return A[0:HD, at:at + n * t].rearrange("p (h t) -> p h t", h=n)

    ck, nk = heads(0, 2, TOK), heads(2 * TOK, HEADS, TOK)
    cq, nq = heads(10 * TOK, HEADS, LAT), heads(14 * TOK, HEADS, LAT)
    bias = k.side[:, 0:2 * HEADS * LAT].rearrange("p (q h k) -> p q h k", q=2, h=HEADS)

    spec = k.spec("in1")
    first, landed, masked = k.tally("first_bank_out"), k.tally("bias_landed"), k.tally("bias_masked")
    rows = LAT // GRID_W
    with nc.Block() as block:
        stream_ahead(k, block, spec)

        @block.tensor
        def _(pe):
            for c in range(spec.n):
                slot = wait_weights(k, pe, spec, 0, c)
                W = wide_tile(k.slots[slot])
                T = slice(0, TOK if c < 5 else LAT)
                if c in (0, 1, 2, 5, 6, 7, 8):
                    for t in range(1 if c == 0 else 2):
                        for kc in range(KD):
                            mm = nc.tensor.matmul(k.psum[:, 2 * slot + t, T], W[:, kc, t * P:(t + 1) * P], k.h[:, kc, T],
                                                  start=kc == 0, stop=kc == KD - 1)
                if c in (0, 3, 4):
                    n = P if c == 0 else 256
                    for tt in range(4):
                        at = k.psum[:, 2 * slot + 1, tt * P:(tt + 1) * P] if c == 0 else \
                            k.psum[:, 2 * slot + tt // 2, (tt % 2) * n:(tt % 2 + 1) * n]
                        for kc in range(KD):
                            mm = nc.tensor.matmul(at, k.h[:, kc, tt * P:(tt + 1) * P], W[:, kc, 256 - n:256],
                                                  start=kc == 0, stop=kc == KD - 1)
                mm.then_inc(k.unit_done, 1)

        def place(engine, copy, bank, c):
            slot = (spec.start + c) % RING
            src = k.psum[:, 2 * slot + bank, :]
            if c == 0 and bank == 1:
                return copy(k.v_shared[:, :, :], src.rearrange("p (t e) -> p t e", t=4))
            if c in (3, 4):
                return copy(k.v[:, 2 * bank:2 * bank + 2, (c - 3) * 256:(c - 2) * 256], src.rearrange("p (t e) -> p t e", t=2))
            to, h, T = {0: (ck, 0, TOK), 1: (nk, 0, TOK), 2: (nk, 4, TOK), 5: (cq, 0, LAT), 6: (cq, 4, LAT),
                        7: (nq, 0, LAT), 8: (nq, 4, LAT)}[c]
            for hh in range(2):
                last = copy(to[:, h + 2 * bank + hh, :], src[hh * HD:(hh + 1) * HD, 0:T])
            return last

        @block.scalar
        def _(act):
            for r in range(rows):
                for j in range(rows):
                    src = bass.AP(w["l1_na_rpb"].tensor, (j - r + RPB_H // 2) * RPB_W + RPB_W // 2 - GRID_W + 1,
                                  [[1, GRID_W], [RPB_H * RPB_W, HEADS], [1, GRID_W]])
                    dst = bias[(r % 2) * GRID_W:(r % 2 + 1) * GRID_W, r // 2, :, j * GRID_W:(j + 1) * GRID_W]
                    act.dma_start(dst, src).then_inc(landed.sem, 16)
            for c in range(spec.n):
                wait_product(k, act, spec, 0, c)
                place(act, lambda o, i: nc.scalar.activation(o, i, ACT.Copy), 0, c).then_inc(first.sem, 1)

        @block.vector
        def _(dve):
            for c in range(spec.n):
                wait_product(k, dve, spec, 0, c)
                dve.wait_ge(first.sem, first.base + c + 1)
                place(dve, nc.vector.tensor_copy, 1, c).then_inc(k.banks_free, 1)
            dve.wait_ge(landed.sem, landed.base + 16 * rows * rows)
            for qt in range(2):
                for h in range(HEADS):
                    nc.vector.tensor_tensor(bias[:, qt, h, :], bias[:, qt, h, :], k.const("window"), ALU.add)\
                        .then_inc(masked.sem, 1)
    first.close(spec.n), landed.close(16 * rows * rows), masked.close(2 * HEADS)

    scaled_gains(k, HD ** -0.5, ["gqa_q", "na_q"])
    for src, n, T, gain in ((ck, 2, TOK, "gqa_k"), (nk, HEADS, TOK, "na_k"), (cq, HEADS, LAT, "gqa_q"), (nq, HEADS, LAT, "na_q")):
        if T == LAT:
            src = src.rearrange("p (a b) t -> p a (b t)", b=2)
            n //= 2
        norm_heads(k, src, HD, n, TOK, k.const("mean64"), column(k.vec, k.vec_at[gain], slice(0, HD)))
    rotate_heads(k, ck, HD, 2, k.const("turn64"), k.const("cos64"), k.const("sin64"))
    rotate_heads(k, cq, HD, HEADS, k.const("turn64"), k.const("cos64"), k.const("sin64"))

    for g in range(2):
        def score(ps, b, hh, qt, g=g):
            return nc.tensor.matmul(ps, k.q_stage[0:HD, hh, qt * P:(qt + 1) * P], ck[:, g, :], start=True, stop=True)

        attention(k, 2, 4, lambda b: [(k.q_stage[0:HD], cq[:, bass.ds(b * 2 + 4 * g, 2), :])], score,
                  lambda b, hh, kt: k.v_shared[:, kt, g * HD:(g + 1) * HD], HD, lambda b: one(k.mix, b + 2 * g, col=slice(0, LAT)))

    def score(ps, b, hh, qt):
        nc.tensor.matmul(ps, k.q_stage[0:HD, hh, qt * P:(qt + 1) * P], one(nk, b * 2 + hh), start=True, stop=False)
        return nc.tensor.matmul(ps[:, 0:LAT], k.const("flip"), one(bias[:, qt], b * 2 + hh), start=False, stop=True)

    attention(k, HEADS // 2, 4, lambda b: [(k.q_stage[0:HD], nq[:, bass.ds(b * 2, 2), :])], score,
              lambda b, hh, kt: k.v[:, kt, bass.ds(b * P + hh * HD, HD)], HD, lambda b: one(k.mix, b + 4, col=slice(0, LAT)))



def rope_tables(k):
    nc = k.nc
    step, done, landed = k.tally("angle_step"), k.tally("table_done"), k.tally("selector_landed")
    R = slice(0, ROPE2)
    ang, turns, low = k.square[R, 0, 0:LAT], k.square[R, 1, 0:LAT], k.roots[R, 0, 0:LAT]
    magic = 1.5 * 2.0 ** 23
    two_pi = 2 * np.pi
    c1 = 6.28125
    c2 = float(np.float32(two_pi - c1))
    c3 = float(two_pi - c1 - c2)
    with nc.Block() as block:
        @block.vector
        def _(dve):
            n = [0]

            def chained(ins):
                n[0] += 1
                ins.then_inc(step.sem, 1)
                dve.wait_ge(step.sem, step.base + n[0])

            chained(nc.vector.tensor_copy(ang, k.positions[:, :]))
            chained(nc.vector.tensor_scalar(ang, ang, k.const("freq")[:, 0:1], None, ALU.mult))
            chained(nc.vector.tensor_scalar(turns, ang, float(1 / two_pi), magic, ALU.mult, ALU.add))
            chained(nc.vector.tensor_scalar(turns, turns, -magic, None, ALU.add))
            for c in (c1, c2, c3):
                chained(nc.vector.scalar_tensor_tensor(ang, turns, -c, ang, ALU.mult, ALU.add))
            top = float(np.nextafter(np.float32(np.pi), np.float32(0)))
            chained(nc.vector.tensor_scalar(ang, ang, top, -top, ALU.min, ALU.max))

        @block.scalar
        def _(act):
            act.wait_ge(step.sem, step.base + 8)
            nc.scalar.activation(low, ang, ACT.Abs).then_inc(done.sem, 1)
            nc.scalar.activation(k.sin2, ang, ACT.Sin).then_inc(done.sem, 1)
            act.wait_ge(done.sem, done.base + 1)
            nc.scalar.activation(k.cos2, low, ACT.Sin, scale=-1.0, bias=k.half_pi[R, 0:1]).then_inc(done.sem, 1)

        @block.sync
        def _(sp):
            sp.dma_start(k.sel, k.selector).then_inc(landed.sem, 16)
            sp.wait_ge(landed.sem, landed.base + 16)
    step.close(8), done.close(3), landed.close(16)


def lambda_init(l):
    return 0.8 - 0.6 * float(np.exp(-0.3 * l))


HEAD_AT = dict(aq=0, ak=8, dq=16, dk=20, iq=24, ik=32, bq=33, bk=37, cq=41, ck=45)
N_HEADS2 = 49
SCALED_UNITS = (0, 1, 4, 8, 10)


def project_heads(k, l):
    nc, spec = k.nc, k.spec(f"in_b{l}")
    first = k.tally("first_bank_out")
    T = slice(0, LAT)
    n_qk, n_v = len(QK_COLUMNS), len(V_COLUMNS)
    values = [k.va[:, :, 0:256], k.va[:, :, 256:512], k.bv, k.cv, k.dv]
    with nc.Block() as block:
        stream_ahead(k, block, spec)

        @block.tensor
        def _(pe):
            for c in range(spec.n):
                slot = wait_weights(k, pe, spec, 0, c)
                W = wide_tile(k.slots[slot])
                b0, b1 = k.psum[:, 2 * slot], k.psum[:, 2 * slot + 1]
                if c < n_qk:
                    parts = [(bank[:, T], lambda kc, t=t: W[:, kc, t * P:(t + 1) * P], lambda kc: k.h[:, kc, T])
                             for t, bank in enumerate((b0, b1))]
                elif c < n_qk + n_v:
                    parts = [(bank[:, T], lambda kc, t=t: k.h[:, kc, t * P:(t + 1) * P], lambda kc: W[:, kc, :])
                             for t, bank in enumerate((b0, b1))]
                else:
                    parts = [(b0[0:HD, T], lambda kc: W[:, kc, 0:HD], lambda kc: k.h[:, kc, T]),
                             (b0[0:4, LAT:TOK], lambda kc: W[:, kc, 72:76], lambda kc: k.h[:, kc, T])]
                    parts += [(b1[:, t * 8:(t + 1) * 8], lambda kc, t=t: k.h[:, kc, t * P:(t + 1) * P],
                               lambda kc: W[:, kc, HD:72]) for t in range(2)]
                for to, lhs, rhs in parts:
                    for kc in range(KD):
                        mm = nc.tensor.matmul(to, lhs(kc), rhs(kc), start=kc == 0, stop=kc == KD - 1)
                mm.then_inc(k.unit_done, 1)

        def head_of(c):
            return 4 * c if c < 8 else HEAD_AT["bq"] + 4 * (c - 8)

        @block.scalar
        def _(act):
            for c in range(spec.n):
                slot = wait_product(k, act, spec, 0, c)
                bank = k.psum[:, 2 * slot]
                if c < n_qk:
                    for hh in range(2):
                        last = nc.scalar.activation(k.heads[:, head_of(c) + hh, :], bank[hh * HD:(hh + 1) * HD, T], ACT.Copy,
                                                    scale=HD ** -0.5 if c in SCALED_UNITS else 1.0)
                elif c < n_qk + n_v:
                    last = nc.scalar.activation(values[c - n_qk][:, 0], bank[:, T], ACT.Copy)
                else:
                    nc.scalar.activation(k.heads[:, HEAD_AT["ik"], :], bank[0:HD, T], ACT.Copy)
                    last = nc.scalar.activation(k.forget, bank[0:4, LAT:TOK], ACT.Identity,
                                                bias=column(k.vec, k.vec_at[f"fgt{l}"], slice(0, 4)))
                last.then_inc(first.sem, 1)

        @block.vector
        def _(dve):
            for c in range(spec.n):
                slot = wait_product(k, dve, spec, 0, c)
                dve.wait_ge(first.sem, first.base + c + 1)
                bank = k.psum[:, 2 * slot + 1]
                if c < n_qk:
                    for hh in range(2):
                        last = nc.vector.tensor_scalar(k.heads[:, head_of(c) + 2 + hh, :], bank[hh * HD:(hh + 1) * HD, T],
                                                       HD ** -0.5 if c in SCALED_UNITS else 1.0, None, ALU.mult)
                elif c < n_qk + n_v:
                    last = nc.vector.tensor_copy(values[c - n_qk][:, 1], bank[:, T])
                else:
                    last = nc.vector.tensor_copy(k.index_weight, bank[:, 0:16])
                last.then_inc(k.banks_free, 1)
    first.close(spec.n)


def log_sigmoids(k, l):
    nc = k.nc
    t = {n: k.tally(n) for n in ("magnitude", "exp_done", "log_done", "sum_step", "dots", "lambda_exp")}
    mag, low = k.square[0:4, 0, 0:LAT], k.square[0:4, 1, 0:LAT]
    with nc.Block() as block:
        @block.vector
        def _(dve):
            nc.vector.memset(k.ones_row, 1.0).then_inc(t["sum_step"].sem, 1)
            for v in range(2):
                nc.vector.scalar_tensor_tensor(k.roots[:, v, 0:HD], k.lam[:, l, 2 * v, :], 1.0, k.lam[:, l, 2 * v + 1, :],
                                               ALU.mult, ALU.mult, accum_out=k.lam_exp[:, v:v + 1]).then_inc(t["dots"].sem, 1)
            dve.wait_ge(t["log_done"].sem, t["log_done"].base + 1)
            nc.vector.scalar_tensor_tensor(low, k.forget, 0.0, mag, ALU.min, ALU.subtract).then_inc(t["sum_step"].sem, 1)
            dve.wait_ge(t["sum_step"].sem, t["sum_step"].base + 2)
            nc.vector.tensor_tensor_scan(k.cum, k.ones_row, low, 0.0, ALU.mult, ALU.add).then_inc(t["sum_step"].sem, 1)
            dve.wait_ge(t["sum_step"].sem, t["sum_step"].base + 3)
            for h in range(4):
                nc.vector.scalar_tensor_tensor(k.minus_cum[:, h, :], k.sel[:, h, :], -1.0, k.cum, ALU.mult, ALU.mult)\
                    .then_inc(t["sum_step"].sem, 1)
            dve.wait_ge(t["lambda_exp"].sem, t["lambda_exp"].base + 1)
            nc.vector.tensor_scalar(k.lam_exp[:, 1:2], k.lam_exp[:, 1:2], -lambda_init(l), None, ALU.add)\
                .then_inc(t["sum_step"].sem, 1)
            dve.wait_ge(t["sum_step"].sem, t["sum_step"].base + 8)
            nc.vector.tensor_tensor(k.minus_lam, k.lam_exp[:, 1:2], k.lam_exp[:, 0:1], ALU.subtract).then_inc(t["sum_step"].sem, 1)

        @block.scalar
        def _(act):
            nc.scalar.activation(mag, k.forget, ACT.Abs).then_inc(t["magnitude"].sem, 1)
            act.wait_ge(t["magnitude"].sem, t["magnitude"].base + 1)
            nc.scalar.activation(mag, mag, ACT.Exp, scale=-1.0).then_inc(t["exp_done"].sem, 1)
            act.wait_ge(t["dots"].sem, t["dots"].base + 2)
            nc.scalar.activation(k.lam_exp[:, 0:2], k.lam_exp[:, 0:2], ACT.Exp).then_inc(t["lambda_exp"].sem, 1)
            act.wait_ge(t["exp_done"].sem, t["exp_done"].base + 1)
            nc.scalar.activation(mag, mag, ACT.Ln, bias=1.0).then_inc(t["log_done"].sem, 1)
    for name, n in dict(magnitude=1, exp_done=1, log_done=1, sum_step=9, dots=2, lambda_exp=1).items():
        t[name].close(n)


def select_keys(k):
    nc = k.nc
    t = {n: k.tally(n) for n in ("scored", "rectified", "summed", "best_found", "taken")}
    n_pairs, rounds = 4, TOPK // 8
    with nc.Block() as block:
        @block.tensor
        def _(pe):
            for qt in range(2):
                for j in range(n_pairs):
                    n = qt * n_pairs + j
                    for jj in range(2):
                        mm = nc.tensor.matmul(k.psum[:, n, jj * LAT:(jj + 1) * LAT],
                                              k.heads[:, HEAD_AT["iq"] + 2 * j + jj, qt * P:(qt + 1) * P],
                                              k.heads[:, HEAD_AT["ik"], :], start=True, stop=True)
                    mm.then_inc(t["scored"].sem, 1)

        @block.scalar
        def _(act):
            for n in range(2 * n_pairs):
                act.wait_ge(t["scored"].sem, t["scored"].base + n + 1)
                if n >= 2:
                    act.wait_ge(t["summed"].sem, t["summed"].base + 2 * (n - 1))
                nc.scalar.activation(k.square[:, n % 2, :], k.psum[:, n, :], ACT.Relu).then_inc(t["rectified"].sem, 1)

        @block.vector
        def _(dve):
            for n in range(2 * n_pairs):
                qt, j = n // n_pairs, n % n_pairs
                dve.wait_ge(t["rectified"].sem, t["rectified"].base + n + 1)
                for jj in range(2):
                    if (j, jj) == (0, 0):
                        before = k.const("causal")[:, qt * LAT:(qt + 1) * LAT]
                    else:
                        before = k.score[:, qt, :]
                        dve.wait_ge(t["summed"].sem, t["summed"].base + 2 * n + jj)
                    nc.vector.scalar_tensor_tensor(k.score[:, qt, :], k.square[:, n % 2, jj * LAT:(jj + 1) * LAT],
                                                   k.index_weight[:, qt * 8 + 2 * j + jj:qt * 8 + 2 * j + jj + 1], before,
                                                   ALU.mult, ALU.add).then_inc(t["summed"].sem, 1)
            dve.wait_ge(t["summed"].sem, t["summed"].base + 4 * n_pairs)
            for r in range(rounds):
                for qt in range(2):
                    if r:
                        dve.wait_ge(t["taken"].sem, t["taken"].base + 2 * (r - 1) + qt + 1)
                    nc.vector.max(k.best[:, qt, :], k.score[:, qt, :]).then_inc(t["best_found"].sem, 1)
                for qt in range(2):
                    dve.wait_ge(t["best_found"].sem, t["best_found"].base + 2 * r + qt + 1)
                    nc.vector.match_replace(k.score[:, qt, :], k.best[:, qt, :], k.score[:, qt, :], TAKEN).then_inc(t["taken"].sem, 1)
            for qt in range(2):
                dve.wait_ge(t["taken"].sem, t["taken"].base + 2 * rounds + qt - 1)
                nc.vector.tensor_scalar(k.chosen[:, qt, :], k.score[:, qt, :], TAKEN / 2, MASKED, ALU.is_gt, ALU.mult)\
                    .then_inc(t["taken"].sem, 1)
            for qt in range(2):
                dve.wait_ge(t["taken"].sem, t["taken"].base + 2 * rounds + qt + 1)
                nc.vector.tensor_tensor(k.chosen[:, qt, :], k.chosen[:, qt, :], k.const("causal")[:, qt * LAT:(qt + 1) * LAT], ALU.add)\
                    .then_inc(t["taken"].sem, 1)
    for name, n in dict(scored=2 * n_pairs, rectified=2 * n_pairs, summed=4 * n_pairs, best_found=2 * rounds,
                        taken=2 * rounds + 4).items():
        t[name].close(n)


def stick_breaking(k):
    nc, N = k.nc, 4
    names = ("logits", "magnitude", "exp_done", "log_done", "softplus", "kept", "summed_later", "in_exponent", "exponent",
             "weight_exp", "masked", "weighted", "placed")
    t = {n: k.tally("sb_" + n) for n in names}
    strict = k.const("strict")

    def buf(h):
        return k.square[:, h % 2, :], k.roots[:, h % 2, :], k.rinvs[:, h % 2, :]

    def weigh(pe, h):
        _, _, weights = buf(h)
        pe.wait_ge(t["masked"].sem, t["masked"].base + h + 1)
        if h >= 2:
            pe.wait_ge(t["placed"].sem, t["placed"].base + h - 1)
        for kt in range(2):
            mm = nc.tensor.matmul(k.psum[0:HD, 6 + h % 2, 0:LAT], k.cv[:, kt, h * HD:(h + 1) * HD],
                                  weights[:, kt * LAT:(kt + 1) * LAT], start=kt == 0, stop=kt == 1)
        mm.then_inc(t["weighted"].sem, 1)

    with nc.Block() as block:
        @block.tensor
        def _(pe):
            for h in range(N):
                for kt in range(2):
                    mm = nc.tensor.matmul(k.psum[:, h, kt * LAT:(kt + 1) * LAT],
                                          k.heads[:, HEAD_AT["ck"] + h, kt * P:(kt + 1) * P],
                                          k.heads[:, HEAD_AT["cq"] + h, :], start=True, stop=True)
                mm.then_inc(t["logits"].sem, 1)
            for h in range(N):
                _, _, kept = buf(h)
                pe.wait_ge(t["kept"].sem, t["kept"].base + h + 1)
                if h >= 2:
                    pe.wait_ge(t["exponent"].sem, t["exponent"].base + h - 1)
                bank = k.psum[:, 4 + h % 2, :]
                nc.tensor.matmul(bank[:, 0:LAT], k.const("later"), kept[:, 0:LAT], start=True, stop=False)
                nc.tensor.matmul(bank[:, 0:LAT], k.const("ones"), kept[:, LAT:TOK], start=False, stop=True)
                nc.tensor.matmul(bank[:, LAT:TOK], k.const("later"), kept[:, LAT:TOK], start=True, stop=True)\
                    .then_inc(t["summed_later"].sem, 1)
                if h >= 1:
                    weigh(pe, h - 1)
            weigh(pe, N - 1)

        @block.vector
        def _(dve):
            def middle(h):
                low, soft, kept = buf(h)
                dve.wait_ge(t["log_done"].sem, t["log_done"].base + h + 1)
                if h >= 2:
                    dve.wait_ge(t["masked"].sem, t["masked"].base + h - 1)
                nc.vector.scalar_tensor_tensor(soft, k.psum[:, h, :], 0.0, low, ALU.max, ALU.add).then_inc(t["softplus"].sem, 1)
                dve.wait_ge(t["softplus"].sem, t["softplus"].base + h + 1)
                if h >= 2:
                    dve.wait_ge(t["weighted"].sem, t["weighted"].base + h - 1)
                nc.vector.scalar_tensor_tensor(kept, soft, -1.0, strict, ALU.mult, ALU.mult).then_inc(t["kept"].sem, 1)
                nc.vector.tensor_tensor(low, k.psum[:, h, :], soft, ALU.subtract).then_inc(t["in_exponent"].sem, 1)
                dve.wait_ge(t["in_exponent"].sem, t["in_exponent"].base + h + 1)
                dve.wait_ge(t["summed_later"].sem, t["summed_later"].base + h + 1)
                nc.vector.tensor_tensor(soft, low, k.psum[:, 4 + h % 2, :], ALU.add).then_inc(t["exponent"].sem, 1)

            def end(h):
                low, soft, kept = buf(h)
                dve.wait_ge(t["weight_exp"].sem, t["weight_exp"].base + h + 1)
                nc.vector.tensor_tensor(kept, soft, strict, ALU.mult).then_inc(t["masked"].sem, 1)

            middle(0), middle(1)
            for h in range(N):
                end(h)
                if h >= 1 and h + 1 < N:
                    middle(h + 1)

        @block.scalar
        def _(act):
            def begin(h):
                low, soft, kept = buf(h)
                act.wait_ge(t["logits"].sem, t["logits"].base + h + 1)
                if h >= 2:
                    act.wait_ge(t["exponent"].sem, t["exponent"].base + h - 1)
                nc.scalar.activation(low, k.psum[:, h, :], ACT.Abs).then_inc(t["magnitude"].sem, 1)
                act.wait_ge(t["magnitude"].sem, t["magnitude"].base + h + 1)
                nc.scalar.activation(low, low, ACT.Exp, scale=-1.0).then_inc(t["exp_done"].sem, 1)
                act.wait_ge(t["exp_done"].sem, t["exp_done"].base + h + 1)
                nc.scalar.activation(low, low, ACT.Ln, bias=1.0).then_inc(t["log_done"].sem, 1)

            def end(h):
                low, soft, kept = buf(h)
                act.wait_ge(t["exponent"].sem, t["exponent"].base + h + 1)
                nc.scalar.activation(soft, soft, ACT.Exp).then_inc(t["weight_exp"].sem, 1)

            def place(h):
                act.wait_ge(t["weighted"].sem, t["weighted"].base + h + 1)
                nc.scalar.activation(k.mix[(h % 2) * HD:(h % 2 + 1) * HD, 6 + h // 2, 0:LAT], k.psum[0:HD, 6 + h % 2, 0:LAT],
                                     ACT.Copy).then_inc(t["placed"].sem, 1)

            begin(0), begin(1)
            for h in range(N):
                end(h)
                if h + 2 < N:
                    begin(h + 2)
                if h >= 1:
                    place(h - 1)
            place(N - 1)
    for name in names:
        t[name].close(N)


def merge_branches(k, l):
    nc, spec = k.nc, k.spec(f"merge_b{l}")
    T = slice(0, LAT)
    opened, product, summed = (k.tally(n) for n in ("gates_open", "gated", "gated_sum"))
    bias = k.vec_at[f"gate_b{l}"]
    y = dict(a=[k.mix[:, c, T] for c in range(4)], b=[k.mix[:, c, T] for c in (4, 5)],
             c=[k.mix[:, c, T] for c in (6, 7)], d=[k.mix[:, c, LAT:TOK] for c in range(2)])
    parts = [[(0, 16, y["a"]), (3, 20, y["d"])], [(1, 16, y["b"]), (2, 18, y["c"])]]
    with nc.Block() as block:
        stream_ahead(k, block, spec)

        @block.tensor
        def _(pe):
            def unit(i, c):
                slot = wait_weights(k, pe, spec, i, c)
                W = tall_tile(k.slots[slot])
                for n, (_, row, chunks) in enumerate(parts[c % 2]):
                    half = slice(n * LAT, (n + 1) * LAT)
                    for kc in range(KD):
                        nc.tensor.matmul(k.psum[:, 2 * slot, half], W[:, n * KD + kc, :], k.h[:, kc, T],
                                         start=kc == 0, stop=kc == KD - 1)
                    for kc, chunk in enumerate(chunks):
                        mm = nc.tensor.matmul(k.psum[:, 2 * slot + 1, half], W[:, row + kc, :], chunk,
                                              start=kc == 0, stop=kc == len(chunks) - 1)
                mm.then_inc(k.unit_done, 1)
            each_unit(pe, 0, spec.n, unit)

        @block.scalar
        def _(act):
            def unit(i, c):
                slot = wait_product(k, act, spec, i, c)
                act.wait_ge(k.banks_free, i * RING + (RING + spec.start + c - 1))
                for n, (gate, _, _) in enumerate(parts[c % 2]):
                    at = i * (RING // 2) + (bias + gate * KD + c // 2)
                    last = nc.scalar.activation(k.square[:, c % 2, n * LAT:(n + 1) * LAT],
                                                k.psum[:, 2 * slot, n * LAT:(n + 1) * LAT], ACT.Sigmoid,
                                                bias=column(k.vec, at))
                last.then_inc(opened.sem, 1)
            each_unit(act, 0, spec.n, unit)

        @block.vector
        def _(dve):
            def unit(i, c):
                slot = wait_product(k, dve, spec, i, c)
                dve.wait_ge(opened.sem, i * RING + (opened.base + c + 1))
                tmp = k.roots[:, c % 2, :]
                nc.vector.tensor_tensor(tmp, k.square[:, c % 2, :], k.psum[:, 2 * slot + 1, :], ALU.mult).then_inc(product.sem, 1)
                dve.wait_ge(product.sem, i * RING + (product.base + c + 1))
                row = one(k.merged, i * (RING // 2) + c // 2)
                if c % 2 == 0:
                    nc.vector.tensor_tensor(row, tmp[:, 0:LAT], tmp[:, LAT:TOK], ALU.add).then_inc(k.banks_free, 1)
                else:
                    nc.vector.tensor_tensor(row, row, tmp[:, 0:LAT], ALU.add).then_inc(summed.sem, 1)
                    dve.wait_ge(summed.sem, i * (RING // 2) + (summed.base + c // 2 + 1))
                    nc.vector.tensor_tensor(row, row, tmp[:, LAT:TOK], ALU.add).then_inc(k.banks_free, 1)
            each_unit(dve, 0, spec.n, unit)
    opened.close(spec.n), product.close(spec.n), summed.close(spec.n // 2)


def hybrid_mixer(k, l):
    nc = k.nc
    causal = [k.const("causal")[:, qt * LAT:(qt + 1) * LAT] for qt in range(2)]
    project_heads(k, l)
    rotate_heads(k, k.heads, ROPE2, HEAD_AT["ik"] + 1, k.const("turn16"), k.cos2, k.sin2)
    log_sigmoids(k, l)

    def logits(ps, q, hh, qt, key_head, last=False):
        return nc.tensor.matmul(ps, k.q_stage[0:HD, hh, qt * P:(qt + 1) * P], one(k.heads, key_head), start=True, stop=last)

    def queries(name):
        return lambda b: [(k.q_stage[0:HD], k.heads[:, bass.ds(b * 2 + HEAD_AT[name], 2), :])]

    def score(ps, b, hh, qt):
        logits(ps, "aq", hh, qt, b * 2 + (HEAD_AT["ak"] + hh))
        return nc.tensor.matmul(ps, k.const("ident"), causal[qt], start=False, stop=True)

    attention(k, 4, 2, queries("aq"), score, lambda b, hh, kt: k.va[:, kt, bass.ds(b * P, P)], P,
              lambda b: one(k.mix, b, col=slice(0, LAT)), difference=k.minus_lam)
    scaled_gains(k, 1.0 - lambda_init(l), [f"diff{l}"])
    norm_heads(k, k.mix, P, 4, LAT, k.const("ones"), column(k.vec, k.vec_at[f"diff{l}"]), scale=1.0 / P, eps=k.eps5)

    def score(ps, b, hh, qt):
        logits(ps, "bq", hh, qt, b * 2 + (HEAD_AT["bk"] + hh))
        nc.tensor.matmul(ps, k.const("ident"), causal[qt], start=False, stop=False)
        nc.tensor.matmul(ps, k.cum[:, qt * P:(qt + 1) * P], one(k.sel, b * 2 + hh), start=False, stop=False)
        return nc.tensor.matmul(ps, k.const("ones")[0:4, :], one(k.minus_cum, b * 2 + hh), start=False, stop=True)

    attention(k, 2, 2, queries("bq"), score, lambda b, hh, kt: k.bv[:, kt, bass.ds(b * P + hh * HD, HD)], HD,
              lambda b: one(k.mix, b + 4, col=slice(0, LAT)))

    stick_breaking(k)

    select_keys(k)

    def score(ps, b, hh, qt):
        logits(ps, "dq", hh, qt, b * 2 + (HEAD_AT["dk"] + hh))
        return nc.tensor.matmul(ps, k.const("ident"), k.chosen[:, qt, :], start=False, stop=True)

    attention(k, 2, 2, queries("dq"), score, lambda b, hh, kt: k.dv[:, kt, bass.ds(b * P + hh * HD, HD)], HD,
              lambda b: one(k.mix, b, col=slice(LAT, TOK)))
    merge_branches(k, l)
    add_product(k, k.spec(f"out_b{l}"), LAT, k.merged, KD, wide_lhs, 2, 1.0)


def second_block(k, w):
    k.heads = k.arena[0:HD, 0:N_HEADS2 * LAT].rearrange("p (h t) -> p h t", h=N_HEADS2)
    k.merged = k.arena[:, 0:KD * LAT].rearrange("p (c t) -> p c t", c=KD)
    k.va = k.v[:, 0:2, :]
    k.bv, k.cv = (k.v[:, n, :].rearrange("p (t e) -> p t e", t=2) for n in (2, 3))
    k.dv = k.v_shared[:, :, :].rearrange("p a b -> p (a b)").rearrange("p (t e) -> p t e", t=2)
    at = [0]

    def side(rows, *shape):
        n = int(np.prod(shape))
        part = k.side[0:rows, at[0]:at[0] + n]
        at[0] += n
        return part if len(shape) == 1 else part.rearrange("p (a b) -> p a b", a=shape[0])

    k.sel, k.minus_cum = side(4, 4, LAT), side(4, 4, LAT)
    k.forget, k.cum, k.ones_row = side(4, LAT), side(4, LAT), side(4, LAT)
    k.chosen, k.score = side(P, 2, LAT), side(P, 2, LAT)
    k.best, k.index_weight = side(P, 2, 8), side(P, 16)
    k.lam_exp, k.minus_lam = side(P, 2), side(P, 1)
    k.cos2, k.sin2 = k.r_stage[0:ROPE2, 0, :], k.r_stage[0:ROPE2, 1, :]
    k.selector = w["selector"].rearrange("j (h t) -> j h t", h=4)
    rope_tables(k)
    for l in (0, 1):
        for m in ("ffn1", "mix", "ffn2"):
            at_gain = k.vec_at[f"{m}_b{l}"]
            gain = lambda c, cond, at_gain=at_gain: column(k.vec, at_gain + c)
            if m == "mix":
                norm_tokens(k, LAT, gain)
                hybrid_mixer(k, l)
            else:
                half_ffn(k, LAT, (f"{m}_in_b{l}", f"{m}_out_b{l}"), gain, None, 0.5)



def program(nc, w, out):
    rows, vec_at = vector_rows()
    _, const_at = constant_table()
    with ExitStack() as ctx:
        def sb(name, shape, dt=F32):
            return ctx.enter_context(nc.sbuf_tensor(name, shape, dt))

        tallies = {}

        def tally(name):
            if name not in tallies:
                tallies[name] = Tally(ctx.enter_context(nc.semaphore(name)))
            return tallies[name]

        k = Shared()
        k.nc, k.tally = nc, tally
        k.vec_rows, k.vec_at, k.n_rows = rows, vec_at, sum(r[2] for r in rows)
        n_const = sum(n for _, _, n in const_at.values())
        k.consts = sb("consts", [P, n_const])
        k.const = lambda name: k.consts[0:const_at[name][0], const_at[name][1]:const_at[name][1] + const_at[name][2]]
        k.vec = sb("vec", [P, 4 * P])
        k.eps, k.eps5, k.half_pi = sb("eps", [P, 1]), sb("eps5", [P, 1]), sb("half_pi", [P, 1])
        k.cond = sb("cond", [P, KD, 2])
        k.mod = sb("mod", [P, N_MOD * KD, 2])
        k.gain, k.gate = sb("gain", [P, 3, KD, 2]), sb("gate", [P, 2, KD, 2])
        k.lam = sb("lam", [P, 2, 4, HD])
        k.positions = sb("positions", [ROPE2, LAT], mybir.dt.int32)
        k.x, k.h, k.mix = sb("x", [P, KD, TOK]), sb("h", [P, KD, TOK]), sb("mix", [P, KD, TOK])
        k.arena = sb("arena", [P, 12800])
        k.side = sb("side", [P, 4096])
        k.slots = [sb(f"weights{s}", [P, SLOT]) for s in range(RING)]
        k.v, k.v_shared = sb("v", [P, 4, 512]), sb("v_shared", [P, 4, P])
        k.prob = lambda j, keys: k.h[:, j, TOK - keys:TOK]
        k.prob_t = lambda u, keys: k.h[:, 4 + u, TOK - keys:TOK]
        k.out_rows = k.h[:, 6, LAT:TOK].rearrange("p (q e) -> p q e", q=2)
        k.q_stage, k.r_stage = sb("q_stage", [HD, 2, LAT]), sb("r_stage", [MLA_ROPE, 2, LAT])
        k.negmax, k.rowsum, k.inverse = sb("negmax", [P, 4]), sb("rowsum", [P, 4]), sb("inverse", [P, 8])
        k.square, k.roots, k.rinvs = sb("square", [P, 2, TOK]), sb("roots", [P, 2, TOK]), sb("rinvs", [P, 2, TOK])
        k.root, k.rinv = k.roots[:, 0, :], k.rinvs[:, 0, :]
        k.psum = ctx.enter_context(nc.psum_tensor("psum", [P, 8, BANK], F32))
        k.weights_ready = [ctx.enter_context(nc.semaphore(f"weights_ready{s}")) for s in range(RING)]
        k.unit_done = ctx.enter_context(nc.semaphore("unit_done"))
        k.banks_free = ctx.enter_context(nc.semaphore("banks_free"))
        k.plan = weight_plan(w)
        k.spec = lambda name: next(s for s in k.plan if s.name == name)

        opening(k, w)
        for l in (0, 1):
            conditioning(k, l)
            tokens = TOK
            half_ffn(k, tokens, (f"ffn1_in{l}", f"ffn1_out{l}"), *modulated(k, 0), half_gate(k, 0))
            norm_tokens(k, tokens, *modulated(k, 1))
            if l == 0:
                even_mixer(k)
            else:
                odd_mixer(k, w)
                tokens = LAT
            add_product(k, k.spec(f"out{l}"), tokens, k.mix, KD, wide_lhs, 2, mix_gate(k))
            half_ffn(k, tokens, (f"ffn2_in{l}", f"ffn2_out{l}"), *modulated(k, 2), half_gate(k, 1))
        second_block(k, w)
        final = vec_at["final"]
        norm_tokens(k, LAT, lambda c, cond: column(k.vec, final + c))
        ending(k, out)



def kernel(**inputs):
    import concourse.bacc as bacc
    from concourse.bass_utils import run_bass_kernel_spmd

    nc = bacc.Bacc("TRN2", target_bir_lowering=False, num_devices=1)
    arrays, w = {}, {}
    for name, value in {**inputs, "constants": constant_table()[0], "selector": selector()}.items():
        a = np.ascontiguousarray(value)
        arrays["in_" + name] = a
        w[name] = nc.dram_tensor("in_" + name, a.shape, mybir.dt.from_np(a.dtype), kind="ExternalInput").ap()
    out = nc.dram_tensor("out", (1, LAT, D), F32, kind="ExternalOutput").ap()
    program(nc, w, out)
    return run_bass_kernel_spmd(nc, [arrays], core_ids=[0]).results[0]["out"]
```

```python
from contextlib import ExitStack

import numpy as np

import concourse.bass as bass
from concourse import mybir

F32 = mybir.dt.float32
F32R = mybir.dt.float32r
ACT = mybir.ActivationFunctionType
ALU = mybir.AluOpType
AX = mybir.AxisListType

P = 128
D = 1024
KD = D // P
LAT, CTX = 256, 256
TOK = LAT + CTX
FF = 2816
KF = FF // P
N_MOD = 9
EPS = 1e-6
HD = 64
HEADS = 8
MLA_ROPE = 32
GRID_W = 64
WIN_W = 16
RPB_H, RPB_W = 15, 31
CONV_W = 31
PAD = CONV_W // 2
ROPE2 = 16
TOPK = 64
BANK = 512

QK_COLUMNS = (0, 256, 512, 768, 3076, 3332, 3844, 4100, 1536, 1792, 2308, 2564)
V_COLUMNS = (1024, 1280, 2048, 2820, 3588)

RING = 4
SLOT = KF * P
MASKED = -1.0e30
TAKEN = -3.0e38


class Tally:

    def __init__(self, sem):
        self.sem, self.base = sem, 0

    def close(self, n):
        self.base += n


class Product:

    def __init__(self, name, n, load, looped, dmas):
        self.name, self.n, self.load, self.looped, self.dmas = name, n, load, looped, dmas
        self.start, self.ready = 0, []


class Shared:
    pass



def constant_table():
    parts, rows = {}, {}

    def put(name, a):
        full = np.zeros((P, a.shape[1]), np.float32)
        full[: a.shape[0]] = a
        parts[name] = full
        rows[name] = a.shape[0]

    put("ident", np.eye(P, dtype=np.float32))
    for n in (512, 64):
        put(f"mean{n}", np.full((min(n, P), P), 1.0 / n, np.float32))
    mean = np.zeros((P, P), np.float32)
    mean[:HD, :HD], mean[HD:HD + MLA_ROPE, HD:HD + MLA_ROPE] = 1.0 / HD, 1.0 / MLA_ROPE
    put("mean96", mean)
    put("ones", np.ones((P, P), np.float32))
    put("later", np.tril(np.ones((P, P), np.float32), -1))

    def pairs(n):
        r = np.zeros((n, P), np.float32)
        for i in range(0, n, 2):
            r[i + 1, i] = -1.0
            r[i, i + 1] = 1.0
        return r

    put("turn64", pairs(64))
    turn = np.zeros((P, P), np.float32)
    turn[HD:HD + MLA_ROPE, HD:HD + MLA_ROPE] = pairs(MLA_ROPE)[:, 0:MLA_ROPE]
    put("turn96", turn)
    r = np.zeros((ROPE2, P), np.float32)
    for i in range(ROPE2 // 2):
        r[ROPE2 // 2 + i, i] = -1.0
        r[i, ROPE2 // 2 + i] = 1.0
    put("turn16", r)
    t = np.arange(LAT)
    for n in (64, 32):
        q = n // 4
        inv = (np.float32(10000.0) ** (-np.arange(q, dtype=np.float32) / np.float32(q))).astype(np.float32)
        ang = np.concatenate([(t // GRID_W).astype(np.float32)[:, None] * inv,
                              (t % GRID_W).astype(np.float32)[:, None] * inv], axis=1)
        at, name = (0, "64") if n == 64 else (HD, "96")
        cos, sin = np.ones((P, LAT), np.float32), np.zeros((P, LAT), np.float32)
        cos[at:at + n], sin[at:at + n] = np.repeat(np.cos(ang), 2, axis=1).T, np.repeat(np.sin(ang), 2, axis=1).T
        put(f"cos{name}", cos)
        put(f"sin{name}", sin)
    f = (np.float32(500000.0) ** (-np.arange(0, ROPE2, 2, dtype=np.float32) / np.float32(ROPE2))).astype(np.float32)
    put("freq", np.concatenate([f, f])[:, None])
    q, key = np.arange(P)[:, None], np.arange(LAT)[None, :]
    put("causal", np.concatenate([np.where(key <= q + P * i, 0.0, MASKED) for i in range(2)], 1).astype(np.float32))
    put("strict", np.concatenate([(q + P * i < key) for i in range(2)], 1).astype(np.float32))
    qc, kc = GRID_W - 1 - np.arange(P)[:, None] % GRID_W, np.arange(LAT)[None, :] % GRID_W
    start = np.clip(qc - WIN_W // 2, 0, GRID_W - WIN_W)
    put("window", np.where((kc >= start) & (kc < start + WIN_W), 0.0, MASKED).astype(np.float32))
    put("flip", np.kron(np.eye(P // GRID_W), np.eye(GRID_W)[::-1]).astype(np.float32))
    at, col = {}, 0
    for name, a in parts.items():
        at[name] = (rows[name], col, a.shape[1])
        col += a.shape[1]
    return np.ascontiguousarray(np.concatenate(list(parts.values()), axis=1)), at


def selector():
    return np.repeat(np.eye(4, dtype=np.float32), LAT, axis=1)


def vector_rows():
    rows, at = [], {}

    def put(name, source, n, width=P, layer=None, off=0):
        at[name] = sum(r[2] for r in rows)
        rows.append((source, layer, n, width, off))

    put("c", "c", 8)
    put("c_ctx", "c_ctx", 8)
    for l in (0, 1):
        put(f"mod_b{l}", f"l{l}_mod_b", 72)
        for m in ("ffn1", "mix", "ffn2"):
            put(f"{m}_{l}", f"l{l}_{m}_norm", 8)
    put("q_norm", "l0_mla_q_norm", 3)
    put("kv_norm", "l0_mla_kv_norm", 2)
    put("mla_q", "l0_mla_q_gain", 1, HD + MLA_ROPE)
    put("mla_k", "l0_mla_k_gain", 1, HD + MLA_ROPE)
    put("glu_b", "l0_conv_glu_b", 8)
    put("dw_b", "l0_conv_dw_b", 4)
    put("ln_g", "l0_conv_ln_g", 4)
    put("ln_b", "l0_conv_ln_b", 4)
    put("dw_w", "l0_conv_dw_w", CONV_W * 4)
    for g in ("gqa_q", "gqa_k", "na_q", "na_k"):
        put(g, f"l1_{g}_gain", 1, 64)
    for l in (0, 1):
        for m in ("ffn1", "mix", "ffn2"):
            put(f"{m}_b{l}", f"{m}_norm_2", 8, layer=l)
        put(f"gate_b{l}", "b_gate_2", 32, layer=l)
        put(f"diff{l}", "diff_gain_2", 1, layer=l)
        put(f"fgt{l}", "b_fgt_2", 1, 4, layer=l)
    put("final", "final_norm_2", 8)
    return rows, at



def by_chunk(w):
    return w.rearrange("(k p) n -> p k n", p=P)


def pair_tiles(slot):
    return slot[:, 0:2 * KD * P].rearrange("p (t k c) -> p t k c", t=2, k=KD)


def wide_tile(slot):
    return slot[:, 0:KD * 2 * P].rearrange("p (k c) -> p k c", k=KD)


def tall_tile(slot):
    return slot[:, 0:SLOT].rearrange("p (k c) -> p k c", k=KF)


def cols(start, n):
    return slice(start, start + n) if isinstance(start, int) else bass.ds(start, n)


def weight_plan(w):
    plan = []

    def add(name, n, load, dmas=1, looped=True):
        plan.append(Product(name, n, load, looped, dmas if isinstance(dmas, list) else [dmas] * n))

    def wide(name, mat, n, first=0):
        m = by_chunk(mat)
        add(name, n, lambda slot, i, c: [(wide_tile(slot), m[:, :, cols(i * (RING * 256) + (first + c * 256), 256)])])

    def ffn(name, layer, mat_in, mat_out):
        m, o = by_chunk(mat_in), by_chunk(mat_out)
        kh = KF // 2
        for half, tag in enumerate("ab"):
            at = half * kh
            add(f"{name}_in{tag}{layer}", kh, lambda slot, i, c, at=at: [
                (pair_tiles(slot)[:, t], m[:, :, cols(i * (RING * P) + (t * FF + (at + c) * P), P)]) for t in (0, 1)], 2)
            add(f"{name}_out{tag}{layer}", KD, lambda slot, i, c, at=at: [
                (tall_tile(slot)[:, a:b, :], o[:, at + a:at + b, cols(i * (RING * P) + c * P, P)])
                for a, b in ((0, kh // 2), (kh // 2, kh))], 2)

    def listed(name, mat, units):
        m = by_chunk(mat)
        add(name, len(units), lambda slot, i, c: [(dst(slot), m[:, :, at:at + n]) for dst, at, n in units[c]],
            [len(u) for u in units], looped=False)

    def whole(slot, n=256):
        return wide_tile(slot)[:, :, 0:n]

    def tile(t, n=P):
        return lambda slot: pair_tiles(slot)[:, t, :, 0:n]

    for l in (0, 1):
        wide(f"mod{l}", w[f"l{l}_mod_w"], N_MOD * D // 256)
        ffn("ffn1", l, w[f"l{l}_ffn1_w_in"], w[f"l{l}_ffn1_w_out"])
        if l == 0:
            units = [[(tile(0), 672 + P * c, P), (tile(1), 1184 + P * c, P)] for c in range(4)]
            units += [[(whole, 0, 256)], [(whole, 288, 256)], [(tile(0), 544, 128), (tile(1, 32), 256, 32)]]
            listed("in0", w["l0_w_in"], units)
            uq = by_chunk(w["l0_mla_w_uq"])
            heads = w["l0_mla_w_ukv"].rearrange("(k p) (h e) -> p k h e", p=P, h=HEADS)

            def latents_out(slot, i, c):
                if c == 1:
                    return [(slot[:, 0:2304].rearrange("p (k n) -> p k n", k=3), uq)]
                return [(slot[:, (2 * part + kc) * 512:(2 * part + kc + 1) * 512].rearrange("p (h e) -> p h e", h=HEADS),
                         heads[:, kc, :, part * HD:(part + 1) * HD]) for part in range(2) for kc in range(2)]

            add("heads0", 2, latents_out, [4, 1], looped=False)
        else:
            wide("in1", w["l1_w_in"], 9)
        wide(f"out{l}", w[f"l{l}_w_out"], 4)
        ffn("ffn2", l, w[f"l{l}_ffn2_w_in"], w[f"l{l}_ffn2_w_out"])
    for l in (0, 1):
        ffn("ffn1", f"_b{l}", w["ffn1_w_gu_2"][l], w["ffn1_w_down_2"][l])
        order = list(QK_COLUMNS) + list(V_COLUMNS)
        units = [[(whole, c, 256)] for c in order]
        units += [[(lambda slot: whole(slot, 72), 4356, 72), (lambda slot: wide_tile(slot)[:, :, 72:76], 2304, 4)]]
        listed(f"in_b{l}", w["w_in_2"][l], units)
        gates = w["w_gate_2"][l].rearrange("(k p) (b n) -> p b k n", p=P, b=4)
        br = {n: by_chunk(w[f"w_br_{n}_2"][l]) for n in "abcd"}

        def merge(slot, i, c, gates=gates, br=br):
            n = cols(i * (RING // 2 * P) + c // 2 * P, P)
            two = ((0, "a", 16, 4), (3, "d", 20, 2)) if c % 2 == 0 else ((1, "b", 16, 2), (2, "c", 18, 2))
            out = []
            for t, (gate, name, row, rows) in enumerate(two):
                out.append((tall_tile(slot)[:, t * KD:(t + 1) * KD, :], gates[:, gate, :, n]))
                out.append((tall_tile(slot)[:, row:row + rows, :], br[name][:, :, n]))
            return out

        add(f"merge_b{l}", 16, merge, 4)
        wide(f"out_b{l}", w["w_out_2"][l], 4)
        ffn("ffn2", f"_b{l}", w["ffn2_w_gu_2"][l], w["ffn2_w_down_2"][l])
    start = 0
    raised = [0] * RING
    for spec in plan:
        spec.start = start
        spec.ready = []
        for j in range(spec.n):
            slot = (start + j) % RING
            raised[slot] += 16 * spec.dmas[j]
            spec.ready.append(raised[slot])
        start += spec.n
    return plan


def each_unit(engine, first, last, body, looped=True):
    full = (last - first) // RING if looped else 0
    if full > 1:
        with engine.Fori(0, full) as i:
            for s in range(RING):
                body(i, first + s)
    elif full == 1:
        for s in range(RING):
            body(0, first + s)
    for c in range(first + full * RING, last):
        body(0, c)


def load_weights(k, sp, first, last):
    for spec in k.plan:
        a, b = max(first, spec.start) - spec.start, min(last, spec.start + spec.n) - spec.start
        if a >= b:
            continue

        def unit(i, c, spec=spec):
            slot = (spec.start + c) % RING
            if first > 0:
                sp.wait_ge(k.unit_done, i * RING + (spec.start + c - RING + 1))
            for dst, src in spec.load(k.slots[slot], i, c):
                sp.dma_start(dst, src).then_inc(k.weights_ready[slot], 16)

        each_unit(sp, a, b, unit, spec.looped)


def wait_weights(k, pe, spec, i, c):
    slot = (spec.start + c) % RING
    pe.wait_ge(k.weights_ready[slot], i * (16 * spec.dmas[c]) + spec.ready[c])
    pe.wait_ge(k.banks_free, i * RING + (spec.start + c + 1))
    return slot


def wait_product(k, engine, spec, i, c):
    engine.wait_ge(k.unit_done, i * RING + (spec.start + c + 1))
    return (spec.start + c) % RING


def stream_ahead(k, block, spec):
    total = k.plan[-1].start + k.plan[-1].n

    @block.sync
    def _(sp):
        load_weights(k, sp, spec.start + RING, min(spec.start + spec.n + RING, total))



def halves(tokens):
    return [(0, slice(0, LAT)), (1, slice(LAT, TOK))][: tokens // LAT]


def one(t, h, rows=slice(None), col=slice(None)):
    if isinstance(h, int):
        return t[rows, h, col]
    return t[rows, bass.ds(h, 1), col].rearrange("p o n -> p (o n)")


def column(t, n, rows=slice(None)):
    return t[rows, cols(n, 1)]


def norm_tokens(k, tokens, gain, shift=None, dst=None):
    x, dst = k.x, k.h if dst is None else dst
    squared, mean, root, scaled = (k.tally(n) for n in ("squared", "mean_done", "root_done", "scaled"))
    T = slice(0, tokens)
    with k.nc.Block() as block:
        @block.scalar
        def _(act):
            for c in range(KD):
                k.nc.scalar.activation(k.mix[:, c, T], x[:, c, T], ACT.Square).then_inc(squared.sem, 1)
            act.wait_ge(mean.sem, mean.base + 1)
            k.nc.scalar.activation(k.root[:, T], k.psum[:, 0, T], ACT.Sqrt, bias=k.eps[:, 0:1],
                                   scale=1.0 / D).then_inc(root.sem, 1)
            if shift is not None:
                for c in range(KD):
                    for cond, part in halves(tokens):
                        act.wait_ge(scaled.sem, scaled.base + 2 + c)
                        k.nc.scalar.activation(dst[:, c, part], dst[:, c, part], ACT.Identity,
                                               bias=shift(c, cond), scale=gain(c, cond))

        @block.tensor
        def _(pe):
            for c in range(KD):
                pe.wait_ge(squared.sem, squared.base + c + 1)
                mm = k.nc.tensor.matmul(k.psum[:, 0, T], k.const("ones"), k.mix[:, c, T], start=c == 0, stop=c == KD - 1)
            mm.then_inc(mean.sem, 1)

        @block.vector
        def _(dve):
            dve.wait_ge(root.sem, root.base + 1)
            k.nc.vector.reciprocal(k.rinv[:, T], k.root[:, T]).then_inc(scaled.sem, 1)
            dve.wait_ge(scaled.sem, scaled.base + 1)
            for c in range(KD):
                if shift is None:
                    k.nc.vector.scalar_tensor_tensor(dst[:, c, T], x[:, c, T], gain(c, 0), k.rinv[:, T],
                                                     ALU.mult, ALU.mult).then_inc(scaled.sem, 1)
                else:
                    k.nc.vector.tensor_tensor(dst[:, c, T], x[:, c, T], k.rinv[:, T], ALU.mult).then_inc(scaled.sem, 1)
    for t, n in ((squared, KD), (mean, 1), (root, 1), (scaled, 1 + KD)):
        t.close(n)


def add_product(k, spec, tokens, source, chunks, tile_of, tiles, gate):
    T = slice(0, tokens)
    with k.nc.Block() as block:
        stream_ahead(k, block, spec)

        @block.tensor
        def _(pe):
            def unit(i, c):
                slot = wait_weights(k, pe, spec, i, c)
                for t in range(tiles):
                    for kc in range(chunks):
                        mm = k.nc.tensor.matmul(k.psum[:, 2 * slot + t, T], tile_of(k.slots[slot], kc, t),
                                                source[:, kc, T], start=kc == 0, stop=kc == chunks - 1)
                mm.then_inc(k.unit_done, 1)
            each_unit(pe, 0, spec.n, unit)

        @block.vector
        def _(dve):
            def unit(i, c):
                slot = wait_product(k, dve, spec, i, c)
                for t in range(tiles):
                    chunk = i * (RING * tiles) + (c * tiles + t)
                    for cond, part in (halves(tokens) if callable(gate) else [(0, T)]):
                        row = one(k.x, chunk, col=part)
                        last = k.nc.vector.scalar_tensor_tensor(row, k.psum[:, 2 * slot + t, part],
                                                                gate(chunk, cond) if callable(gate) else gate, row,
                                                                ALU.mult, ALU.add)
                last.then_inc(k.banks_free, 1)
            each_unit(dve, 0, spec.n, unit)


def wide_lhs(slot, kc, t):
    return wide_tile(slot)[:, kc, t * P:(t + 1) * P]


def norm_heads(k, src, rows, groups, n, mean, gain, scale=1.0, eps=None):
    squared, mean_done, root, inv, normed = (k.tally(t) for t in ("squared", "mean_done", "root_done", "inverse_done", "normed"))
    R, N = slice(0, rows), slice(0, n)
    eps = k.eps if eps is None else eps
    with k.nc.Block() as block:
        @block.scalar
        def _(act):
            act.sem_inc(inv.sem, 2)
            with act.Fori(0, groups // 2) as i:
                for u in range(2):
                    k.nc.scalar.activation(k.square[R, u, N], one(src, i * 2 + u, R, N), ACT.Square).then_inc(squared.sem, 1)
                for u in range(2):
                    act.wait_ge(mean_done.sem, i * 2 + (mean_done.base + u + 1))
                    act.wait_ge(inv.sem, i * 2 + (inv.base + u + 1))
                    k.nc.scalar.activation(k.roots[R, u, N], k.psum[R, u, N], ACT.Sqrt, bias=eps[R, 0:1], scale=scale)\
                        .then_inc(root.sem, 1)

        @block.tensor
        def _(pe):
            with pe.Fori(0, groups // 2) as i:
                for u in range(2):
                    pe.wait_ge(squared.sem, i * 2 + (squared.base + u + 1))
                    k.nc.tensor.matmul(k.psum[:, u, N], mean, k.square[R, u, N], start=True, stop=True)\
                        .then_inc(mean_done.sem, 1)

        @block.vector
        def _(dve):
            with dve.Fori(0, groups // 2) as i:
                for u in range(2):
                    dve.wait_ge(root.sem, i * 2 + (root.base + u + 1))
                    k.nc.vector.reciprocal(k.rinvs[R, u, N], k.roots[R, u, N]).then_inc(inv.sem, 1)
                    dve.wait_ge(inv.sem, i * 2 + (inv.base + 2 + u + 1))
                    row = one(src, i * 2 + u, R, N)
                    k.nc.vector.scalar_tensor_tensor(row, row, gain, k.rinvs[R, u, N], ALU.mult, ALU.mult)\
                        .then_inc(normed.sem, 1)
    for t, n in ((squared, groups), (mean_done, groups), (root, groups), (inv, groups + 2), (normed, groups)):
        t.close(n)


def rotate_heads(k, src, rows, groups, turn, cos, sin):
    turned, by_cos, by_sin, rotated = (k.tally(t) for t in ("turned", "by_cos", "by_sin", "rotated"))
    R, N = slice(0, rows), slice(0, LAT)
    steps = (groups + 1) // 2

    def operands(i, u, n):
        rows_ = src[R, cols(i * 2, n), N]
        bank, product = (t[R, u, 0:n * LAT].rearrange("p (g t) -> p g t", g=n) for t in (k.psum, k.square))
        return rows_, bank, product, *(t.unsqueeze(1).broadcast_to([rows, n, LAT]) for t in (cos, sin))

    def each_step(engine, body):
        full = groups // 2
        if full > 1:
            with engine.Fori(0, full // 2) as i:
                for u in range(2):
                    body(i * 2 + u, u, 2)
        if full % 2:
            body(full - 1, 0, 2)
        if groups % 2:
            body(full, full % 2, 1)

    with k.nc.Block() as block:
        @block.tensor
        def _(pe):
            pe.sem_inc(by_sin.sem, 2)

            def step(i, u, n):
                pe.wait_ge(by_sin.sem, i + (by_sin.base + 1))
                for g in range(n):
                    mm = k.nc.tensor.matmul(k.psum[:, u, g * LAT:(g + 1) * LAT], turn, one(src, i * 2 + g, R, N),
                                            start=True, stop=True)
                mm.then_inc(turned.sem, 1)
            each_step(pe, step)

        @block.gpsimd
        def _(pool):
            def step(i, u, n):
                x, _, _, c, _ = operands(i, u, n)
                pool.wait_ge(turned.sem, i + (turned.base + 1))
                k.nc.gpsimd.tensor_tensor(x, x, c, ALU.mult).then_inc(by_cos.sem, 1)
            each_step(pool, step)

        @block.vector
        def _(dve):
            def step(i, u, n):
                x, bank, product, _, s = operands(i, u, n)
                dve.wait_ge(turned.sem, i + (turned.base + 1))
                k.nc.vector.tensor_tensor(product, bank, s, ALU.mult).then_inc(by_sin.sem, 1)
                dve.wait_ge(by_sin.sem, i + (by_sin.base + 3))
                dve.wait_ge(by_cos.sem, i + (by_cos.base + 1))
                k.nc.vector.tensor_tensor(x, x, product, ALU.add).then_inc(rotated.sem, 1)
            each_step(dve, step)
    for t, n in ((turned, steps), (by_cos, steps), (by_sin, steps + 2), (rotated, steps)):
        t.close(n)


def attention(k, pairs, key_tiles, staging, score, value, width, dst, difference=None):
    nc, J = k.nc, 4
    keys = key_tiles * P
    steps = 1 if difference is None else 2
    t = {n: k.tally(n) for n in (
        "staged", "scored", "maxed", "exp_done", "probs_turned", "even_copied", "odd_copied", "weighted",
        "sums_inverted", "out_normed", "out_turned", "out_placed")}
    S = [k.psum[:, j, 0:keys] for j in range(J)]
    PT = [k.psum[:, 4 + u, 0:keys] for u in range(2)]
    O = [k.psum[:, 6, j * width:(j + 1) * width] for j in range(J)]
    OT = k.psum[:, 7, 0:2 * P]
    jobs = [(j, j // 2, j % 2) for j in range(J)]
    prob = [k.prob(j, keys) for j in range(J)]
    prob_t = [k.prob_t(u, keys) for u in range(2)]
    with nc.Block() as block:
        @block.gpsimd
        def _(pool):
            with pool.Fori(0, pairs) as b:
                copies = staging(b)
                for n, (to, of) in enumerate(copies):
                    last = nc.gpsimd.tensor_copy(to, of)
                last.then_inc(t["staged"].sem, 1)
                pool.wait_ge(t["scored"].sem, b * J + (t["scored"].base + J))

        @block.tensor
        def _(pe):
            pe.sem_inc(t["out_placed"].sem, 1)

            def weigh(b, j, hh):
                copied = t["even_copied"] if j % 2 == 0 else t["odd_copied"]
                pe.wait_ge(copied.sem, b * (J // 2) + (copied.base + j // 2 + 1))
                for kt in range(key_tiles):
                    mm = nc.tensor.matmul(O[j], prob_t[j % 2][:, kt * P:(kt + 1) * P], value(b, hh, kt),
                                          start=kt == 0, stop=kt == key_tiles - 1)
                mm.then_inc(t["weighted"].sem, 1)

            def form_logits(b, some):
                for j, hh, qt in some:
                    score(S[j], b, hh, qt).then_inc(t["scored"].sem, 1)

            def round_of(b, more):
                for j, hh, qt in jobs:
                    pe.wait_ge(t["exp_done"].sem, b * J + (t["exp_done"].base + j + 1))
                    for kt in range(key_tiles):
                        mm = nc.tensor.transpose(PT[j % 2][:, kt * P:(kt + 1) * P], prob[j][:, kt * P:(kt + 1) * P],
                                                 k.const("ident"))
                    mm.then_inc(t["probs_turned"].sem, 1)
                    if j >= 1:
                        weigh(b, j - 1, (j - 1) // 2)
                weigh(b, J - 1, 1)
                if more:
                    pe.wait_ge(t["staged"].sem, b + (t["staged"].base + 2))
                    form_logits(b + 1, jobs[:2])
                pe.wait_ge(t["out_normed"].sem, b * J + (t["out_normed"].base + J))
                pe.wait_ge(t["out_placed"].sem, b + (t["out_placed"].base + 1))
                for qt in range(2):
                    mm = nc.tensor.transpose(OT[:, qt * P:(qt + 1) * P], k.out_rows[:, qt, :], k.const("ident"))
                mm.then_inc(t["out_turned"].sem, 1)
                if more:
                    form_logits(b + 1, jobs[2:])

            pe.wait_ge(t["staged"].sem, t["staged"].base + 1)
            form_logits(0, jobs)
            if pairs > 2:
                with pe.Fori(0, pairs - 1) as b:
                    round_of(b, True)
            else:
                round_of(0, True)
            round_of(pairs - 1, False)

        @block.vector
        def _(dve):
            dve.sem_inc(t["out_turned"].sem, 1)
            with dve.Fori(0, pairs) as b:
                for j, hh, qt in jobs:
                    dve.wait_ge(t["scored"].sem, b * J + (t["scored"].base + j + 1))
                    nc.vector.tensor_reduce(k.negmax[:, j:j + 1], S[j], AX.X, ALU.max, negate=True).then_inc(t["maxed"].sem, 1)
                for j in (0, 2):
                    dve.wait_ge(t["probs_turned"].sem, b * J + (t["probs_turned"].base + j + 1))
                    if j == 2:
                        dve.wait_ge(t["weighted"].sem, b * J + (t["weighted"].base + 1))
                    nc.vector.tensor_copy(prob_t[0], PT[0]).then_inc(t["even_copied"].sem, 1)
                dve.wait_ge(t["exp_done"].sem, b * J + (t["exp_done"].base + J))
                inverse = nc.vector.reciprocal(k.inverse[:, 0:J], k.rowsum[:, 0:J])
                inverse.then_inc(t["sums_inverted"].sem, 1)
                dve.wait_ge(t["sums_inverted"].sem, b * steps + (t["sums_inverted"].base + 1))
                if difference is not None:
                    nc.vector.tensor_scalar(k.inverse[:, J:J + 2], k.inverse[:, 2:4], difference, None, ALU.mult)\
                        .then_inc(t["sums_inverted"].sem, 1)
                    dve.wait_ge(t["sums_inverted"].sem, b * steps + (t["sums_inverted"].base + 2))
                dve.wait_ge(t["out_turned"].sem, b + (t["out_turned"].base + 1))
                dve.wait_ge(t["weighted"].sem, b * J + (t["weighted"].base + J))
                for j, hh, qt in jobs:
                    if difference is None:
                        nc.vector.tensor_scalar(k.out_rows[:, qt, hh * width:(hh + 1) * width], O[j],
                                                k.inverse[:, j:j + 1], None, ALU.mult).then_inc(t["out_normed"].sem, 1)
                    elif hh == 0:
                        nc.vector.tensor_scalar(k.out_rows[:, qt, :], O[j], k.inverse[:, j:j + 1], None, ALU.mult)\
                            .then_inc(t["out_normed"].sem, 1)
                    else:
                        dve.wait_ge(t["out_normed"].sem, b * J + (t["out_normed"].base + j - 1))
                        nc.vector.scalar_tensor_tensor(k.out_rows[:, qt, :], O[j], k.inverse[:, J + qt:J + qt + 1],
                                                       k.out_rows[:, qt, :], ALU.mult, ALU.add).then_inc(t["out_normed"].sem, 1)

        @block.scalar
        def _(act):
            with act.Fori(0, pairs) as b:
                for j, hh, qt in jobs:
                    act.wait_ge(t["maxed"].sem, b * J + (t["maxed"].base + j + 1))
                    nc.scalar.activation(prob[j], S[j], ACT.Exp, bias=k.negmax[:, j:j + 1],
                                         accum_out=k.rowsum[:, j:j + 1]).then_inc(t["exp_done"].sem, 1)
                for j in (1, 3):
                    act.wait_ge(t["probs_turned"].sem, b * J + (t["probs_turned"].base + j + 1))
                    if j == 3:
                        act.wait_ge(t["weighted"].sem, b * J + (t["weighted"].base + 2))
                    nc.scalar.activation(prob_t[1], PT[1], ACT.Copy).then_inc(t["odd_copied"].sem, 1)
                act.wait_ge(t["out_turned"].sem, b + (t["out_turned"].base + 2))
                nc.scalar.activation(dst(b), OT, ACT.Copy).then_inc(t["out_placed"].sem, 1)
    for name, n in dict(staged=1, scored=J, maxed=J, exp_done=J, probs_turned=J, even_copied=2, odd_copied=2, weighted=J,
                        sums_inverted=steps, out_normed=J, out_turned=1, out_placed=1).items():
        t[name].close(n * pairs)
    t["out_turned"].close(1)
    t["out_placed"].close(1)



KH = KF // 2
WIDE = 2 * KD * P
PASSES = ((0, 0), (0, 1), (1, 0))


def ffn_buffers(k, tokens, depth):
    stack = ExitStack()
    k.scope += 1

    def sb(name, shape):
        return stack.enter_context(k.nc.sbuf_tensor(f"{name}_{k.scope}", shape, F32R))

    k.normed = [sb(f"normed{n}", [P, KD, tokens]) for n in range(2)]
    k.hidden = [sb(f"hidden{n}", [P, KH, tokens]) for n in range(2)]
    k.parts = [[sb(f"weights_part{n}_{d}", [P, WIDE]) for n in range(2)] for d in range(depth)]
    k.rows = [k.roots[:, 1, 0:tokens], k.rinvs[:, 1, 0:tokens]]
    return stack


def half_ffn(k, tokens, name, layer, gain, shift, gate):
    nc, T = k.nc, slice(0, tokens)
    depth = 2 if tokens == TOK else 4
    ahead = depth - 1
    specs = [k.spec(f"{name}_{part}{half}{layer}") for half in "ab" for part in ("in", "out")]
    first, total = specs[0].start, sum(s.n for s in specs)
    per_unit = 16 * specs[0].dmas[0]
    t = {n: k.tally("ffn_" + n) for n in ("squared", "summed", "root_done", "inverse_done", "scaled", "shifted", "normed",
                                          "high_done", "split_done", "silu_done", "gated", "hidden_high")}
    parts_of_tokens = halves(tokens) if shift is not None else [(0, T)]

    def at(spec, c):
        return spec.start - first + c

    def split_high(act, i, q):
        if q >= total:
            return
        slot, part = (first + q) % RING, (first + q) % depth
        act.wait_ge(k.weights_ready[slot], i * per_unit + (specs[0].ready[q % RING] + q // RING * per_unit))
        act.wait_ge(k.unit_done, i * RING + (first + q - depth + 1))
        nc.scalar.activation(k.parts[part][0][:, :], k.slots[slot][:, 0:WIDE], ACT.Copy).then_inc(t["high_done"].sem, 1)

    def split_low(dve, i, q):
        if q >= total:
            return
        slot, part = (first + q) % RING, (first + q) % depth
        dve.wait_ge(t["high_done"].sem, i * RING + (t["high_done"].base + q + 1))
        nc.vector.tensor_tensor(k.parts[part][1][:, :], k.slots[slot][:, 0:WIDE], k.parts[part][0][:, :].bitcast(F32),
                                ALU.subtract).then_inc(t["split_done"].sem, 1)

    with ffn_buffers(k, tokens, depth), nc.Block() as block:
        total_units = k.plan[-1].start + k.plan[-1].n

        @block.sync
        def _(sp):
            load_weights(k, sp, first + RING, min(first + total + RING, total_units))

        @block.scalar
        def _(act):
            for c in range(KD):
                if c >= 2:
                    act.wait_ge(t["summed"].sem, t["summed"].base + c - 1)
                nc.scalar.activation(k.square[:, c % 2, T], k.x[:, c, T], ACT.Square).then_inc(t["squared"].sem, 1)
            act.wait_ge(t["summed"].sem, t["summed"].base + KD)
            nc.scalar.activation(k.root[:, T], k.psum[:, 0, T], ACT.Sqrt, bias=k.eps[:, 0:1], scale=1.0 / D)\
                .then_inc(t["root_done"].sem, 1)
            split_high(act, 0, 0)
            for c in range(KD):
                act.wait_ge(t["scaled"].sem, t["scaled"].base + c + 1)
                for cond, part in parts_of_tokens:
                    if shift is None:
                        last = nc.scalar.activation(k.normed[0][:, c, part], k.rows[c % 2][:, part], ACT.Copy)
                    else:
                        last = nc.scalar.activation(k.normed[0][:, c, part], k.rows[c % 2][:, part], ACT.Identity,
                                                    bias=shift(c, cond))
                last.then_inc(t["shifted"].sem, 1)
            for q in range(1, ahead):
                split_high(act, 0, q)
            for s, spec in enumerate(specs):
                def unit_in(i, c, spec=spec, half=s // 2):
                    split_high(act, i, at(spec, c) + ahead)
                    slot = wait_product(k, act, spec, i, c)
                    row, n = k.rows[(half * KH + c) % 2], half * KH + c + 1
                    act.wait_ge(k.banks_free, i * RING + (spec.start + c + RING - 1))
                    nc.scalar.activation(row[:, T], k.psum[:, 2 * slot, T], ACT.Silu).then_inc(t["silu_done"].sem, 1)
                    act.wait_ge(t["gated"].sem, i * RING + (t["gated"].base + n))
                    nc.scalar.activation(one(k.hidden[0], i * RING + c, col=T), row[:, T], ACT.Copy)\
                        .then_inc(t["hidden_high"].sem, 1)

                def unit_out(i, c, spec=spec):
                    split_high(act, i, at(spec, c) + ahead)

                each_unit(act, 0, spec.n, unit_in if s % 2 == 0 else unit_out, s < len(specs) - 1)

        @block.tensor
        def _(pe):
            for c in range(KD):
                pe.wait_ge(t["squared"].sem, t["squared"].base + c + 1)
                nc.tensor.matmul(k.psum[:, 0, T], k.const("ones"), k.square[:, c % 2, T], start=c == 0, stop=c == KD - 1)\
                    .then_inc(t["summed"].sem, 1)

            def product(to, weights, tokens_parts, kc, chunks):
                for n, (a, b) in enumerate(PASSES):
                    mm = nc.tensor.matmul(to, weights[a], tokens_parts[b][:, kc, T], start=kc == 0 and n == 0,
                                          stop=kc == chunks - 1 and n == len(PASSES) - 1)
                return mm

            def wait_unit(spec, i, c):
                pe.wait_ge(t["split_done"].sem, i * RING + (t["split_done"].base + at(spec, c) + 1))
                pe.wait_ge(k.banks_free, i * RING + (spec.start + c + 1))
                return (spec.start + c) % RING, k.parts[(spec.start + c) % depth]

            for s, spec in enumerate(specs):
                def unit_in(i, c, spec=spec, first_unit=False):
                    slot, parts = wait_unit(spec, i, c)
                    for tile in range(2):
                        for kc in range(KD):
                            if first_unit and tile == 0:
                                pe.wait_ge(t["normed"].sem, t["normed"].base + kc + 1)
                            mm = product(k.psum[:, 2 * slot + tile, T], [pair_tiles(w)[:, tile, kc] for w in parts],
                                         k.normed, kc, KD)
                    mm.then_inc(k.unit_done, 1)

                def unit_out(i, c, spec=spec):
                    slot, parts = wait_unit(spec, i, c)
                    for kc in range(KH):
                        mm = product(k.psum[:, 2 * slot, T], [w[:, kc * P:(kc + 1) * P] for w in parts], k.hidden, kc, KH)
                    mm.then_inc(k.unit_done, 1)

                if s == 0:
                    unit_in(0, 0, first_unit=True)
                    each_unit(pe, 1, 3, unit_in)
                    each_unit(pe, 3, spec.n, unit_in)
                elif s % 2 == 0:
                    each_unit(pe, 0, spec.n, unit_in)
                else:
                    pe.wait_ge(k.banks_free, spec.start + RING)
                    each_unit(pe, 0, spec.n, unit_out, s < len(specs) - 1)

        @block.vector
        def _(dve):
            dve.wait_ge(t["root_done"].sem, t["root_done"].base + 1)
            nc.vector.reciprocal(k.rinv[:, T], k.root[:, T]).then_inc(t["inverse_done"].sem, 1)
            split_low(dve, 0, 0)
            dve.wait_ge(t["inverse_done"].sem, t["inverse_done"].base + 1)

            def scale(c):
                if c >= 2:
                    dve.wait_ge(t["normed"].sem, t["normed"].base + c - 1)
                for cond, part in parts_of_tokens:
                    last = nc.vector.scalar_tensor_tensor(k.rows[c % 2][:, part], k.x[:, c, part], gain(c, cond),
                                                          k.rinv[:, part], ALU.mult, ALU.mult)
                last.then_inc(t["scaled"].sem, 1)

            scale(0)
            for c in range(KD):
                if c + 1 < KD:
                    scale(c + 1)
                dve.wait_ge(t["shifted"].sem, t["shifted"].base + c + 1)
                for cond, part in parts_of_tokens:
                    row, high = k.rows[c % 2][:, part], k.normed[0][:, c, part].bitcast(F32)
                    if shift is None:
                        last = nc.vector.tensor_tensor(k.normed[1][:, c, part], row, high, ALU.subtract)
                    else:
                        last = nc.vector.scalar_tensor_tensor(k.normed[1][:, c, part], row, shift(c, cond), high,
                                                              ALU.add, ALU.subtract)
                last.then_inc(t["normed"].sem, 1)
            for q in range(1, ahead):
                split_low(dve, 0, q)
            for s, spec in enumerate(specs):
                def unit_in(i, c, spec=spec, half=s // 2):
                    split_low(dve, i, at(spec, c) + ahead)
                    slot = wait_product(k, dve, spec, i, c)
                    row, n = k.rows[(half * KH + c) % 2][:, T], half * KH + c + 1
                    dve.wait_ge(t["silu_done"].sem, i * RING + (t["silu_done"].base + n))
                    nc.vector.tensor_tensor(row, row, k.psum[:, 2 * slot + 1, T], ALU.mult).then_inc(t["gated"].sem, 1)
                    dve.wait_ge(t["hidden_high"].sem, i * RING + (t["hidden_high"].base + n))
                    nc.vector.tensor_tensor(one(k.hidden[1], i * RING + c, col=T), row,
                                            one(k.hidden[0], i * RING + c, col=T).bitcast(F32), ALU.subtract)\
                        .then_inc(k.banks_free, 1)

                def unit_out(i, c, spec=spec):
                    split_low(dve, i, at(spec, c) + ahead)
                    slot = wait_product(k, dve, spec, i, c)
                    chunk = i * RING + c
                    for cond, part in (halves(tokens) if callable(gate) else [(0, T)]):
                        row = one(k.x, chunk, col=part)
                        last = nc.vector.scalar_tensor_tensor(row, k.psum[:, 2 * slot, part],
                                                              gate(chunk, cond) if callable(gate) else gate, row,
                                                              ALU.mult, ALU.add)
                    last.then_inc(k.banks_free, 1)

                each_unit(dve, 0, spec.n, unit_in if s % 2 == 0 else unit_out, s < len(specs) - 1)
    for name, n in dict(squared=KD, summed=KD, root_done=1, inverse_done=1, scaled=KD, shifted=KD, normed=KD,
                        high_done=total, split_done=total, silu_done=KF, gated=KF, hidden_high=KF).items():
        t[name].close(n)



def opening(k, w):
    nc = k.nc
    t = {n: k.tally(n) for n in ("cleared", "consts_landed", "tokens_landed", "vectors_landed",
                                                   "tokens_turned", "tokens_placed", "vectors_turned", "vectors_placed")}
    tokens = k.arena[:, 0:4 * D].rearrange("p (t n) -> p t n", t=4)
    tiles = (k.n_rows + P - 1) // P
    rows = k.arena[:, 4 * D:4 * D + tiles * P].rearrange("p (t n) -> p t n", t=tiles)
    loads = []
    for name, (source, layer, n, width, off) in zip(k.vec_at, k.vec_rows):
        src = w[source] if layer is None else w[source][layer:layer + 1]
        if len(src.shape) == 1:
            src = src.unsqueeze(0)
        flat = src.rearrange("a b -> (a b)")
        flat = flat[off:off + n * width].rearrange("(r c) -> r c", c=width)
        r, done = k.vec_at[name], 0
        while done < n:
            m = min(n - done, P - (r + done) % P)
            at = (r + done) % P
            loads.append((rows[at:at + m, (r + done) // P, 0:width], flat[done:done + m, :]))
            done += m
    lams = [(k.lam[:, l, v, :], w[f"lam_{n}_2"][l:l + 1, :].partition_broadcast(P))
            for l in (0, 1) for v, n in enumerate(("q1", "k1", "q2", "k2"))]
    with nc.Block() as block:
        @block.vector
        def _(dve):
            dve.sem_inc(k.banks_free, RING)
            nc.vector.memset(rows, 0.0).then_inc(t["cleared"].sem, 1)
            nc.vector.memset(k.eps[:, :], EPS).then_inc(t["cleared"].sem, 1)
            nc.vector.memset(k.eps5[:, :], 1e-5).then_inc(t["cleared"].sem, 1)
            nc.vector.memset(k.half_pi[:, :], float(np.pi / 2)).then_inc(t["cleared"].sem, 1)
            for c in range(KD):
                dve.wait_ge(t["tokens_turned"].sem, c + 1)
                nc.vector.tensor_copy(k.x[:, c, :], k.psum[:, c, :]).then_inc(t["tokens_placed"].sem, 1)
            dve.wait_ge(t["vectors_turned"].sem, 1)
            nc.vector.tensor_copy(k.vec[:, 0:tiles * P], k.psum[:, 0, 0:tiles * P]).then_inc(t["vectors_placed"].sem, 1)

        @block.sync
        def _(sp):
            sp.dma_start(tokens[:, 0:2, :], w["x"][0].rearrange("(t p) n -> p t n", p=P)).then_inc(t["tokens_landed"].sem, 16)
            sp.dma_start(tokens[:, 2:4, :], w["ctx"][0].rearrange("(t p) n -> p t n", p=P)).then_inc(t["tokens_landed"].sem, 16)
            sp.dma_start(k.consts[:, :], w["constants"]).then_inc(t["consts_landed"].sem, 16)
            load_weights(k, sp, 0, RING)

        @block.scalar
        def _(act):
            act.wait_ge(t["cleared"].sem, 1)
            for to, of in loads:
                act.dma_start(to, of).then_inc(t["vectors_landed"].sem, 16)
            for to, of in lams:
                act.dma_start(to, of).then_inc(t["vectors_landed"].sem, 16)
            act.dma_start(k.positions[:, :], w["positions_2"].unsqueeze(0).partition_broadcast(ROPE2))\
                .then_inc(t["vectors_landed"].sem, 16)
            act.wait_ge(t["vectors_placed"].sem, 1)
            for cond, name in enumerate(("c", "c_ctx")):
                at = k.vec_at[name]
                last = nc.scalar.activation(k.cond[:, :, cond], k.vec[:, at:at + KD], ACT.Silu)

        @block.tensor
        def _(pe):
            pe.wait_ge(t["consts_landed"].sem, 16)
            pe.wait_ge(t["tokens_landed"].sem, 32)
            for c in range(KD):
                for tt in range(4):
                    mm = nc.tensor.transpose(k.psum[:, c, tt * P:(tt + 1) * P], tokens[:, tt, c * P:(c + 1) * P],
                                             k.const("ident"))
                mm.then_inc(t["tokens_turned"].sem, 1)
            pe.wait_ge(t["vectors_landed"].sem, 16 * (len(loads) + len(lams) + 1))
            pe.wait_ge(t["tokens_placed"].sem, 1)
            for tt in range(tiles):
                mm = nc.tensor.transpose(k.psum[:, 0, tt * P:(tt + 1) * P], rows[:, tt, :], k.const("ident"))
            mm.then_inc(t["vectors_turned"].sem, 1)
    for name, n in dict(cleared=4, tokens_turned=KD, tokens_placed=KD, vectors_turned=1, vectors_placed=1).items():
        t[name].close(n)


def conditioning(k, l):
    nc, spec = k.nc, k.spec(f"mod{l}")
    derived = k.tally("derived")
    bias = k.vec_at[f"mod_b{l}"]
    copied, turned = k.tally("mod_copied"), k.tally("mod_turned")
    rows = [k.square[0:2, 0, n * 256:(n + 1) * 256] for n in range(2)] + [k.roots[0:2, 0, n * 256:(n + 1) * 256] for n in range(2)]
    with nc.Block() as block:
        stream_ahead(k, block, spec)

        @block.tensor
        def _(pe):
            def turn(i, c):
                slot = (spec.start + c) % RING
                pe.wait_ge(copied.sem, i * RING + (copied.base + c + 1))
                for t in range(2):
                    mm = nc.tensor.matmul(k.psum[:, 2 * slot + 1, 2 * t:2 * t + 2], rows[slot][:, t * P:(t + 1) * P],
                                             k.const("ident")[0:2, 0:2], start=True, stop=True)
                mm.then_inc(turned.sem, 1)

            def unit(i, c):
                slot = wait_weights(k, pe, spec, i, c)
                for kc in range(KD):
                    mm = nc.tensor.matmul(k.psum[0:2, 2 * slot, 0:256], k.cond[:, kc, :], wide_tile(k.slots[slot])[:, kc, :],
                                          start=kc == 0, stop=kc == KD - 1)
                mm.then_inc(k.unit_done, 1)
                if c > 0:
                    turn(i, c - 1)

            unit(0, 0)
            each_unit(pe, 1, spec.n, unit)
            turn(0, spec.n - 1)

        @block.vector
        def _(dve):
            def place(i, c):
                slot = (spec.start + c) % RING
                dve.wait_ge(turned.sem, i * RING + (turned.base + c + 1))
                for t in range(2):
                    chunk = i * (RING * 2) + (c * 2 + t)
                    last = nc.vector.tensor_scalar(one(k.mod, chunk), k.psum[:, 2 * slot + 1, 2 * t:2 * t + 2],
                                                   column(k.vec, chunk + bias), None, ALU.add)
                last.then_inc(k.banks_free, 1)

            def unit(i, c):
                slot = wait_product(k, dve, spec, i, c)
                nc.vector.tensor_copy(rows[slot], k.psum[0:2, 2 * slot, 0:256]).then_inc(copied.sem, 1)
                if c > 0:
                    place(i, c - 1)

            unit(0, 0)
            each_unit(dve, 1, spec.n, unit)
            place(0, spec.n - 1)
            dve.wait_ge(k.banks_free, spec.start + spec.n + RING)
            for m, name in enumerate(("ffn1", "mix", "ffn2")):
                gain = k.vec_at[f"{name}_{l}"]
                for cond in range(2):
                    nc.vector.scalar_tensor_tensor(k.gain[:, m, :, cond], k.mod[:, (3 * m + 1) * KD:(3 * m + 2) * KD, cond],
                                                   1.0, k.vec[:, gain:gain + KD], ALU.add, ALU.mult).then_inc(derived.sem, 1)
            for m, at in ((0, 2), (1, 8)):
                nc.vector.tensor_scalar(k.gate[:, m], k.mod[:, at * KD:(at + 1) * KD, :], 0.5, None, ALU.mult)\
                    .then_inc(derived.sem, 1)
    derived.close(8), copied.close(spec.n), turned.close(spec.n)


def modulated(k, m):
    return (lambda c, cond: k.gain[:, m, c, cond:cond + 1],
            lambda c, cond: k.mod[:, 3 * m * KD + c, cond:cond + 1])


def half_gate(k, m):
    def gate(chunk, cond):
        if isinstance(chunk, int):
            return k.gate[:, m, chunk, cond:cond + 1]
        return k.gate[:, m, bass.ds(chunk, 1), cond]
    return gate


def mix_gate(k):
    def gate(chunk, cond):
        if isinstance(chunk, int):
            return k.mod[:, 5 * KD + chunk, cond:cond + 1]
        return k.mod[:, bass.ds(chunk + 5 * KD, 1), cond]
    return gate


def ending(k, out):
    nc = k.nc
    turned, placed, stored = (k.tally(n) for n in ("tokens_turned", "tokens_placed", "stored"))
    rows = k.arena[:, 0:2 * D].rearrange("p (t n) -> p t n", t=2)
    with nc.Block() as block:
        @block.tensor
        def _(pe):
            for tt in range(2):
                for c in range(KD):
                    mm = nc.tensor.transpose(k.psum[:, 2 * tt + c // 4, (c % 4) * P:(c % 4 + 1) * P],
                                             k.h[:, c, tt * P:(tt + 1) * P], k.const("ident"))
                    if c % 4 == 3:
                        mm.then_inc(turned.sem, 1)

        @block.vector
        def _(dve):
            for n in range(4):
                dve.wait_ge(turned.sem, turned.base + n + 1)
                nc.vector.tensor_copy(rows[:, n // 2, (n % 2) * BANK:(n % 2 + 1) * BANK], k.psum[:, n, :])\
                    .then_inc(placed.sem, 1)

        @block.sync
        def _(sp):
            for n in range(4):
                sp.wait_ge(placed.sem, placed.base + n + 1)
                sp.dma_start(out[0][(n // 2) * P:(n // 2 + 1) * P, (n % 2) * BANK:(n % 2 + 1) * BANK],
                             rows[:, n // 2, (n % 2) * BANK:(n % 2 + 1) * BANK]).then_inc(stored.sem, 16)
            sp.wait_ge(stored.sem, 64)



def even_mixer(k):
    nc = k.nc
    qn, kn = (k.arena[:, n * HEADS * TOK:(n + 1) * HEADS * TOK].rearrange("p (h t) -> p h t", h=HEADS) for n in range(2))
    width = HD + MLA_ROPE
    ypad = k.side[:, 0:4 * 2 * (LAT + 2 * PAD)].rearrange("p (c s t) -> p c s t", c=4, s=2)

    spec = k.spec("in0")
    first, cleared, taps = k.tally("first_bank_out"), k.tally("cleared"), k.tally("tap_done")
    sums = [k.side[:, at:at + TOK] for at in (4 * 2 * (LAT + 2 * PAD), 4 * 2 * (LAT + 2 * PAD) + TOK)]
    sums += [k.mix[:, c, :] for c in (6, 7)]
    n_conv = 4
    with nc.Block() as block:
        stream_ahead(k, block, spec)

        @block.gpsimd
        def _(pool):
            nc.gpsimd.memset(ypad[:, :, :, 0:PAD], 0.0).then_inc(cleared.sem, 1)
            nc.gpsimd.memset(ypad[:, :, :, PAD + LAT:], 0.0).then_inc(cleared.sem, 1)
            pool.wait_ge(cleared.sem, cleared.base + 2)
            nc.gpsimd.memset(k.arena[width:P, 0:2 * HEADS * TOK], 0.0)

        @block.tensor
        def _(pe):
            for c in range(spec.n):
                slot = wait_weights(k, pe, spec, 0, c)
                for t in range(2):
                    m = MLA_ROPE if (c, t) == (n_conv + 2, 1) else P
                    for kc in range(KD):
                        lhs = wide_lhs(k.slots[slot], kc, t) if c in (n_conv, n_conv + 1) else \
                            pair_tiles(k.slots[slot])[:, t, kc, 0:m]
                        mm = nc.tensor.matmul(k.psum[0:m, 2 * slot + t, :], lhs, k.h[:, kc, :], start=kc == 0, stop=kc == KD - 1)
                mm.then_inc(k.unit_done, 1)

        @block.scalar
        def _(act):
            for c in range(spec.n):
                slot = wait_product(k, act, spec, 0, c)
                if c >= n_conv:
                    last = nc.scalar.activation(k.mix[:, 2 * (c - n_conv), :], k.psum[:, 2 * slot, :], ACT.Copy)
                else:
                    if c >= 2:
                        act.wait_ge(k.banks_free, RING + spec.start + c - 1)
                    last = nc.scalar.activation(k.square[:, c % 2, :], k.psum[:, 2 * slot + 1, :], ACT.Sigmoid,
                                                bias=column(k.vec, k.vec_at["glu_b"] + 4 + c))
                last.then_inc(first.sem, 1)

        @block.vector
        def _(dve):
            dve.wait_ge(cleared.sem, cleared.base + 2)
            for c in range(spec.n):
                slot = wait_product(k, dve, spec, 0, c)
                dve.wait_ge(first.sem, first.base + c + 1)
                if c >= n_conv:
                    m = MLA_ROPE if c == n_conv + 2 else P
                    nc.vector.tensor_copy(k.mix[0:m, 2 * (c - n_conv) + 1, :], k.psum[0:m, 2 * slot + 1, :])\
                        .then_inc(k.banks_free, 1)
                    continue
                nc.vector.scalar_tensor_tensor(
                    ypad[:, c, :, PAD:PAD + LAT], k.psum[:, 2 * slot, :].rearrange("p (s t) -> p s t", s=2),
                    column(k.vec, k.vec_at["glu_b"] + c), k.square[:, c % 2, :].rearrange("p (s t) -> p s t", s=2),
                    ALU.add, ALU.mult).then_inc(k.banks_free, 1)
                if c % 2 == 0:
                    continue
                dve.wait_ge(k.banks_free, RING + spec.start + c + 1)
                two = [(sums[n].rearrange("p (s t) -> p s t", s=2), ypad[:, n], n, k.vec_at["dw_w"] + n) for n in (c - 1, c)]
                base = taps.base + (c - 1) * CONV_W
                for total, y, n, w in two:
                    nc.vector.tensor_scalar(total, y[:, :, 0:LAT], column(k.vec, w), column(k.vec, k.vec_at["dw_b"] + n),
                                            ALU.mult, ALU.add).then_inc(taps.sem, 1)
                per_round = 5
                with dve.Fori(0, (CONV_W - 1) // per_round) as i:
                    for u in range(1, per_round + 1):
                        for m, (total, y, n, w) in enumerate(two):
                            dve.wait_ge(taps.sem, i * (2 * per_round) + (base + 2 * u + m - 1))
                            nc.vector.scalar_tensor_tensor(total, y[:, :, bass.ds(i * per_round + u, LAT)],
                                                           column(k.vec, i * (per_round * n_conv) + (w + u * n_conv)), total,
                                                           ALU.mult, ALU.add).then_inc(taps.sem, 1)
    first.close(spec.n)
    cleared.close(2)
    taps.close(n_conv * CONV_W)

    squared, mean, root, inv = (k.tally(n) for n in ("squared", "mean_done", "root_done", "inverse_done"))
    groups = [([0, 1], P, "kv_norm"), ([2, 3, 4], P, "q_norm")]
    with nc.Block() as block:
        @block.scalar
        def _(act):
            for chunks, rows, _ in groups:
                for c in chunks:
                    nc.scalar.activation(k.h[0:rows, c, :], k.mix[0:rows, c, :], ACT.Square).then_inc(squared.sem, 1)
            for g, (chunks, rows, _) in enumerate(groups):
                act.wait_ge(mean.sem, mean.base + g + 1)
                if g == 2:
                    act.wait_ge(inv.sem, inv.base + 1)
                nc.scalar.activation(k.roots[0:rows, g % 2, :], k.psum[0:rows, g, :], ACT.Sqrt, bias=k.eps[0:rows, 0:1],
                                     scale=1.0 / (rows * len(chunks)))\
                    .then_inc(root.sem, 1)

        @block.tensor
        def _(pe):
            done = 0
            for g, (chunks, rows, _) in enumerate(groups):
                for n, c in enumerate(chunks):
                    done += 1
                    pe.wait_ge(squared.sem, squared.base + done)
                    mm = nc.tensor.matmul(k.psum[0:rows, g, :], k.const("ones")[0:rows, 0:rows], k.h[0:rows, c, :],
                                          start=n == 0, stop=n == len(chunks) - 1)
                mm.then_inc(mean.sem, 1)

        @block.vector
        def _(dve):
            for g, (chunks, rows, gain) in enumerate(groups):
                dve.wait_ge(root.sem, root.base + g + 1)
                nc.vector.reciprocal(k.rinvs[0:rows, g % 2, :], k.roots[0:rows, g % 2, :]).then_inc(inv.sem, 1)
                dve.wait_ge(inv.sem, inv.base + g + 1)
                for n, c in enumerate(chunks):
                    nc.vector.scalar_tensor_tensor(k.mix[0:rows, c, :], k.mix[0:rows, c, :], column(k.vec, k.vec_at[gain] + n, slice(0, rows)),
                                                   k.rinvs[0:rows, g % 2, :], ALU.mult, ALU.mult)
    squared.close(5), mean.close(2), root.close(2), inv.close(2)

    spec = k.spec("heads0")
    item, out = k.tally("item_done"), k.tally("item_out")
    with nc.Block() as block:
        stream_ahead(k, block, spec)
        slots = [(spec.start + c) % RING for c in range(2)]
        uk, uv = (k.slots[slots[0]][:, n * 1024:(n + 1) * 1024].rearrange("p (k n) -> p k n", k=2) for n in range(2))
        uq = k.slots[slots[1]][:, 0:2304].rearrange("p (k h e) -> p k h e", k=3, h=HEADS)

        @block.scalar
        def _(act):
            for h in range(HEADS):
                nc.scalar.activation(kn[HD:width, h, :], k.mix[0:MLA_ROPE, 5, :], ACT.Copy)

        @block.tensor
        def _(pe):
            n = 0

            def free_bank():
                if n >= 8:
                    pe.wait_ge(out.sem, out.base + n - 7)
                return n % 8

            wait_weights(k, pe, spec, 0, 0)
            for pair in range(HEADS // 2):
                bank = free_bank()
                for kc in range(2):
                    mm = nc.tensor.matmul(k.psum[:, bank, :], uk[:, kc, pair * P:(pair + 1) * P], k.mix[:, kc, :],
                                          start=kc == 0, stop=kc == 1)
                mm.then_inc(item.sem, 1)
                n += 1
            for tt in range(4):
                bank = free_bank()
                for kc in range(2):
                    mm = nc.tensor.matmul(k.psum[:, bank, :], k.mix[:, kc, tt * P:(tt + 1) * P], uv[:, kc, :],
                                          start=kc == 0, stop=kc == 1)
                mm.then_inc(item.sem, 1)
                n += 1
            wait_weights(k, pe, spec, 0, 1)
            for h in range(HEADS):
                bank = free_bank()
                for kc in range(3):
                    mm = nc.tensor.matmul(k.psum[0:HD + MLA_ROPE, bank, :], uq[:, kc, h, :], k.mix[:, 2 + kc, :],
                                          start=kc == 0, stop=kc == 2)
                mm.then_inc(item.sem, 1)
                n += 1

        @block.vector
        def _(dve):
            for n in range(HEADS // 2 + 4 + HEADS):
                dve.wait_ge(item.sem, item.base + n + 1)
                bank = k.psum[:, n % 8, :]
                if n < 4:
                    for hh in range(2):
                        last = nc.vector.tensor_copy(kn[0:HD, 2 * n + hh, :], bank[hh * HD:(hh + 1) * HD])
                elif n < 8:
                    last = nc.vector.tensor_copy(k.v[:, n - 4, :], bank)
                else:
                    last = nc.vector.tensor_copy(qn[0:width, n - 8, :], bank[0:width])
                last.then_inc(out.sem, 1)
            dve.sem_inc(k.unit_done, 2)
            dve.sem_inc(k.banks_free, 2)
    item.close(16), out.close(16)

    scaled_gains(k, width ** -0.5, ["mla_q"])
    for heads, gain in ((kn, "mla_k"), (qn, "mla_q")):
        norm_heads(k, heads, P, HEADS, TOK, k.const("mean96"), column(k.vec, k.vec_at[gain]))
    both = k.arena[:, 0:2 * HEADS * TOK].rearrange("p (h t) -> p h t", h=2 * HEADS)
    rotate_heads(k, both, P, 2 * HEADS, k.const("turn96"), k.const("cos96"), k.const("sin96"))

    convolution(k, sums)
    for queries, keys, tile0, tiles in ((slice(0, LAT), slice(0, TOK), 0, 4), (slice(LAT, TOK), slice(LAT, TOK), 2, 2)):
        def score(ps, b, hh, qt, keys=keys):
            tile = slice(qt * P, (qt + 1) * P)
            return nc.tensor.matmul(ps, k.q_stage[:, hh, tile], one(kn, b * 2 + hh, col=keys), start=True, stop=True)

        attention(k, HEADS // 2, tiles, lambda b: [(k.q_stage[:, :, :], qn[:, bass.ds(b * 2, 2), queries])],
                  score, lambda b, hh, kt: k.v[:, tile0 + kt, bass.ds(b * P + hh * HD, HD)], HD,
                  lambda b: one(k.mix, b, col=queries))


def scaled_gains(k, scale, names):
    done = k.tally("derived")
    with k.nc.Block() as block:
        @block.vector
        def _(dve):
            for name in names:
                c = column(k.vec, k.vec_at[name])
                k.nc.vector.tensor_scalar(c, c, scale, None, ALU.mult).then_inc(done.sem, 1)
    done.close(len(names))


def convolution(k, acc):
    nc, C = k.nc, 4
    t = {n: k.tally(n) for n in ("mean_done", "centred", "squared", "root_done", "inverse_done", "normed")}
    dst = [k.mix[:, 4 + c, :] for c in range(C)]
    with nc.Block() as block:
        @block.vector
        def _(dve):
            dve.wait_ge(t["mean_done"].sem, t["mean_done"].base + 1)
            for c in range(C):
                nc.vector.tensor_tensor(acc[c], acc[c], k.psum[:, 0, :], ALU.subtract).then_inc(t["centred"].sem, 1)
            dve.wait_ge(t["root_done"].sem, t["root_done"].base + 1)
            nc.vector.reciprocal(k.rinv[:, :], k.root[:, :]).then_inc(t["inverse_done"].sem, 1)
            dve.wait_ge(t["inverse_done"].sem, t["inverse_done"].base + 1)
            for c in range(C):
                nc.vector.scalar_tensor_tensor(dst[c], acc[c], column(k.vec, k.vec_at["ln_g"] + c), k.rinv[:, :],
                                               ALU.mult, ALU.mult).then_inc(t["normed"].sem, 1)

        @block.tensor
        def _(pe):
            for c in range(C):
                mm = nc.tensor.matmul(k.psum[:, 0, :], k.const("mean512"), acc[c], start=c == 0, stop=c == C - 1)
            mm.then_inc(t["mean_done"].sem, 1)
            for c in range(C):
                pe.wait_ge(t["squared"].sem, t["squared"].base + c + 1)
                mm = nc.tensor.matmul(k.psum[:, 1, :], k.const("mean512"), k.h[:, c, :], start=c == 0, stop=c == C - 1)
            mm.then_inc(t["mean_done"].sem, 1)

        @block.scalar
        def _(act):
            for c in range(C):
                act.wait_ge(t["centred"].sem, t["centred"].base + c + 1)
                nc.scalar.activation(k.h[:, c, :], acc[c], ACT.Square).then_inc(t["squared"].sem, 1)
            act.wait_ge(t["mean_done"].sem, t["mean_done"].base + 2)
            nc.scalar.activation(k.root[:, :], k.psum[:, 1, :], ACT.Sqrt, bias=k.eps[:, 0:1]).then_inc(t["root_done"].sem, 1)
            for c in range(C):
                act.wait_ge(t["normed"].sem, t["normed"].base + c + 1)
                nc.scalar.activation(dst[c], dst[c], ACT.Silu, bias=column(k.vec, k.vec_at["ln_b"] + c))
    for name, n in dict(mean_done=2, centred=C, squared=C, root_done=1, inverse_done=1, normed=C).items():
        t[name].close(n)



def odd_mixer(k, w):
    nc = k.nc
    A = k.arena

    def heads(at, n, t):
        return A[:, at:at + n * t].rearrange("p (h t) -> p h t", h=n)

    ck, nk = heads(0, 2, TOK), heads(2 * TOK, HEADS, TOK)
    cq, nq = heads(10 * TOK, HEADS, LAT), heads(14 * TOK, HEADS, LAT)
    bias = k.side[:, 0:2 * HEADS * LAT].rearrange("p (q h k) -> p q h k", q=2, h=HEADS)

    spec = k.spec("in1")
    first, landed, masked = k.tally("first_bank_out"), k.tally("bias_landed"), k.tally("bias_masked")
    rows = LAT // GRID_W
    with nc.Block() as block:
        stream_ahead(k, block, spec)

        @block.gpsimd
        def _(pool):
            nc.gpsimd.memset(A[HD:P, 0:18 * TOK], 0.0)

        @block.tensor
        def _(pe):
            for c in range(spec.n):
                slot = wait_weights(k, pe, spec, 0, c)
                W = wide_tile(k.slots[slot])
                T = slice(0, TOK if c < 5 else LAT)
                if c in (0, 1, 2, 5, 6, 7, 8):
                    for t in range(1 if c == 0 else 2):
                        for kc in range(KD):
                            mm = nc.tensor.matmul(k.psum[:, 2 * slot + t, T], W[:, kc, t * P:(t + 1) * P], k.h[:, kc, T],
                                                  start=kc == 0, stop=kc == KD - 1)
                if c in (0, 3, 4):
                    n = P if c == 0 else 256
                    for tt in range(4):
                        at = k.psum[:, 2 * slot + 1, tt * P:(tt + 1) * P] if c == 0 else \
                            k.psum[:, 2 * slot + tt // 2, (tt % 2) * n:(tt % 2 + 1) * n]
                        for kc in range(KD):
                            mm = nc.tensor.matmul(at, k.h[:, kc, tt * P:(tt + 1) * P], W[:, kc, 256 - n:256],
                                                  start=kc == 0, stop=kc == KD - 1)
                mm.then_inc(k.unit_done, 1)

        def place(engine, copy, bank, c):
            slot = (spec.start + c) % RING
            src = k.psum[:, 2 * slot + bank, :]
            if c == 0 and bank == 1:
                return copy(k.v_shared[:, :, :], src.rearrange("p (t e) -> p t e", t=4))
            if c in (3, 4):
                return copy(k.v[:, 2 * bank:2 * bank + 2, (c - 3) * 256:(c - 2) * 256], src.rearrange("p (t e) -> p t e", t=2))
            to, h, T = {0: (ck, 0, TOK), 1: (nk, 0, TOK), 2: (nk, 4, TOK), 5: (cq, 0, LAT), 6: (cq, 4, LAT),
                        7: (nq, 0, LAT), 8: (nq, 4, LAT)}[c]
            for hh in range(2):
                last = copy(to[0:HD, h + 2 * bank + hh, :], src[hh * HD:(hh + 1) * HD, 0:T])
            return last

        @block.scalar
        def _(act):
            for r in range(rows):
                for j in range(rows):
                    src = bass.AP(w["l1_na_rpb"].tensor, (j - r + RPB_H // 2) * RPB_W + RPB_W // 2 - GRID_W + 1,
                                  [[1, GRID_W], [RPB_H * RPB_W, HEADS], [1, GRID_W]])
                    dst = bias[(r % 2) * GRID_W:(r % 2 + 1) * GRID_W, r // 2, :, j * GRID_W:(j + 1) * GRID_W]
                    act.dma_start(dst, src).then_inc(landed.sem, 16)
            for c in range(spec.n):
                wait_product(k, act, spec, 0, c)
                place(act, lambda o, i: nc.scalar.activation(o, i, ACT.Copy), 0, c).then_inc(first.sem, 1)

        @block.vector
        def _(dve):
            for c in range(spec.n):
                wait_product(k, dve, spec, 0, c)
                dve.wait_ge(first.sem, first.base + c + 1)
                place(dve, nc.vector.tensor_copy, 1, c).then_inc(k.banks_free, 1)
            dve.wait_ge(landed.sem, landed.base + 16 * rows * rows)
            for qt in range(2):
                for h in range(HEADS):
                    nc.vector.tensor_tensor(bias[:, qt, h, :], bias[:, qt, h, :], k.const("window"), ALU.add)\
                        .then_inc(masked.sem, 1)
    first.close(spec.n), landed.close(16 * rows * rows), masked.close(2 * HEADS)

    scaled_gains(k, HD ** -0.5, ["gqa_q", "na_q"])
    for src, n, T, gain in ((ck, 2, TOK, "gqa_k"), (nk, HEADS, TOK, "na_k"), (cq, HEADS, LAT, "gqa_q"), (nq, HEADS, LAT, "na_q")):
        if T == LAT:
            src = src.rearrange("p (a b) t -> p a (b t)", b=2)
            n //= 2
        norm_heads(k, src, P, n, TOK, k.full("mean64"), column(k.vec, k.vec_at[gain]))
    rotate_heads(k, ck, P, 2, k.full("turn64"), k.const("cos64"), k.const("sin64"))
    rotate_heads(k, cq, P, HEADS, k.full("turn64"), k.const("cos64"), k.const("sin64"))

    for g in range(2):
        def score(ps, b, hh, qt, g=g):
            return nc.tensor.matmul(ps, k.q_stage[:, hh, qt * P:(qt + 1) * P], ck[:, g, :], start=True, stop=True)

        attention(k, 2, 4, lambda b: [(k.q_stage[:, :, :], cq[:, bass.ds(b * 2 + 4 * g, 2), :])], score,
                  lambda b, hh, kt: k.v_shared[:, kt, g * HD:(g + 1) * HD], HD, lambda b: one(k.mix, b + 2 * g, col=slice(0, LAT)))

    def score(ps, b, hh, qt):
        nc.tensor.matmul(ps, k.q_stage[:, hh, qt * P:(qt + 1) * P], one(nk, b * 2 + hh), start=True, stop=False)
        return nc.tensor.matmul(ps[:, 0:LAT], k.const("flip"), one(bias[:, qt], b * 2 + hh), start=False, stop=True)

    attention(k, HEADS // 2, 4, lambda b: [(k.q_stage[:, :, :], nq[:, bass.ds(b * 2, 2), :])], score,
              lambda b, hh, kt: k.v[:, kt, bass.ds(b * P + hh * HD, HD)], HD, lambda b: one(k.mix, b + 4, col=slice(0, LAT)))



def rope_tables(k):
    nc = k.nc
    step, done = k.tally("angle_step"), k.tally("table_done")
    R = slice(0, ROPE2)
    ang, turns, low = k.square[R, 0, 0:LAT], k.square[R, 1, 0:LAT], k.roots[R, 0, 0:LAT]
    magic = 1.5 * 2.0 ** 23
    two_pi = 2 * np.pi
    c1 = 6.28125
    c2 = float(np.float32(two_pi - c1))
    c3 = float(two_pi - c1 - c2)
    with nc.Block() as block:
        @block.vector
        def _(dve):
            n = [0]

            def chained(ins):
                n[0] += 1
                ins.then_inc(step.sem, 1)
                dve.wait_ge(step.sem, step.base + n[0])

            nc.vector.memset(k.r_stage[:, 0, :], 1.0)
            nc.vector.memset(k.r_stage[:, 1, :], 0.0)
            chained(nc.vector.tensor_copy(ang, k.positions[:, :]))
            chained(nc.vector.tensor_scalar(ang, ang, k.const("freq")[:, 0:1], None, ALU.mult))
            chained(nc.vector.tensor_scalar(turns, ang, float(1 / two_pi), magic, ALU.mult, ALU.add))
            chained(nc.vector.tensor_scalar(turns, turns, -magic, None, ALU.add))
            for c in (c1, c2, c3):
                chained(nc.vector.scalar_tensor_tensor(ang, turns, -c, ang, ALU.mult, ALU.add))
            top = float(np.nextafter(np.float32(np.pi), np.float32(0)))
            chained(nc.vector.tensor_scalar(ang, ang, top, -top, ALU.min, ALU.max))

        @block.scalar
        def _(act):
            act.wait_ge(step.sem, step.base + 8)
            nc.scalar.activation(low, ang, ACT.Abs).then_inc(done.sem, 1)
            nc.scalar.activation(k.sin2, ang, ACT.Sin).then_inc(done.sem, 1)
            act.wait_ge(done.sem, done.base + 1)
            nc.scalar.activation(k.cos2, low, ACT.Sin, scale=-1.0, bias=k.half_pi[R, 0:1]).then_inc(done.sem, 1)
    step.close(8), done.close(3)


def lambda_init(l):
    return 0.8 - 0.6 * float(np.exp(-0.3 * l))


HEAD_AT = dict(aq=0, ak=8, dq=16, dk=20, iq=24, ik=32, bq=33, bk=37, cq=41, ck=45)
N_HEADS2 = 49
SCALED_UNITS = (0, 1, 4, 8, 10)


def project_heads(k, l):
    nc, spec = k.nc, k.spec(f"in_b{l}")
    first = k.tally("first_bank_out")
    T = slice(0, LAT)
    n_qk, n_v = len(QK_COLUMNS), len(V_COLUMNS)
    values = [k.va[:, :, 0:256], k.va[:, :, 256:512], k.bv, k.cv, k.dv]
    with nc.Block() as block:
        stream_ahead(k, block, spec)

        @block.gpsimd
        def _(pool):
            nc.gpsimd.memset(k.arena[HD:P, 0:N_HEADS2 * LAT], 0.0)

        @block.tensor
        def _(pe):
            for c in range(spec.n):
                slot = wait_weights(k, pe, spec, 0, c)
                W = wide_tile(k.slots[slot])
                b0, b1 = k.psum[:, 2 * slot], k.psum[:, 2 * slot + 1]
                if c < n_qk:
                    parts = [(bank[:, T], lambda kc, t=t: W[:, kc, t * P:(t + 1) * P], lambda kc: k.h[:, kc, T])
                             for t, bank in enumerate((b0, b1))]
                elif c < n_qk + n_v:
                    parts = [(bank[:, T], lambda kc, t=t: k.h[:, kc, t * P:(t + 1) * P], lambda kc: W[:, kc, :])
                             for t, bank in enumerate((b0, b1))]
                else:
                    parts = [(b0[0:HD, T], lambda kc: W[:, kc, 0:HD], lambda kc: k.h[:, kc, T]),
                             (b0[0:4, LAT:TOK], lambda kc: W[:, kc, 72:76], lambda kc: k.h[:, kc, T])]
                    parts += [(b1[:, t * 8:(t + 1) * 8], lambda kc, t=t: k.h[:, kc, t * P:(t + 1) * P],
                               lambda kc: W[:, kc, HD:72]) for t in range(2)]
                for to, lhs, rhs in parts:
                    for kc in range(KD):
                        mm = nc.tensor.matmul(to, lhs(kc), rhs(kc), start=kc == 0, stop=kc == KD - 1)
                mm.then_inc(k.unit_done, 1)

        def head_of(c):
            return 4 * c if c < 8 else HEAD_AT["bq"] + 4 * (c - 8)

        @block.scalar
        def _(act):
            for c in range(spec.n):
                slot = wait_product(k, act, spec, 0, c)
                bank = k.psum[:, 2 * slot]
                if c < n_qk:
                    for hh in range(2):
                        last = nc.scalar.activation(k.heads[0:HD, head_of(c) + hh, :], bank[hh * HD:(hh + 1) * HD, T], ACT.Copy,
                                                    scale=HD ** -0.5 if c in SCALED_UNITS else 1.0)
                elif c < n_qk + n_v:
                    last = nc.scalar.activation(values[c - n_qk][:, 0], bank[:, T], ACT.Copy)
                else:
                    nc.scalar.activation(k.heads[0:HD, HEAD_AT["ik"], :], bank[0:HD, T], ACT.Copy)
                    last = nc.scalar.activation(k.forget, bank[0:4, LAT:TOK], ACT.Identity,
                                                bias=column(k.vec, k.vec_at[f"fgt{l}"], slice(0, 4)))
                last.then_inc(first.sem, 1)

        @block.vector
        def _(dve):
            for c in range(spec.n):
                slot = wait_product(k, dve, spec, 0, c)
                dve.wait_ge(first.sem, first.base + c + 1)
                bank = k.psum[:, 2 * slot + 1]
                if c < n_qk:
                    for hh in range(2):
                        last = nc.vector.tensor_scalar(k.heads[0:HD, head_of(c) + 2 + hh, :], bank[hh * HD:(hh + 1) * HD, T],
                                                       HD ** -0.5 if c in SCALED_UNITS else 1.0, None, ALU.mult)
                elif c < n_qk + n_v:
                    last = nc.vector.tensor_copy(values[c - n_qk][:, 1], bank[:, T])
                else:
                    last = nc.vector.tensor_copy(k.index_weight, bank[:, 0:16])
                last.then_inc(k.banks_free, 1)
    first.close(spec.n)


def log_sigmoids(k, l):
    nc = k.nc
    t = {n: k.tally(n) for n in ("magnitude", "exp_done", "log_done", "sum_step", "dots", "lambda_exp", "selector_landed")}
    mag, low = k.square[0:4, 0, 0:LAT], k.square[0:4, 1, 0:LAT]
    with nc.Block() as block:
        @block.vector
        def _(dve):
            nc.vector.memset(k.ones_row, 1.0).then_inc(t["sum_step"].sem, 1)
            for v in range(2):
                nc.vector.scalar_tensor_tensor(k.roots[:, v, 0:HD], k.lam[:, l, 2 * v, :], 1.0, k.lam[:, l, 2 * v + 1, :],
                                               ALU.mult, ALU.mult, accum_out=k.lam_exp[:, v:v + 1]).then_inc(t["dots"].sem, 1)
            dve.wait_ge(t["log_done"].sem, t["log_done"].base + 1)
            nc.vector.scalar_tensor_tensor(low, k.forget, 0.0, mag, ALU.min, ALU.subtract).then_inc(t["sum_step"].sem, 1)
            dve.wait_ge(t["sum_step"].sem, t["sum_step"].base + 2)
            nc.vector.tensor_tensor_scan(k.cum, k.ones_row, low, 0.0, ALU.mult, ALU.add).then_inc(t["sum_step"].sem, 1)
            dve.wait_ge(t["sum_step"].sem, t["sum_step"].base + 3)
            dve.wait_ge(t["selector_landed"].sem, t["selector_landed"].base + 16)
            for h in range(4):
                nc.vector.scalar_tensor_tensor(k.minus_cum[:, h, :], k.sel[:, h, :], -1.0, k.cum, ALU.mult, ALU.mult)\
                    .then_inc(t["sum_step"].sem, 1)
            dve.wait_ge(t["lambda_exp"].sem, t["lambda_exp"].base + 1)
            nc.vector.tensor_scalar(k.lam_exp[:, 1:2], k.lam_exp[:, 1:2], -lambda_init(l), None, ALU.add)\
                .then_inc(t["sum_step"].sem, 1)
            dve.wait_ge(t["sum_step"].sem, t["sum_step"].base + 8)
            nc.vector.tensor_tensor(k.minus_lam, k.lam_exp[:, 1:2], k.lam_exp[:, 0:1], ALU.subtract).then_inc(t["sum_step"].sem, 1)

        @block.scalar
        def _(act):
            nc.scalar.activation(mag, k.forget, ACT.Abs).then_inc(t["magnitude"].sem, 1)
            act.wait_ge(t["magnitude"].sem, t["magnitude"].base + 1)
            nc.scalar.activation(mag, mag, ACT.Exp, scale=-1.0).then_inc(t["exp_done"].sem, 1)
            act.wait_ge(t["dots"].sem, t["dots"].base + 2)
            nc.scalar.activation(k.lam_exp[:, 0:2], k.lam_exp[:, 0:2], ACT.Exp).then_inc(t["lambda_exp"].sem, 1)
            act.wait_ge(t["exp_done"].sem, t["exp_done"].base + 1)
            nc.scalar.activation(mag, mag, ACT.Ln, bias=1.0).then_inc(t["log_done"].sem, 1)

        @block.sync
        def _(sp):
            sp.dma_start(k.sel, k.selector).then_inc(t["selector_landed"].sem, 16)
    for name, n in dict(magnitude=1, exp_done=1, log_done=1, sum_step=9, dots=2, lambda_exp=1, selector_landed=16).items():
        t[name].close(n)


def select_keys(k):
    nc = k.nc
    t = {n: k.tally(n) for n in ("scored", "rectified", "summed", "best_found", "taken")}
    n_pairs, rounds = 4, TOPK // 8
    with nc.Block() as block:
        @block.tensor
        def _(pe):
            for qt in range(2):
                for j in range(n_pairs):
                    n = qt * n_pairs + j
                    for jj in range(2):
                        mm = nc.tensor.matmul(k.psum[:, n, jj * LAT:(jj + 1) * LAT],
                                              k.heads[:, HEAD_AT["iq"] + 2 * j + jj, qt * P:(qt + 1) * P],
                                              k.heads[:, HEAD_AT["ik"], :], start=True, stop=True)
                    mm.then_inc(t["scored"].sem, 1)

        @block.scalar
        def _(act):
            for n in range(2 * n_pairs):
                act.wait_ge(t["scored"].sem, t["scored"].base + n + 1)
                if n >= 2:
                    act.wait_ge(t["summed"].sem, t["summed"].base + 2 * (n - 1))
                nc.scalar.activation(k.square[:, n % 2, :], k.psum[:, n, :], ACT.Relu).then_inc(t["rectified"].sem, 1)

        @block.vector
        def _(dve):
            for n in range(2 * n_pairs):
                qt, j = n // n_pairs, n % n_pairs
                dve.wait_ge(t["rectified"].sem, t["rectified"].base + n + 1)
                for jj in range(2):
                    if (j, jj) == (0, 0):
                        before = k.const("causal")[:, qt * LAT:(qt + 1) * LAT]
                    else:
                        before = k.score[:, qt, :]
                        dve.wait_ge(t["summed"].sem, t["summed"].base + 2 * n + jj)
                    nc.vector.scalar_tensor_tensor(k.score[:, qt, :], k.square[:, n % 2, jj * LAT:(jj + 1) * LAT],
                                                   k.index_weight[:, qt * 8 + 2 * j + jj:qt * 8 + 2 * j + jj + 1], before,
                                                   ALU.mult, ALU.add).then_inc(t["summed"].sem, 1)
            dve.wait_ge(t["summed"].sem, t["summed"].base + 4 * n_pairs)
            for r in range(rounds):
                for qt in range(2):
                    if r:
                        dve.wait_ge(t["taken"].sem, t["taken"].base + 2 * (r - 1) + qt + 1)
                    nc.vector.max(k.best[:, qt, :], k.score[:, qt, :]).then_inc(t["best_found"].sem, 1)
                for qt in range(2):
                    dve.wait_ge(t["best_found"].sem, t["best_found"].base + 2 * r + qt + 1)
                    nc.vector.match_replace(k.score[:, qt, :], k.best[:, qt, :], k.score[:, qt, :], TAKEN).then_inc(t["taken"].sem, 1)
            for qt in range(2):
                dve.wait_ge(t["taken"].sem, t["taken"].base + 2 * rounds + qt - 1)
                nc.vector.tensor_scalar(k.chosen[:, qt, :], k.score[:, qt, :], TAKEN / 2, MASKED, ALU.is_gt, ALU.mult)\
                    .then_inc(t["taken"].sem, 1)
            for qt in range(2):
                dve.wait_ge(t["taken"].sem, t["taken"].base + 2 * rounds + qt + 1)
                nc.vector.tensor_tensor(k.chosen[:, qt, :], k.chosen[:, qt, :], k.const("causal")[:, qt * LAT:(qt + 1) * LAT], ALU.add)\
                    .then_inc(t["taken"].sem, 1)
    for name, n in dict(scored=2 * n_pairs, rectified=2 * n_pairs, summed=4 * n_pairs, best_found=2 * rounds,
                        taken=2 * rounds + 4).items():
        t[name].close(n)


def stick_breaking(k):
    nc, N = k.nc, 4
    names = ("logits", "magnitude", "exp_done", "log_done", "softplus", "kept", "summed_later", "in_exponent", "exponent",
             "weight_exp", "masked", "weighted", "placed")
    t = {n: k.tally("sb_" + n) for n in names}
    strict = k.const("strict")

    def buf(h):
        return k.square[:, h % 2, :], k.roots[:, h % 2, :], k.rinvs[:, h % 2, :]

    def weigh(pe, h):
        _, _, weights = buf(h)
        pe.wait_ge(t["masked"].sem, t["masked"].base + h + 1)
        if h >= 2:
            pe.wait_ge(t["placed"].sem, t["placed"].base + h - 1)
        for kt in range(2):
            mm = nc.tensor.matmul(k.psum[0:HD, 6 + h % 2, 0:LAT], k.cv[:, kt, h * HD:(h + 1) * HD],
                                  weights[:, kt * LAT:(kt + 1) * LAT], start=kt == 0, stop=kt == 1)
        mm.then_inc(t["weighted"].sem, 1)

    with nc.Block() as block:
        @block.tensor
        def _(pe):
            for h in range(N):
                for kt in range(2):
                    mm = nc.tensor.matmul(k.psum[:, h, kt * LAT:(kt + 1) * LAT],
                                          k.heads[:, HEAD_AT["ck"] + h, kt * P:(kt + 1) * P],
                                          k.heads[:, HEAD_AT["cq"] + h, :], start=True, stop=True)
                mm.then_inc(t["logits"].sem, 1)
            for h in range(N):
                _, _, kept = buf(h)
                pe.wait_ge(t["kept"].sem, t["kept"].base + h + 1)
                if h >= 2:
                    pe.wait_ge(t["exponent"].sem, t["exponent"].base + h - 1)
                bank = k.psum[:, 4 + h % 2, :]
                nc.tensor.matmul(bank[:, 0:LAT], k.const("later"), kept[:, 0:LAT], start=True, stop=False)
                nc.tensor.matmul(bank[:, 0:LAT], k.const("ones"), kept[:, LAT:TOK], start=False, stop=True)
                nc.tensor.matmul(bank[:, LAT:TOK], k.const("later"), kept[:, LAT:TOK], start=True, stop=True)\
                    .then_inc(t["summed_later"].sem, 1)
                if h >= 1:
                    weigh(pe, h - 1)
            weigh(pe, N - 1)

        @block.vector
        def _(dve):
            def middle(h):
                low, soft, kept = buf(h)
                dve.wait_ge(t["log_done"].sem, t["log_done"].base + h + 1)
                if h >= 2:
                    dve.wait_ge(t["masked"].sem, t["masked"].base + h - 1)
                nc.vector.scalar_tensor_tensor(soft, k.psum[:, h, :], 0.0, low, ALU.max, ALU.add).then_inc(t["softplus"].sem, 1)
                dve.wait_ge(t["softplus"].sem, t["softplus"].base + h + 1)
                if h >= 2:
                    dve.wait_ge(t["weighted"].sem, t["weighted"].base + h - 1)
                nc.vector.scalar_tensor_tensor(kept, soft, -1.0, strict, ALU.mult, ALU.mult).then_inc(t["kept"].sem, 1)
                nc.vector.tensor_tensor(low, k.psum[:, h, :], soft, ALU.subtract).then_inc(t["in_exponent"].sem, 1)
                dve.wait_ge(t["in_exponent"].sem, t["in_exponent"].base + h + 1)
                dve.wait_ge(t["summed_later"].sem, t["summed_later"].base + h + 1)
                nc.vector.tensor_tensor(soft, low, k.psum[:, 4 + h % 2, :], ALU.add).then_inc(t["exponent"].sem, 1)

            def end(h):
                low, soft, kept = buf(h)
                dve.wait_ge(t["weight_exp"].sem, t["weight_exp"].base + h + 1)
                nc.vector.tensor_tensor(kept, soft, strict, ALU.mult).then_inc(t["masked"].sem, 1)

            middle(0), middle(1)
            for h in range(N):
                end(h)
                if h >= 1 and h + 1 < N:
                    middle(h + 1)

        @block.scalar
        def _(act):
            def begin(h):
                low, soft, kept = buf(h)
                act.wait_ge(t["logits"].sem, t["logits"].base + h + 1)
                if h >= 2:
                    act.wait_ge(t["exponent"].sem, t["exponent"].base + h - 1)
                nc.scalar.activation(low, k.psum[:, h, :], ACT.Abs).then_inc(t["magnitude"].sem, 1)
                act.wait_ge(t["magnitude"].sem, t["magnitude"].base + h + 1)
                nc.scalar.activation(low, low, ACT.Exp, scale=-1.0).then_inc(t["exp_done"].sem, 1)
                act.wait_ge(t["exp_done"].sem, t["exp_done"].base + h + 1)
                nc.scalar.activation(low, low, ACT.Ln, bias=1.0).then_inc(t["log_done"].sem, 1)

            def end(h):
                low, soft, kept = buf(h)
                act.wait_ge(t["exponent"].sem, t["exponent"].base + h + 1)
                nc.scalar.activation(soft, soft, ACT.Exp).then_inc(t["weight_exp"].sem, 1)

            def place(h):
                act.wait_ge(t["weighted"].sem, t["weighted"].base + h + 1)
                nc.scalar.activation(k.mix[(h % 2) * HD:(h % 2 + 1) * HD, 6 + h // 2, 0:LAT], k.psum[0:HD, 6 + h % 2, 0:LAT],
                                     ACT.Copy).then_inc(t["placed"].sem, 1)

            begin(0), begin(1)
            for h in range(N):
                end(h)
                if h + 2 < N:
                    begin(h + 2)
                if h >= 1:
                    place(h - 1)
            place(N - 1)
    for name in names:
        t[name].close(N)


def merge_branches(k, l):
    nc, spec = k.nc, k.spec(f"merge_b{l}")
    T = slice(0, LAT)
    opened, product, summed = (k.tally(n) for n in ("gates_open", "gated", "gated_sum"))
    bias = k.vec_at[f"gate_b{l}"]
    y = dict(a=[k.mix[:, c, T] for c in range(4)], b=[k.mix[:, c, T] for c in (4, 5)],
             c=[k.mix[:, c, T] for c in (6, 7)], d=[k.mix[:, c, LAT:TOK] for c in range(2)])
    parts = [[(0, 16, y["a"]), (3, 20, y["d"])], [(1, 16, y["b"]), (2, 18, y["c"])]]
    with nc.Block() as block:
        stream_ahead(k, block, spec)

        @block.tensor
        def _(pe):
            def unit(i, c):
                slot = wait_weights(k, pe, spec, i, c)
                W = tall_tile(k.slots[slot])
                for n, (_, row, chunks) in enumerate(parts[c % 2]):
                    half = slice(n * LAT, (n + 1) * LAT)
                    for kc in range(KD):
                        nc.tensor.matmul(k.psum[:, 2 * slot, half], W[:, n * KD + kc, :], k.h[:, kc, T],
                                         start=kc == 0, stop=kc == KD - 1)
                    for kc, chunk in enumerate(chunks):
                        mm = nc.tensor.matmul(k.psum[:, 2 * slot + 1, half], W[:, row + kc, :], chunk,
                                              start=kc == 0, stop=kc == len(chunks) - 1)
                mm.then_inc(k.unit_done, 1)
            each_unit(pe, 0, spec.n, unit)

        @block.scalar
        def _(act):
            def unit(i, c):
                slot = wait_product(k, act, spec, i, c)
                act.wait_ge(k.banks_free, i * RING + (RING + spec.start + c - 1))
                for n, (gate, _, _) in enumerate(parts[c % 2]):
                    at = i * (RING // 2) + (bias + gate * KD + c // 2)
                    last = nc.scalar.activation(k.square[:, c % 2, n * LAT:(n + 1) * LAT],
                                                k.psum[:, 2 * slot, n * LAT:(n + 1) * LAT], ACT.Sigmoid,
                                                bias=column(k.vec, at))
                last.then_inc(opened.sem, 1)
            each_unit(act, 0, spec.n, unit)

        @block.vector
        def _(dve):
            def unit(i, c):
                slot = wait_product(k, dve, spec, i, c)
                dve.wait_ge(opened.sem, i * RING + (opened.base + c + 1))
                tmp = k.roots[:, c % 2, :]
                nc.vector.tensor_tensor(tmp, k.square[:, c % 2, :], k.psum[:, 2 * slot + 1, :], ALU.mult).then_inc(product.sem, 1)
                dve.wait_ge(product.sem, i * RING + (product.base + c + 1))
                row = one(k.merged, i * (RING // 2) + c // 2)
                if c % 2 == 0:
                    nc.vector.tensor_tensor(row, tmp[:, 0:LAT], tmp[:, LAT:TOK], ALU.add).then_inc(k.banks_free, 1)
                else:
                    nc.vector.tensor_tensor(row, row, tmp[:, 0:LAT], ALU.add).then_inc(summed.sem, 1)
                    dve.wait_ge(summed.sem, i * (RING // 2) + (summed.base + c // 2 + 1))
                    nc.vector.tensor_tensor(row, row, tmp[:, LAT:TOK], ALU.add).then_inc(k.banks_free, 1)
            each_unit(dve, 0, spec.n, unit)
    opened.close(spec.n), product.close(spec.n), summed.close(spec.n // 2)


def hybrid_mixer(k, l):
    nc = k.nc
    causal = [k.const("causal")[:, qt * LAT:(qt + 1) * LAT] for qt in range(2)]
    project_heads(k, l)
    rotate_heads(k, k.heads, P, HEAD_AT["ik"] + 1, k.full("turn16"), k.r_stage[:, 0, :], k.r_stage[:, 1, :])
    log_sigmoids(k, l)

    def logits(ps, q, hh, qt, key_head, last=False):
        return nc.tensor.matmul(ps, k.q_stage[:, hh, qt * P:(qt + 1) * P], one(k.heads, key_head), start=True, stop=last)

    def queries(name):
        return lambda b: [(k.q_stage[:, :, :], k.heads[:, bass.ds(b * 2 + HEAD_AT[name], 2), :])]

    def score(ps, b, hh, qt):
        logits(ps, "aq", hh, qt, b * 2 + (HEAD_AT["ak"] + hh))
        return nc.tensor.matmul(ps, k.const("ident"), causal[qt], start=False, stop=True)

    attention(k, 4, 2, queries("aq"), score, lambda b, hh, kt: k.va[:, kt, bass.ds(b * P, P)], P,
              lambda b: one(k.mix, b, col=slice(0, LAT)), difference=k.minus_lam)
    scaled_gains(k, 1.0 - lambda_init(l), [f"diff{l}"])
    norm_heads(k, k.mix, P, 4, LAT, k.const("ones"), column(k.vec, k.vec_at[f"diff{l}"]), scale=1.0 / P, eps=k.eps5)

    def score(ps, b, hh, qt):
        logits(ps, "bq", hh, qt, b * 2 + (HEAD_AT["bk"] + hh))
        nc.tensor.matmul(ps, k.const("ident"), causal[qt], start=False, stop=False)
        nc.tensor.matmul(ps, k.cum[:, qt * P:(qt + 1) * P], one(k.sel, b * 2 + hh), start=False, stop=False)
        return nc.tensor.matmul(ps, k.const("ones")[0:4, :], one(k.minus_cum, b * 2 + hh), start=False, stop=True)

    attention(k, 2, 2, queries("bq"), score, lambda b, hh, kt: k.bv[:, kt, bass.ds(b * P + hh * HD, HD)], HD,
              lambda b: one(k.mix, b + 4, col=slice(0, LAT)))

    stick_breaking(k)

    select_keys(k)

    def score(ps, b, hh, qt):
        logits(ps, "dq", hh, qt, b * 2 + (HEAD_AT["dk"] + hh))
        return nc.tensor.matmul(ps, k.const("ident"), k.chosen[:, qt, :], start=False, stop=True)

    attention(k, 2, 2, queries("dq"), score, lambda b, hh, kt: k.dv[:, kt, bass.ds(b * P + hh * HD, HD)], HD,
              lambda b: one(k.mix, b, col=slice(LAT, TOK)))
    merge_branches(k, l)
    add_product(k, k.spec(f"out_b{l}"), LAT, k.merged, KD, wide_lhs, 2, 1.0)


def second_buffers(k):
    k.heads = k.arena[:, 0:N_HEADS2 * LAT].rearrange("p (h t) -> p h t", h=N_HEADS2)
    k.merged = k.arena[:, 0:KD * LAT].rearrange("p (c t) -> p c t", c=KD)
    k.va = k.v[:, 0:2, :]
    k.bv, k.cv = (k.v[:, n, :].rearrange("p (t e) -> p t e", t=2) for n in (2, 3))
    k.dv = k.v_shared[:, :, :].rearrange("p a b -> p (a b)").rearrange("p (t e) -> p t e", t=2)
    at = [0]

    def side(rows, *shape):
        n = int(np.prod(shape))
        part = k.side[0:rows, at[0]:at[0] + n]
        at[0] += n
        return part if len(shape) == 1 else part.rearrange("p (a b) -> p a b", a=shape[0])

    k.sel, k.minus_cum = side(4, 4, LAT), side(4, 4, LAT)
    k.forget, k.cum, k.ones_row = side(4, LAT), side(4, LAT), side(4, LAT)
    k.chosen, k.score = side(P, 2, LAT), side(P, 2, LAT)
    k.best, k.index_weight = side(P, 2, 8), side(P, 16)
    k.lam_exp, k.minus_lam = side(P, 2), side(P, 1)


def second_block(k, w):
    k.cos2, k.sin2 = k.r_stage[0:ROPE2, 0, :], k.r_stage[0:ROPE2, 1, :]
    k.selector = w["selector"].rearrange("j (h t) -> j h t", h=4)
    rope_tables(k)
    for l in (0, 1):
        for m in ("ffn1", "mix", "ffn2"):
            at_gain = k.vec_at[f"{m}_b{l}"]
            gain = lambda c, cond, at_gain=at_gain: column(k.vec, at_gain + c)
            if m == "mix":
                with mixer_buffers(k):
                    second_buffers(k)
                    norm_tokens(k, LAT, gain)
                    hybrid_mixer(k, l)
            else:
                half_ffn(k, LAT, m, f"_b{l}", gain, None, 0.5)



def mixer_buffers(k):
    stack = ExitStack()
    k.scope += 1

    def sb(name, shape):
        return stack.enter_context(k.nc.sbuf_tensor(f"{name}_{k.scope}", shape, F32))

    k.h, k.mix = sb("h", [P, KD, TOK]), sb("mix", [P, KD, TOK])
    k.arena = sb("arena", [P, 12800])
    k.side = sb("side", [P, 4096])
    k.v, k.v_shared = sb("v", [P, 4, 512]), sb("v_shared", [P, 4, P])
    k.prob = lambda j, keys: k.h[:, j, TOK - keys:TOK]
    k.prob_t = lambda u, keys: k.h[:, 4 + u, TOK - keys:TOK]
    k.out_rows = k.h[:, 6, LAT:TOK].rearrange("p (q e) -> p q e", q=2)
    return stack


def program(nc, w, out):
    rows, vec_at = vector_rows()
    _, const_at = constant_table()
    with ExitStack() as ctx:
        def sb(name, shape, dt=F32):
            return ctx.enter_context(nc.sbuf_tensor(name, shape, dt))

        tallies = {}

        def tally(name):
            if name not in tallies:
                tallies[name] = Tally(ctx.enter_context(nc.semaphore(name)))
            return tallies[name]

        k = Shared()
        k.nc, k.tally = nc, tally
        k.vec_rows, k.vec_at, k.n_rows = rows, vec_at, sum(r[2] for r in rows)
        n_const = sum(n for _, _, n in const_at.values())
        k.consts = sb("consts", [P, n_const])
        k.const = lambda name: k.consts[0:const_at[name][0], const_at[name][1]:const_at[name][1] + const_at[name][2]]
        k.full = lambda name: k.consts[:, const_at[name][1]:const_at[name][1] + const_at[name][2]]
        k.vec = sb("vec", [P, 4 * P])
        k.eps, k.eps5, k.half_pi = sb("eps", [P, 1]), sb("eps5", [P, 1]), sb("half_pi", [P, 1])
        k.cond = sb("cond", [P, KD, 2])
        k.mod = sb("mod", [P, N_MOD * KD, 2])
        k.gain, k.gate = sb("gain", [P, 3, KD, 2]), sb("gate", [P, 2, KD, 2])
        k.lam = sb("lam", [P, 2, 4, HD])
        k.positions = sb("positions", [ROPE2, LAT], mybir.dt.int32)
        k.x = sb("x", [P, KD, TOK])
        k.slots = [sb(f"weights{s}", [P, SLOT]) for s in range(RING)]
        k.q_stage, k.r_stage = sb("q_stage", [P, 2, LAT]), sb("r_stage", [P, 2, LAT])
        k.negmax, k.rowsum, k.inverse = sb("negmax", [P, 4]), sb("rowsum", [P, 4]), sb("inverse", [P, 8])
        k.square, k.roots, k.rinvs = sb("square", [P, 2, TOK]), sb("roots", [P, 2, TOK]), sb("rinvs", [P, 2, TOK])
        k.root, k.rinv = k.roots[:, 0, :], k.rinvs[:, 0, :]
        k.psum = ctx.enter_context(nc.psum_tensor("psum", [P, 8, BANK], F32))
        k.weights_ready = [ctx.enter_context(nc.semaphore(f"weights_ready{s}")) for s in range(RING)]
        k.unit_done = ctx.enter_context(nc.semaphore("unit_done"))
        k.banks_free = ctx.enter_context(nc.semaphore("banks_free"))
        k.plan = weight_plan(w)
        k.spec = lambda name: next(s for s in k.plan if s.name == name)

        k.scope = 0
        with mixer_buffers(k):
            opening(k, w)
        for l in (0, 1):
            conditioning(k, l)
            tokens = TOK
            half_ffn(k, tokens, "ffn1", l, *modulated(k, 0), half_gate(k, 0))
            with mixer_buffers(k):
                norm_tokens(k, tokens, *modulated(k, 1))
                if l == 0:
                    even_mixer(k)
                else:
                    odd_mixer(k, w)
                    tokens = LAT
                add_product(k, k.spec(f"out{l}"), tokens, k.mix, KD, wide_lhs, 2, mix_gate(k))
            half_ffn(k, tokens, "ffn2", l, *modulated(k, 2), half_gate(k, 1))
        second_block(k, w)
        with mixer_buffers(k):
            norm_tokens(k, LAT, lambda c, cond: column(k.vec, vec_at["final"] + c))
            ending(k, out)



def kernel(**inputs):
    import concourse.bacc as bacc
    from concourse.bass_utils import run_bass_kernel_spmd

    nc = bacc.Bacc("TRN2", target_bir_lowering=False, num_devices=1)
    arrays, w = {}, {}
    for name, value in {**inputs, "constants": constant_table()[0], "selector": selector()}.items():
        a = np.ascontiguousarray(value)
        arrays["in_" + name] = a
        w[name] = nc.dram_tensor("in_" + name, a.shape, mybir.dt.from_np(a.dtype), kind="ExternalInput").ap()
    out = nc.dram_tensor("out", (1, LAT, D), F32, kind="ExternalOutput").ap()
    program(nc, w, out)
    return run_bass_kernel_spmd(nc, [arrays], core_ids=[0]).results[0]["out"]
```

```python
from contextlib import ExitStack

import numpy as np

import concourse.bass as bass
from concourse import mybir

F32 = mybir.dt.float32
F32R = mybir.dt.float32r
ACT = mybir.ActivationFunctionType
ALU = mybir.AluOpType
AX = mybir.AxisListType

P = 128
D = 1024
KD = D // P
LAT, CTX = 256, 256
TOK = LAT + CTX
FF = 2816
KF = FF // P
N_MOD = 9
EPS = 1e-6
HD = 64
HEADS = 8
MLA_ROPE = 32
GRID_W = 64
WIN_W = 16
RPB_H, RPB_W = 15, 31
CONV_W = 31
PAD = CONV_W // 2
ROPE2 = 16
TOPK = 64
BANK = 512

QK_COLUMNS = (0, 256, 512, 768, 3076, 3332, 3844, 4100, 1536, 1792, 2308, 2564)
V_COLUMNS = (1024, 1280, 2048, 2820, 3588)

RING = 4
SLOT = KF * P
MASKED = -1.0e30
TAKEN = -3.0e38


class Tally:

    def __init__(self, sem):
        self.sem, self.base = sem, 0

    def close(self, n):
        self.base += n


class Product:

    def __init__(self, name, n, load, looped, dmas):
        self.name, self.n, self.load, self.looped, self.dmas = name, n, load, looped, dmas
        self.start, self.ready = 0, []


class Shared:
    pass



def constant_table():
    parts, rows = {}, {}

    def put(name, a):
        full = np.zeros((P, a.shape[1]), np.float32)
        full[: a.shape[0]] = a
        parts[name] = full
        rows[name] = a.shape[0]

    put("ident", np.eye(P, dtype=np.float32))
    n = 512
    put(f"mean{n}", np.full((P, P), 1.0 / n, np.float32))
    means = np.zeros((P, 2 * P), np.float32)
    means[:HD, P - 1], means[HD:HD + MLA_ROPE, P] = 1.0 / HD, 1.0 / MLA_ROPE
    put("means", means)
    put("ones", np.ones((P, P), np.float32))
    put("later", np.tril(np.ones((P, P), np.float32), -1))

    def pairs(n):
        r = np.zeros((n, P), np.float32)
        for i in range(0, n, 2):
            r[i + 1, i] = -1.0
            r[i, i + 1] = 1.0
        return r

    put("turn64", pairs(64))
    turn = np.zeros((P, P), np.float32)
    turn[HD:HD + MLA_ROPE, HD:HD + MLA_ROPE] = pairs(MLA_ROPE)[:, 0:MLA_ROPE]
    put("turn96", turn)
    r = np.zeros((ROPE2, P), np.float32)
    for i in range(ROPE2 // 2):
        r[ROPE2 // 2 + i, i] = -1.0
        r[i, ROPE2 // 2 + i] = 1.0
    put("turn16", r)
    t = np.arange(LAT)
    for n in (64, 32):
        q = n // 4
        inv = (np.float32(10000.0) ** (-np.arange(q, dtype=np.float32) / np.float32(q))).astype(np.float32)
        ang = np.concatenate([(t // GRID_W).astype(np.float32)[:, None] * inv,
                              (t % GRID_W).astype(np.float32)[:, None] * inv], axis=1)
        at, name = (0, "64") if n == 64 else (HD, "96")
        cos, sin = np.ones((P, LAT), np.float32), np.zeros((P, LAT), np.float32)
        cos[at:at + n], sin[at:at + n] = np.repeat(np.cos(ang), 2, axis=1).T, np.repeat(np.sin(ang), 2, axis=1).T
        put(f"cos{name}", cos)
        put(f"sin{name}", sin)
    f = (np.float32(500000.0) ** (-np.arange(0, ROPE2, 2, dtype=np.float32) / np.float32(ROPE2))).astype(np.float32)
    put("freq", np.concatenate([f, f])[:, None])
    q, key = np.arange(P)[:, None], np.arange(LAT)[None, :]
    put("causal", np.concatenate([np.where(key <= q + P * i, 0.0, MASKED) for i in range(2)], 1).astype(np.float32))
    put("strict", np.concatenate([(q + P * i < key) for i in range(2)], 1).astype(np.float32))
    qc, kc = GRID_W - 1 - np.arange(P)[:, None] % GRID_W, np.arange(LAT)[None, :] % GRID_W
    start = np.clip(qc - WIN_W // 2, 0, GRID_W - WIN_W)
    put("window", np.where((kc >= start) & (kc < start + WIN_W), 0.0, MASKED).astype(np.float32))
    put("flip", np.kron(np.eye(P // GRID_W), np.eye(GRID_W)[::-1]).astype(np.float32))
    at, col = {}, 0
    for name, a in parts.items():
        at[name] = (rows[name], col, a.shape[1])
        col += a.shape[1]
    return np.ascontiguousarray(np.concatenate(list(parts.values()), axis=1)), at


def selector():
    return np.repeat(np.eye(4, dtype=np.float32), LAT, axis=1)


def vector_rows():
    rows, at = [], {}

    def put(name, source, n, width=P, layer=None, off=0):
        at[name] = sum(r[2] for r in rows)
        rows.append((source, layer, n, width, off))

    put("c", "c", 8)
    put("c_ctx", "c_ctx", 8)
    for l in (0, 1):
        put(f"mod_b{l}", f"l{l}_mod_b", 72)
        for m in ("ffn1", "mix", "ffn2"):
            put(f"{m}_{l}", f"l{l}_{m}_norm", 8)
    put("q_norm", "l0_mla_q_norm", 3)
    put("kv_norm", "l0_mla_kv_norm", 2)
    put("mla_q", "l0_mla_q_gain", 1, HD + MLA_ROPE)
    put("mla_k", "l0_mla_k_gain", 1, HD + MLA_ROPE)
    put("glu_b", "l0_conv_glu_b", 8)
    put("dw_b", "l0_conv_dw_b", 4)
    put("ln_g", "l0_conv_ln_g", 4)
    put("ln_b", "l0_conv_ln_b", 4)
    put("dw_w", "l0_conv_dw_w", CONV_W * 4)
    for g in ("gqa_q", "gqa_k", "na_q", "na_k"):
        put(g, f"l1_{g}_gain", 1, 64)
    for l in (0, 1):
        for m in ("ffn1", "mix", "ffn2"):
            put(f"{m}_b{l}", f"{m}_norm_2", 8, layer=l)
        put(f"gate_b{l}", "b_gate_2", 32, layer=l)
        put(f"diff{l}", "diff_gain_2", 1, layer=l)
        put(f"fgt{l}", "b_fgt_2", 1, 4, layer=l)
    put("final", "final_norm_2", 8)
    return rows, at



def by_chunk(w):
    return w.rearrange("(k p) n -> p k n", p=P)


def pair_tiles(slot):
    return slot[:, 0:2 * KD * P].rearrange("p (t k c) -> p t k c", t=2, k=KD)


def wide_tile(slot):
    return slot[:, 0:KD * 2 * P].rearrange("p (k c) -> p k c", k=KD)


def tall_tile(slot):
    return slot[:, 0:SLOT].rearrange("p (k c) -> p k c", k=KF)


def cols(start, n):
    return slice(start, start + n) if isinstance(start, int) else bass.ds(start, n)


def weight_plan(w):
    plan = []

    def add(name, n, load, dmas=1, looped=True):
        plan.append(Product(name, n, load, looped, dmas if isinstance(dmas, list) else [dmas] * n))

    def wide(name, mat, n, first=0):
        m = by_chunk(mat)
        add(name, n, lambda slot, i, c: [(wide_tile(slot), m[:, :, cols(i * (RING * 256) + (first + c * 256), 256)])])

    def ffn(name, layer, mat_in, mat_out):
        m, o = by_chunk(mat_in), by_chunk(mat_out)
        kh = KF // 2
        for half, tag in enumerate("ab"):
            at = half * kh
            add(f"{name}_in{tag}{layer}", kh, lambda slot, i, c, at=at: [
                (pair_tiles(slot)[:, t], m[:, :, cols(i * (RING * P) + (t * FF + (at + c) * P), P)]) for t in (0, 1)], 2)
            add(f"{name}_out{tag}{layer}", KD, lambda slot, i, c, at=at: [
                (tall_tile(slot)[:, a:b, :], o[:, at + a:at + b, cols(i * (RING * P) + c * P, P)])
                for a, b in ((0, kh // 2), (kh // 2, kh))], 2)

    def listed(name, mat, units):
        m = by_chunk(mat)
        add(name, len(units), lambda slot, i, c: [(dst(slot), m[:, :, at:at + n]) for dst, at, n in units[c]],
            [len(u) for u in units], looped=False)

    def whole(slot, n=256):
        return wide_tile(slot)[:, :, 0:n]

    def tile(t, n=P):
        return lambda slot: pair_tiles(slot)[:, t, :, 0:n]

    for l in (0, 1):
        wide(f"mod{l}", w[f"l{l}_mod_w"], N_MOD * D // 256)
        ffn("ffn1", l, w[f"l{l}_ffn1_w_in"], w[f"l{l}_ffn1_w_out"])
        if l == 0:
            units = [[(tile(0), 672 + P * c, P), (tile(1), 1184 + P * c, P)] for c in range(4)]
            units += [[(whole, 0, 256)], [(whole, 288, 256)], [(tile(0), 544, 128), (tile(1, 32), 256, 32)]]
            listed("in0", w["l0_w_in"], units)
            uq = by_chunk(w["l0_mla_w_uq"])
            heads = w["l0_mla_w_ukv"].rearrange("(k p) (h e) -> p k h e", p=P, h=HEADS)

            def latents_out(slot, i, c):
                if c == 1:
                    return [(slot[:, 0:2304].rearrange("p (k n) -> p k n", k=3), uq)]
                return [(slot[:, (2 * part + kc) * 512:(2 * part + kc + 1) * 512].rearrange("p (h e) -> p h e", h=HEADS),
                         heads[:, kc, :, part * HD:(part + 1) * HD]) for part in range(2) for kc in range(2)]

            add("heads0", 2, latents_out, [4, 1], looped=False)
        else:
            wide("in1", w["l1_w_in"], 9)
        wide(f"out{l}", w[f"l{l}_w_out"], 4)
        ffn("ffn2", l, w[f"l{l}_ffn2_w_in"], w[f"l{l}_ffn2_w_out"])
    for l in (0, 1):
        ffn("ffn1", f"_b{l}", w["ffn1_w_gu_2"][l], w["ffn1_w_down_2"][l])
        order = list(QK_COLUMNS) + list(V_COLUMNS)
        units = [[(whole, c, 256)] for c in order]
        units += [[(lambda slot: whole(slot, 72), 4356, 72), (lambda slot: wide_tile(slot)[:, :, 72:76], 2304, 4)]]
        listed(f"in_b{l}", w["w_in_2"][l], units)
        gates = w["w_gate_2"][l].rearrange("(k p) (b n) -> p b k n", p=P, b=4)
        br = {n: by_chunk(w[f"w_br_{n}_2"][l]) for n in "abcd"}

        def merge(slot, i, c, gates=gates, br=br):
            n = cols(i * (RING // 2 * P) + c // 2 * P, P)
            two = ((0, "a", 16, 4), (3, "d", 20, 2)) if c % 2 == 0 else ((1, "b", 16, 2), (2, "c", 18, 2))
            out = []
            for t, (gate, name, row, rows) in enumerate(two):
                out.append((tall_tile(slot)[:, t * KD:(t + 1) * KD, :], gates[:, gate, :, n]))
                out.append((tall_tile(slot)[:, row:row + rows, :], br[name][:, :, n]))
            return out

        add(f"merge_b{l}", 16, merge, 4)
        wide(f"out_b{l}", w["w_out_2"][l], 4)
        ffn("ffn2", f"_b{l}", w["ffn2_w_gu_2"][l], w["ffn2_w_down_2"][l])
    start = 0
    raised = [0] * RING
    for spec in plan:
        spec.start = start
        spec.ready = []
        for j in range(spec.n):
            slot = (start + j) % RING
            raised[slot] += 16 * spec.dmas[j]
            spec.ready.append(raised[slot])
        start += spec.n
    return plan


def each_unit(engine, first, last, body, looped=True):
    full = (last - first) // RING if looped else 0
    if full > 1:
        with engine.Fori(0, full) as i:
            for s in range(RING):
                body(i, first + s)
    elif full == 1:
        for s in range(RING):
            body(0, first + s)
    for c in range(first + full * RING, last):
        body(0, c)


def load_weights(k, sp, first, last):
    for spec in k.plan:
        a, b = max(first, spec.start) - spec.start, min(last, spec.start + spec.n) - spec.start
        if a >= b:
            continue

        def unit(i, c, spec=spec):
            slot = (spec.start + c) % RING
            if first > 0:
                sp.wait_ge(k.unit_done, i * RING + (spec.start + c - RING + 1))
            for dst, src in spec.load(k.slots[slot], i, c):
                sp.dma_start(dst, src).then_inc(k.weights_ready[slot], 16)

        each_unit(sp, a, b, unit, spec.looped)


def wait_weights(k, pe, spec, i, c):
    slot = (spec.start + c) % RING
    pe.wait_ge(k.weights_ready[slot], i * (16 * spec.dmas[c]) + spec.ready[c])
    pe.wait_ge(k.banks_free, i * RING + (spec.start + c + 1))
    return slot


def wait_product(k, engine, spec, i, c):
    engine.wait_ge(k.unit_done, i * RING + (spec.start + c + 1))
    return (spec.start + c) % RING


def stream_ahead(k, block, spec):
    total = k.plan[-1].start + k.plan[-1].n

    @block.sync
    def _(sp):
        load_weights(k, sp, spec.start + RING, min(spec.start + spec.n + RING, total))



def halves(tokens):
    return [(0, slice(0, LAT)), (1, slice(LAT, TOK))][: tokens // LAT]


def one(t, h, rows=slice(None), col=slice(None)):
    if isinstance(h, int):
        return t[rows, h, col]
    return t[rows, bass.ds(h, 1), col].rearrange("p o n -> p (o n)")


def column(t, n, rows=slice(None)):
    return t[rows, cols(n, 1)]


def square_buffers(k, tokens):
    T = slice(0, tokens)
    return k.square[:, 0, T], [k.square[:, 1, T], k.rinvs[:, 1, T]]


def square_chunk(k, act, tokens, n):
    squared, summed = k.tally("x_squared"), k.tally("x_summed")
    total, buffers = square_buffers(k, tokens)
    if n >= 3:
        act.wait_ge(summed.sem, summed.base + n - 2)
    k.nc.scalar.activation(total if n == 0 else buffers[n % 2], k.x[:, n, 0:tokens], ACT.Square).then_inc(squared.sem, 1)


def sum_squares(k, block, tokens):
    squared, summed = k.tally("x_squared"), k.tally("x_summed")
    total, buffers = square_buffers(k, tokens)
    first, done = squared.base, summed.base

    @block.gpsimd
    def _(pool):
        for n in range(1, KD):
            pool.wait_ge(squared.sem, first + n + 1)
            if n > 1:
                pool.wait_ge(summed.sem, done + n - 1)
            k.nc.gpsimd.tensor_tensor(total, total, buffers[n % 2], ALU.add).then_inc(summed.sem, 1)


def close_squares(k):
    k.tally("x_squared").close(KD)
    k.tally("x_summed").close(KD - 1)


WIDE = 2 * KD * P
PASSES = ((0, 0), (0, 1), (1, 0))


def part_buffers(k, sb, depth):
    k.parts = [[sb(f"weights_part{n}_{d}", [P, WIDE]) for n in range(2)] for d in range(depth)]


def scoped(k, dt):
    stack = ExitStack()
    k.scope += 1
    scope = k.scope

    def sb(name, shape, dt=dt):
        return stack.enter_context(k.nc.sbuf_tensor(f"{name}_{scope}", shape, dt))[(slice(None),) * len(shape)]

    return stack, sb


def weight_parts(k, specs, depth):
    nc, first, total = k.nc, specs[0].start, sum(s.n for s in specs)
    per_unit = 16 * specs[0].dmas[0]
    ready = [r for s in specs for r in s.ready]
    high, low = k.tally("high_done"), k.tally("split_done")
    high_before, low_before = high.base, low.base

    def split_high(act, i, q):
        if q >= total:
            return
        slot, part = (first + q) % RING, (first + q) % depth
        act.wait_ge(k.weights_ready[slot], i * per_unit + ready[q])
        if first + q >= depth:
            act.wait_ge(k.unit_done, i * RING + (first + q - depth + 1))
        nc.scalar.activation(k.parts[part][0][:, :], k.slots[slot][:, 0:WIDE], ACT.Copy).then_inc(high.sem, 1)

    def split_low(dve, i, q):
        if q >= total:
            return
        slot, part = (first + q) % RING, (first + q) % depth
        dve.wait_ge(high.sem, i * RING + (high_before + q + 1))
        nc.vector.tensor_tensor(k.parts[part][1][:, :], k.slots[slot][:, 0:WIDE], k.parts[part][0][:, :].bitcast(F32),
                                ALU.subtract).then_inc(low.sem, 1)

    def wait_parts(pe, i, q):
        pe.wait_ge(low.sem, i * RING + (low_before + q + 1))
        pe.wait_ge(k.banks_free, i * RING + (first + q + 1))
        return (first + q) % RING, k.parts[(first + q) % depth]

    high.close(total), low.close(total)
    return split_high, split_low, wait_parts


def product_of_parts(k, to, left, right, first, last):
    for n, (a, b) in enumerate(PASSES):
        mm = k.nc.tensor.matmul(to, left[a], right[b], start=first and n == 0, stop=last and n == len(PASSES) - 1)
    return mm


def norm_tokens(k, tokens, gain, shift=None, dst=None, parts=None, splits=None):
    x, dst = k.x, k.h if dst is None else dst
    mean, root, scaled, high = (k.tally(n) for n in ("mean_done", "root_done", "scaled", "normed_high"))
    T = slice(0, tokens)
    with k.nc.Block() as block:
        @block.scalar
        def _(act):
            if splits is not None:
                splits[0](act, 0, 0)
            act.wait_ge(mean.sem, mean.base + 1)
            k.nc.scalar.activation(k.root[:, T], k.psum[:, 0, T], ACT.Sqrt, bias=k.eps[:, 0:1],
                                   scale=1.0 / D).then_inc(root.sem, 1)
            if shift is not None:
                for c in range(KD):
                    for cond, part in halves(tokens):
                        act.wait_ge(scaled.sem, scaled.base + 2 + c)
                        k.nc.scalar.activation(dst[:, c, part], dst[:, c, part], ACT.Identity,
                                               bias=shift(c, cond), scale=gain(c, cond))
            if parts is not None:
                for c in range(KD):
                    act.wait_ge(scaled.sem, scaled.base + 2 + c)
                    k.nc.scalar.activation(parts[0][:, c, T], dst[:, c, T], ACT.Copy).then_inc(high.sem, 1)

        @block.tensor
        def _(pe):
            k.nc.tensor.matmul(k.psum[:, 0, T], k.const("ones"), k.square[:, 0, T], start=True, stop=True)\
                .then_inc(mean.sem, 1)

        @block.vector
        def _(dve):
            if splits is not None:
                splits[1](dve, 0, 0)
            dve.wait_ge(root.sem, root.base + 1)
            k.nc.vector.reciprocal(k.rinv[:, T], k.root[:, T]).then_inc(scaled.sem, 1)
            dve.wait_ge(scaled.sem, scaled.base + 1)
            for c in range(KD):
                if shift is None:
                    k.nc.vector.scalar_tensor_tensor(dst[:, c, T], x[:, c, T], gain(c, 0), k.rinv[:, T],
                                                     ALU.mult, ALU.mult).then_inc(scaled.sem, 1)
                else:
                    k.nc.vector.tensor_tensor(dst[:, c, T], x[:, c, T], k.rinv[:, T], ALU.mult).then_inc(scaled.sem, 1)
            if parts is not None:
                for c in range(KD):
                    dve.wait_ge(high.sem, high.base + c + 1)
                    k.nc.vector.tensor_tensor(parts[1][:, c, T], dst[:, c, T], parts[0][:, c, T].bitcast(F32), ALU.subtract)
    for t, n in ((mean, 1), (root, 1), (scaled, 1 + KD), (high, KD if parts is not None else 0)):
        t.close(n)


def add_product_of_parts(k, spec, tokens, source, parts, gate=None, splits=None, before=0):
    nc, T = k.nc, slice(0, tokens)
    high, low = k.tally("source_high"), k.tally("source_low")
    split_high, split_low, wait_parts = splits or weight_parts(k, [spec], 2)
    ready = 0 if splits is None else 2
    with nc.Block() as block:
        stream_ahead(k, block, spec)
        sum_squares(k, block, tokens)

        @block.scalar
        def _(act):
            for c in range(ready, 1):
                split_high(act, 0, before + c)
            for c in range(KD):
                nc.scalar.activation(parts[0][:, c, T], source[:, c, T], ACT.Copy).then_inc(high.sem, 1)
            for c in range(max(ready, 1), 2):
                split_high(act, 0, before + c)
            for c in range(spec.n):
                split_high(act, 0, before + c + 2)
                act.wait_ge(k.banks_free, spec.start + c + 1 + RING)
                for t in range(2):
                    square_chunk(k, act, tokens, c * 2 + t)

        @block.tensor
        def _(pe):
            for c in range(spec.n):
                slot, weights = wait_parts(pe, 0, before + c)
                for t in range(2):
                    for kc in range(KD):
                        if (c, t) == (0, 0):
                            pe.wait_ge(low.sem, low.base + kc + 1)
                        mm = product_of_parts(k, k.psum[:, 2 * slot + t, T], [wide_lhs(w, kc, t) for w in weights],
                                              [p[:, kc, T] for p in parts], kc == 0, kc == KD - 1)
                mm.then_inc(k.unit_done, 1)

        @block.vector
        def _(dve):
            for c in range(ready, 1):
                split_low(dve, 0, before + c)
            for c in range(KD):
                dve.wait_ge(high.sem, high.base + c + 1)
                nc.vector.tensor_tensor(parts[1][:, c, T], source[:, c, T], parts[0][:, c, T].bitcast(F32), ALU.subtract)\
                    .then_inc(low.sem, 1)
            for c in range(max(ready, 1), 2):
                split_low(dve, 0, before + c)
            for c in range(spec.n):
                split_low(dve, 0, before + c + 2)
                slot = wait_product(k, dve, spec, 0, c)
                for t in range(2):
                    for cond, part in (halves(tokens) if gate is not None else [(0, T)]):
                        row, product = k.x[:, c * 2 + t, part], k.psum[:, 2 * slot + t, part]
                        if gate is None:
                            last = nc.vector.tensor_tensor(row, row, product, ALU.add)
                        else:
                            last = nc.vector.scalar_tensor_tensor(row, product, gate(c * 2 + t, cond), row, ALU.mult, ALU.add)
                last.then_inc(k.banks_free, 1)
    high.close(KD), low.close(KD)
    close_squares(k)


def wide_lhs(slot, kc, t):
    return wide_tile(slot)[:, kc, t * P:(t + 1) * P]


def norm_heads(k, src, rows, groups, n, mean, gain, scale=1.0, eps=None):
    squared, mean_done, root, inv, normed = (k.tally(t) for t in ("squared", "mean_done", "root_done", "inverse_done", "normed"))
    R, N = slice(0, rows), slice(0, n)
    eps = k.eps if eps is None else eps
    with k.nc.Block() as block:
        @block.scalar
        def _(act):
            act.sem_inc(inv.sem, 2)
            with act.Fori(0, groups // 2) as i:
                for u in range(2):
                    k.nc.scalar.activation(k.square[R, u, N], one(src, i * 2 + u, R, N), ACT.Square).then_inc(squared.sem, 1)
                for u in range(2):
                    act.wait_ge(mean_done.sem, i * 2 + (mean_done.base + u + 1))
                    act.wait_ge(inv.sem, i * 2 + (inv.base + u + 1))
                    k.nc.scalar.activation(k.roots[R, u, N], k.psum[R, u, N], ACT.Sqrt, bias=eps[R, 0:1], scale=scale)\
                        .then_inc(root.sem, 1)

        @block.tensor
        def _(pe):
            with pe.Fori(0, groups // 2) as i:
                for u in range(2):
                    pe.wait_ge(squared.sem, i * 2 + (squared.base + u + 1))
                    k.nc.tensor.matmul(k.psum[:, u, N], mean, k.square[R, u, N], start=True, stop=True)\
                        .then_inc(mean_done.sem, 1)

        @block.vector
        def _(dve):
            with dve.Fori(0, groups // 2) as i:
                for u in range(2):
                    dve.wait_ge(root.sem, i * 2 + (root.base + u + 1))
                    k.nc.vector.reciprocal(k.rinvs[R, u, N], k.roots[R, u, N]).then_inc(inv.sem, 1)
                    dve.wait_ge(inv.sem, i * 2 + (inv.base + 2 + u + 1))
                    row = one(src, i * 2 + u, R, N)
                    k.nc.vector.scalar_tensor_tensor(row, row, gain, k.rinvs[R, u, N], ALU.mult, ALU.mult)\
                        .then_inc(normed.sem, 1)
    for t, n in ((squared, groups), (mean_done, groups), (root, groups), (inv, groups + 2), (normed, groups)):
        t.close(n)


def norm_all_heads(k, jobs):
    nc = k.nc
    t = {n: k.tally("heads_" + n) for n in ("squared", "summed", "root_done", "inverse_done", "spread_ready", "spread", "normed")}
    groups = [(src[:, g, :], column(k.vec, k.vec_at[gain])) for src, n, gain in jobs for g in range(n)]
    n_groups, n_banks = len(groups), 7
    flat = k.h[:, :, :].rearrange("p a b -> p (a b)")
    spread = flat[:, 0:2 * n_groups * HD]
    with nc.Block() as block:
        @block.gpsimd
        def _(pool):
            nc.gpsimd.tensor_copy(spread.rearrange("p (r c) -> p r c", c=HD),
                                  k.const("ident")[:, 0:2 * n_groups].unsqueeze(2).broadcast_to([P, 2 * n_groups, HD]))\
                .then_inc(t["spread_ready"].sem, 1)

        @block.scalar
        def _(act):
            for g, (row, _) in enumerate(groups):
                if g >= 2:
                    act.wait_ge(t["summed"].sem, t["summed"].base + g - 1)
                nc.scalar.activation(k.square[:, g % 2, :], row, ACT.Square).then_inc(t["squared"].sem, 1)
            act.wait_ge(t["summed"].sem, t["summed"].base + n_groups)
            nc.scalar.activation(k.roots[:, 0, :], k.psum[:, 0, :], ACT.Sqrt, bias=k.eps[:, 0:1]).then_inc(t["root_done"].sem, 1)

        @block.tensor
        def _(pe):
            for g in range(n_groups):
                pe.wait_ge(t["squared"].sem, t["squared"].base + g + 1)
                at = P - 1 - 2 * g
                nc.tensor.matmul(k.psum[:, 0, :], k.const("means")[:, at:at + P], k.square[:, g % 2, :], start=g == 0,
                                 stop=g == n_groups - 1).then_inc(t["summed"].sem, 1)
            pe.wait_ge(t["spread_ready"].sem, t["spread_ready"].base + 1)
            pe.wait_ge(t["inverse_done"].sem, t["inverse_done"].base + 1)
            for g in range(n_groups):
                if g >= n_banks:
                    pe.wait_ge(t["normed"].sem, t["normed"].base + g - n_banks + 1)
                nc.tensor.matmul(k.psum[:, 1 + g % n_banks, :], spread[:, g * P:(g + 1) * P], k.rinvs[:, 0, :], start=True,
                                 stop=True).then_inc(t["spread"].sem, 1)

        @block.vector
        def _(dve):
            dve.wait_ge(t["root_done"].sem, t["root_done"].base + 1)
            nc.vector.reciprocal(k.rinvs[:, 0, :], k.roots[:, 0, :]).then_inc(t["inverse_done"].sem, 1)
            for g, (row, gain) in enumerate(groups):
                dve.wait_ge(t["spread"].sem, t["spread"].base + g + 1)
                nc.vector.scalar_tensor_tensor(row, row, gain, k.psum[:, 1 + g % n_banks, :], ALU.mult, ALU.mult)\
                    .then_inc(t["normed"].sem, 1)
    for name, n in dict(squared=n_groups, summed=n_groups, root_done=1, inverse_done=1, spread_ready=1, spread=n_groups,
                        normed=n_groups).items():
        t[name].close(n)


def rotate_heads(k, src, rows, groups, turn, cos, sin):
    turned, by_cos, by_sin, rotated = (k.tally(t) for t in ("turned", "by_cos", "by_sin", "rotated"))
    R, N = slice(0, rows), slice(0, LAT)
    steps = (groups + 1) // 2

    def operands(i, u, n):
        rows_ = src[R, cols(i * 2, n), N]
        bank, product = (t[R, u, 0:n * LAT].rearrange("p (g t) -> p g t", g=n) for t in (k.psum, k.square))
        return rows_, bank, product, *(t.unsqueeze(1).broadcast_to([rows, n, LAT]) for t in (cos, sin))

    def each_step(engine, body):
        full = groups // 2
        if full > 1:
            with engine.Fori(0, full // 2) as i:
                for u in range(2):
                    body(i * 2 + u, u, 2)
        if full % 2:
            body(full - 1, 0, 2)
        if groups % 2:
            body(full, full % 2, 1)

    with k.nc.Block() as block:
        @block.tensor
        def _(pe):
            pe.sem_inc(by_sin.sem, 2)

            def step(i, u, n):
                pe.wait_ge(by_sin.sem, i + (by_sin.base + 1))
                for g in range(n):
                    mm = k.nc.tensor.matmul(k.psum[:, u, g * LAT:(g + 1) * LAT], turn, one(src, i * 2 + g, R, N),
                                            start=True, stop=True)
                mm.then_inc(turned.sem, 1)
            each_step(pe, step)

        @block.gpsimd
        def _(pool):
            def step(i, u, n):
                x, _, _, c, _ = operands(i, u, n)
                pool.wait_ge(turned.sem, i + (turned.base + 1))
                k.nc.gpsimd.tensor_tensor(x, x, c, ALU.mult).then_inc(by_cos.sem, 1)
            each_step(pool, step)

        @block.vector
        def _(dve):
            def step(i, u, n):
                x, bank, product, _, s = operands(i, u, n)
                dve.wait_ge(turned.sem, i + (turned.base + 1))
                k.nc.vector.tensor_tensor(product, bank, s, ALU.mult).then_inc(by_sin.sem, 1)
                dve.wait_ge(by_sin.sem, i + (by_sin.base + 3))
                dve.wait_ge(by_cos.sem, i + (by_cos.base + 1))
                k.nc.vector.tensor_tensor(x, x, product, ALU.add).then_inc(rotated.sem, 1)
            each_step(dve, step)
    for t, n in ((turned, steps), (by_cos, steps), (by_sin, steps + 2), (rotated, steps)):
        t.close(n)


def attention(k, pairs, key_tiles, staging, score, value, width, dst, difference=None):
    nc, J = k.nc, 4
    keys = key_tiles * P
    steps = 1 if difference is None else 2
    t = {n: k.tally(n) for n in (
        "staged", "scored", "maxed", "exp_done", "probs_turned", "even_copied", "odd_copied", "weighted",
        "sums_inverted", "out_normed", "out_turned", "out_placed")}
    S = [k.psum[:, j, 0:keys] for j in range(J)]
    PT = [k.psum[:, 4 + u, 0:keys] for u in range(2)]
    O = [k.psum[:, 6, j * width:(j + 1) * width] for j in range(J)]
    OT = k.psum[:, 7, 0:2 * P]
    jobs = [(j, j // 2, j % 2) for j in range(J)]
    prob = [k.prob(j, keys) for j in range(J)]
    prob_t = [k.prob_t(u, keys) for u in range(2)]
    with nc.Block() as block:
        @block.gpsimd
        def _(pool):
            with pool.Fori(0, pairs) as b:
                copies = staging(b)
                for n, (to, of) in enumerate(copies):
                    last = nc.gpsimd.tensor_copy(to, of)
                last.then_inc(t["staged"].sem, 1)
                pool.wait_ge(t["scored"].sem, b * J + (t["scored"].base + J))

        @block.tensor
        def _(pe):
            pe.sem_inc(t["out_placed"].sem, 1)

            def weigh(b, j, hh):
                copied = t["even_copied"] if j % 2 == 0 else t["odd_copied"]
                pe.wait_ge(copied.sem, b * (J // 2) + (copied.base + j // 2 + 1))
                for kt in range(key_tiles):
                    mm = nc.tensor.matmul(O[j], prob_t[j % 2][:, kt * P:(kt + 1) * P], value(b, hh, kt),
                                          start=kt == 0, stop=kt == key_tiles - 1)
                mm.then_inc(t["weighted"].sem, 1)

            def form_logits(b, some):
                for j, hh, qt in some:
                    score(S[j], b, hh, qt).then_inc(t["scored"].sem, 1)

            def round_of(b, more):
                for j, hh, qt in jobs:
                    pe.wait_ge(t["exp_done"].sem, b * J + (t["exp_done"].base + j + 1))
                    for kt in range(key_tiles):
                        mm = nc.tensor.transpose(PT[j % 2][:, kt * P:(kt + 1) * P], prob[j][:, kt * P:(kt + 1) * P],
                                                 k.const("ident"))
                    mm.then_inc(t["probs_turned"].sem, 1)
                    if j >= 1:
                        weigh(b, j - 1, (j - 1) // 2)
                weigh(b, J - 1, 1)
                if more:
                    pe.wait_ge(t["staged"].sem, b + (t["staged"].base + 2))
                    form_logits(b + 1, jobs[:2])
                pe.wait_ge(t["out_normed"].sem, b * J + (t["out_normed"].base + J))
                pe.wait_ge(t["out_placed"].sem, b + (t["out_placed"].base + 1))
                for qt in range(2):
                    mm = nc.tensor.transpose(OT[:, qt * P:(qt + 1) * P], k.out_rows[:, qt, :], k.const("ident"))
                mm.then_inc(t["out_turned"].sem, 1)
                if more:
                    form_logits(b + 1, jobs[2:])

            pe.wait_ge(t["staged"].sem, t["staged"].base + 1)
            form_logits(0, jobs)
            if pairs > 2:
                with pe.Fori(0, pairs - 1) as b:
                    round_of(b, True)
            else:
                round_of(0, True)
            round_of(pairs - 1, False)

        @block.vector
        def _(dve):
            dve.sem_inc(t["out_turned"].sem, 1)
            with dve.Fori(0, pairs) as b:
                for j, hh, qt in jobs:
                    dve.wait_ge(t["scored"].sem, b * J + (t["scored"].base + j + 1))
                    nc.vector.tensor_reduce(k.negmax[:, j:j + 1], S[j], AX.X, ALU.max, negate=True).then_inc(t["maxed"].sem, 1)
                for j in (0, 2):
                    dve.wait_ge(t["probs_turned"].sem, b * J + (t["probs_turned"].base + j + 1))
                    if j == 2:
                        dve.wait_ge(t["weighted"].sem, b * J + (t["weighted"].base + 1))
                    nc.vector.tensor_copy(prob_t[0], PT[0]).then_inc(t["even_copied"].sem, 1)
                dve.wait_ge(t["exp_done"].sem, b * J + (t["exp_done"].base + J))
                inverse = nc.vector.reciprocal(k.inverse[:, 0:J], k.rowsum[:, 0:J])
                inverse.then_inc(t["sums_inverted"].sem, 1)
                dve.wait_ge(t["sums_inverted"].sem, b * steps + (t["sums_inverted"].base + 1))
                if difference is not None:
                    nc.vector.tensor_scalar(k.inverse[:, J:J + 2], k.inverse[:, 2:4], difference, None, ALU.mult)\
                        .then_inc(t["sums_inverted"].sem, 1)
                    dve.wait_ge(t["sums_inverted"].sem, b * steps + (t["sums_inverted"].base + 2))
                dve.wait_ge(t["out_turned"].sem, b + (t["out_turned"].base + 1))
                dve.wait_ge(t["weighted"].sem, b * J + (t["weighted"].base + J))
                for j, hh, qt in jobs:
                    if difference is None:
                        nc.vector.tensor_scalar(k.out_rows[:, qt, hh * width:(hh + 1) * width], O[j],
                                                k.inverse[:, j:j + 1], None, ALU.mult).then_inc(t["out_normed"].sem, 1)
                    elif hh == 0:
                        nc.vector.tensor_scalar(k.out_rows[:, qt, :], O[j], k.inverse[:, j:j + 1], None, ALU.mult)\
                            .then_inc(t["out_normed"].sem, 1)
                    else:
                        dve.wait_ge(t["out_normed"].sem, b * J + (t["out_normed"].base + j - 1))
                        nc.vector.scalar_tensor_tensor(k.out_rows[:, qt, :], O[j], k.inverse[:, J + qt:J + qt + 1],
                                                       k.out_rows[:, qt, :], ALU.mult, ALU.add).then_inc(t["out_normed"].sem, 1)

        @block.scalar
        def _(act):
            with act.Fori(0, pairs) as b:
                for j, hh, qt in jobs:
                    act.wait_ge(t["maxed"].sem, b * J + (t["maxed"].base + j + 1))
                    nc.scalar.activation(prob[j], S[j], ACT.Exp, bias=k.negmax[:, j:j + 1],
                                         accum_out=k.rowsum[:, j:j + 1]).then_inc(t["exp_done"].sem, 1)
                for j in (1, 3):
                    act.wait_ge(t["probs_turned"].sem, b * J + (t["probs_turned"].base + j + 1))
                    if j == 3:
                        act.wait_ge(t["weighted"].sem, b * J + (t["weighted"].base + 2))
                    nc.scalar.activation(prob_t[1], PT[1], ACT.Copy).then_inc(t["odd_copied"].sem, 1)
                act.wait_ge(t["out_turned"].sem, b + (t["out_turned"].base + 2))
                nc.scalar.activation(dst(b), OT, ACT.Copy).then_inc(t["out_placed"].sem, 1)
    for name, n in dict(staged=1, scored=J, maxed=J, exp_done=J, probs_turned=J, even_copied=2, odd_copied=2, weighted=J,
                        sums_inverted=steps, out_normed=J, out_turned=1, out_placed=1).items():
        t[name].close(n * pairs)
    t["out_turned"].close(1)
    t["out_placed"].close(1)



KH = KF // 2

def ffn_buffers(k, tokens, depth):
    stack, sb = scoped(k, F32R)
    k.normed = [sb(f"normed{n}", [P, KD, tokens]) for n in range(2)]
    k.hidden = [sb(f"hidden{n}", [P, KH, tokens]) for n in range(2)]
    part_buffers(k, sb, depth)
    k.rows = [k.roots[:, 1, 0:tokens], k.rinvs[:, 1, 0:tokens]]
    return stack


def half_ffn(k, tokens, name, layer, gain, shift, gate):
    nc, T = k.nc, slice(0, tokens)
    depth = 2 if tokens == TOK else 4
    specs = [k.spec(f"{name}_{part}{half}{layer}") for half in "ab" for part in ("in", "out")]
    first, total = specs[0].start, sum(s.n for s in specs)
    t = {n: k.tally("ffn_" + n) for n in ("summed", "root_done", "inverse_done", "scaled", "shifted", "normed",
                                          "silu_done", "gated", "hidden_high")}
    parts_of_tokens = halves(tokens) if shift is not None else [(0, T)]

    def at(spec, c):
        return spec.start - first + c

    split_high, split_low, wait_parts = weight_parts(k, specs, depth)
    with ffn_buffers(k, tokens, depth), nc.Block() as block:
        total_units = k.plan[-1].start + k.plan[-1].n
        sum_squares(k, block, tokens)

        @block.sync
        def _(sp):
            load_weights(k, sp, first + RING, min(first + total + RING, total_units))

        @block.scalar
        def _(act):
            split_high(act, 0, 0)
            act.wait_ge(t["summed"].sem, t["summed"].base + 1)
            nc.scalar.activation(k.root[:, T], k.psum[:, 0, T], ACT.Sqrt, bias=k.eps[:, 0:1], scale=1.0 / D)\
                .then_inc(t["root_done"].sem, 1)
            split_high(act, 0, 1)
            for c in range(KD):
                act.wait_ge(t["scaled"].sem, t["scaled"].base + c + 1)
                for cond, part in parts_of_tokens:
                    if shift is None:
                        last = nc.scalar.activation(k.normed[0][:, c, part], k.rows[c % 2][:, part], ACT.Copy)
                    else:
                        last = nc.scalar.activation(k.normed[0][:, c, part], k.rows[c % 2][:, part], ACT.Identity,
                                                    bias=shift(c, cond))
                last.then_inc(t["shifted"].sem, 1)
            for q in range(2, depth):
                split_high(act, 0, q)
            for s, spec in enumerate(specs):
                def unit_in(i, c, spec=spec, half=s // 2):
                    slot = wait_product(k, act, spec, i, c)
                    row, n = k.rows[(half * KH + c) % 2], half * KH + c + 1
                    act.wait_ge(k.banks_free, i * RING + (spec.start + c + RING - 1))
                    nc.scalar.activation(row[:, T], k.psum[:, 2 * slot, T], ACT.Silu).then_inc(t["silu_done"].sem, 1)
                    act.wait_ge(t["gated"].sem, i * RING + (t["gated"].base + n))
                    nc.scalar.activation(one(k.hidden[0], i * RING + c, col=T), row[:, T], ACT.Copy)\
                        .then_inc(t["hidden_high"].sem, 1)
                    split_high(act, i, at(spec, c) + depth)

                def unit_out(i, c, spec=spec, last=s == len(specs) - 1):
                    split_high(act, i, at(spec, c) + depth)
                    if last:
                        act.wait_ge(k.banks_free, spec.start + c + 1 + RING)
                        square_chunk(k, act, tokens, c)

                each_unit(act, 0, spec.n, unit_in if s % 2 == 0 else unit_out, s < len(specs) - 1)

        @block.tensor
        def _(pe):
            nc.tensor.matmul(k.psum[:, 0, T], k.const("ones"), k.square[:, 0, T], start=True, stop=True)\
                .then_inc(t["summed"].sem, 1)

            for s, spec in enumerate(specs):
                def unit_in(i, c, spec=spec, first_unit=False):
                    slot, parts = wait_parts(pe, i, at(spec, c))
                    tiles = [(tile, kc) for tile in range(2) for kc in range(KD)]
                    if first_unit:
                        tiles = [(tile, kc) for kc in range(KD) for tile in range(2)]
                    for tile, kc in tiles:
                        if first_unit and tile == 0:
                            pe.wait_ge(t["normed"].sem, t["normed"].base + kc + 1)
                        mm = product_of_parts(k, k.psum[:, 2 * slot + tile, T], [pair_tiles(w)[:, tile, kc] for w in parts],
                                              [x[:, kc, T] for x in k.normed], kc == 0, kc == KD - 1)
                    mm.then_inc(k.unit_done, 1)

                def unit_out(i, c, spec=spec):
                    slot, parts = wait_parts(pe, i, at(spec, c))
                    for kc in range(KH):
                        if c == 0:
                            pe.wait_ge(k.banks_free, spec.start - KH + kc + 1 + RING)
                        mm = product_of_parts(k, k.psum[:, 2 * slot, T], [w[:, kc * P:(kc + 1) * P] for w in parts],
                                              [x[:, kc, T] for x in k.hidden], kc == 0, kc == KH - 1)
                    mm.then_inc(k.unit_done, 1)

                if s == 0:
                    unit_in(0, 0, first_unit=True)
                    each_unit(pe, 1, 3, unit_in)
                    each_unit(pe, 3, spec.n, unit_in)
                elif s % 2 == 0:
                    each_unit(pe, 0, spec.n, unit_in)
                else:
                    each_unit(pe, 0, spec.n, unit_out, s < len(specs) - 1)

        @block.vector
        def _(dve):
            split_low(dve, 0, 0)
            dve.wait_ge(t["root_done"].sem, t["root_done"].base + 1)
            nc.vector.reciprocal(k.rinv[:, T], k.root[:, T]).then_inc(t["inverse_done"].sem, 1)
            dve.wait_ge(t["inverse_done"].sem, t["inverse_done"].base + 1)

            def scale(c):
                if c >= 2:
                    dve.wait_ge(t["normed"].sem, t["normed"].base + c - 1)
                for cond, part in parts_of_tokens:
                    last = nc.vector.scalar_tensor_tensor(k.rows[c % 2][:, part], k.x[:, c, part], gain(c, cond),
                                                          k.rinv[:, part], ALU.mult, ALU.mult)
                last.then_inc(t["scaled"].sem, 1)

            scale(0)
            for c in range(KD):
                if c + 1 < KD:
                    scale(c + 1)
                dve.wait_ge(t["shifted"].sem, t["shifted"].base + c + 1)
                for cond, part in parts_of_tokens:
                    row, high = k.rows[c % 2][:, part], k.normed[0][:, c, part].bitcast(F32)
                    if shift is None:
                        last = nc.vector.tensor_tensor(k.normed[1][:, c, part], row, high, ALU.subtract)
                    else:
                        last = nc.vector.scalar_tensor_tensor(k.normed[1][:, c, part], row, shift(c, cond), high,
                                                              ALU.add, ALU.subtract)
                last.then_inc(t["normed"].sem, 1)
            for q in range(1, depth):
                split_low(dve, 0, q)
            for s, spec in enumerate(specs):
                def unit_in(i, c, spec=spec, half=s // 2):
                    slot = wait_product(k, dve, spec, i, c)
                    row, n = k.rows[(half * KH + c) % 2][:, T], half * KH + c + 1
                    dve.wait_ge(t["silu_done"].sem, i * RING + (t["silu_done"].base + n))
                    nc.vector.tensor_tensor(row, row, k.psum[:, 2 * slot + 1, T], ALU.mult).then_inc(t["gated"].sem, 1)
                    dve.wait_ge(t["hidden_high"].sem, i * RING + (t["hidden_high"].base + n))
                    nc.vector.tensor_tensor(one(k.hidden[1], i * RING + c, col=T), row,
                                            one(k.hidden[0], i * RING + c, col=T).bitcast(F32), ALU.subtract)\
                        .then_inc(k.banks_free, 1)
                    split_low(dve, i, at(spec, c) + depth)

                def unit_out(i, c, spec=spec):
                    slot = wait_product(k, dve, spec, i, c)
                    chunk = i * RING + c
                    for cond, part in (halves(tokens) if callable(gate) else [(0, T)]):
                        row = one(k.x, chunk, col=part)
                        last = nc.vector.scalar_tensor_tensor(row, k.psum[:, 2 * slot, part],
                                                              gate(chunk, cond) if callable(gate) else gate, row,
                                                              ALU.mult, ALU.add)
                    last.then_inc(k.banks_free, 1)
                    split_low(dve, i, at(spec, c) + depth)

                each_unit(dve, 0, spec.n, unit_in if s % 2 == 0 else unit_out, s < len(specs) - 1)
    for name, n in dict(summed=1, root_done=1, inverse_done=1, scaled=KD, shifted=KD, normed=KD,
                        silu_done=KF, gated=KF, hidden_high=KF).items():
        t[name].close(n)
    close_squares(k)



def opening(k, w):
    nc = k.nc
    t = {n: k.tally(n) for n in ("cleared", "consts_landed", "tokens_landed", "vectors_landed",
                                                   "tokens_turned", "tokens_placed", "vectors_turned", "vectors_placed")}
    tokens = k.arena[:, 0:4 * D].rearrange("p (t n) -> p t n", t=4)
    tiles = (k.n_rows + P - 1) // P
    rows = k.arena[:, 4 * D:4 * D + tiles * P].rearrange("p (t n) -> p t n", t=tiles)
    loads = []
    for name, (source, layer, n, width, off) in zip(k.vec_at, k.vec_rows):
        src = w[source] if layer is None else w[source][layer:layer + 1]
        if len(src.shape) == 1:
            src = src.unsqueeze(0)
        flat = src.rearrange("a b -> (a b)")
        flat = flat[off:off + n * width].rearrange("(r c) -> r c", c=width)
        r, done = k.vec_at[name], 0
        while done < n:
            m = min(n - done, P - (r + done) % P)
            at = (r + done) % P
            loads.append((rows[at:at + m, (r + done) // P, 0:width], flat[done:done + m, :]))
            done += m
    lams = [(k.lam[:, l, v, :], w[f"lam_{n}_2"][l:l + 1, :].partition_broadcast(P))
            for l in (0, 1) for v, n in enumerate(("q1", "k1", "q2", "k2"))]
    with nc.Block() as block:
        @block.vector
        def _(dve):
            dve.sem_inc(k.banks_free, RING)
            nc.vector.memset(rows, 0.0).then_inc(t["cleared"].sem, 1)
            nc.vector.memset(k.eps[:, :], EPS).then_inc(t["cleared"].sem, 1)
            nc.vector.memset(k.eps5[:, :], 1e-5).then_inc(t["cleared"].sem, 1)
            nc.vector.memset(k.half_pi[:, :], float(np.pi / 2)).then_inc(t["cleared"].sem, 1)
            for c in range(KD):
                dve.wait_ge(t["tokens_turned"].sem, c + 1)
                nc.vector.tensor_copy(k.x[:, c, :], k.psum[:, c, :]).then_inc(t["tokens_placed"].sem, 1)
            dve.wait_ge(t["vectors_turned"].sem, 1)
            nc.vector.tensor_copy(k.vec[:, 0:tiles * P], k.psum[:, 0, 0:tiles * P]).then_inc(t["vectors_placed"].sem, 1)

        @block.sync
        def _(sp):
            sp.dma_start(tokens[:, 0:2, :], w["x"][0].rearrange("(t p) n -> p t n", p=P)).then_inc(t["tokens_landed"].sem, 16)
            sp.dma_start(tokens[:, 2:4, :], w["ctx"][0].rearrange("(t p) n -> p t n", p=P)).then_inc(t["tokens_landed"].sem, 16)
            sp.dma_start(k.consts[:, :], w["constants"]).then_inc(t["consts_landed"].sem, 16)
            load_weights(k, sp, 0, RING)

        @block.scalar
        def _(act):
            act.wait_ge(t["cleared"].sem, 1)
            for to, of in loads:
                act.dma_start(to, of).then_inc(t["vectors_landed"].sem, 16)
            for to, of in lams:
                act.dma_start(to, of).then_inc(t["vectors_landed"].sem, 16)
            act.dma_start(k.positions[:, :], w["positions_2"].unsqueeze(0).partition_broadcast(ROPE2))\
                .then_inc(t["vectors_landed"].sem, 16)
            act.wait_ge(t["vectors_placed"].sem, 1)
            for cond, name in enumerate(("c", "c_ctx")):
                at = k.vec_at[name]
                last = nc.scalar.activation(k.cond[:, :, cond], k.vec[:, at:at + KD], ACT.Silu)

        @block.tensor
        def _(pe):
            pe.wait_ge(t["consts_landed"].sem, 16)
            pe.wait_ge(t["tokens_landed"].sem, 32)
            for c in range(KD):
                for tt in range(4):
                    mm = nc.tensor.transpose(k.psum[:, c, tt * P:(tt + 1) * P], tokens[:, tt, c * P:(c + 1) * P],
                                             k.const("ident"))
                mm.then_inc(t["tokens_turned"].sem, 1)
            pe.wait_ge(t["vectors_landed"].sem, 16 * (len(loads) + len(lams) + 1))
            pe.wait_ge(t["tokens_placed"].sem, 1)
            for tt in range(tiles):
                mm = nc.tensor.transpose(k.psum[:, 0, tt * P:(tt + 1) * P], rows[:, tt, :], k.const("ident"))
            mm.then_inc(t["vectors_turned"].sem, 1)
    for name, n in dict(cleared=4, tokens_turned=KD, tokens_placed=KD, vectors_turned=1, vectors_placed=1).items():
        t[name].close(n)


def conditioning(k, l):
    nc, spec = k.nc, k.spec(f"mod{l}")
    derived = k.tally("derived")
    bias = k.vec_at[f"mod_b{l}"]
    copied, turned = k.tally("mod_copied"), k.tally("mod_turned")
    rows = [t[0:2, 0, n * 256:(n + 1) * 256] for t in (k.rinvs, k.roots) for n in range(2)]
    cond_high, cond_low = k.tally("cond_high"), k.tally("cond_low")
    split_high, split_low, wait_parts = weight_parts(k, [spec], RING)
    stack, sb = scoped(k, F32R)
    with stack, nc.Block() as block:
        part_buffers(k, sb, RING)
        cond_parts = [sb(f"cond_part{n}", [P, KD, 2]) for n in range(2)]
        stream_ahead(k, block, spec)
        if l == 0:
            sum_squares(k, block, TOK)

        @block.scalar
        def _(act):
            nc.scalar.activation(cond_parts[0][:, :, :], k.cond[:, :, :], ACT.Copy).then_inc(cond_high.sem, 1)
            each_unit(act, 0, RING, lambda i, c: split_high(act, i, c))
            each_unit(act, RING, spec.n, lambda i, c: split_high(act, i, c))
            if l == 0:
                for c in range(KD):
                    square_chunk(k, act, TOK, c)

        @block.tensor
        def _(pe):
            def turn(i, c):
                slot = (spec.start + c) % RING
                pe.wait_ge(copied.sem, i * RING + (copied.base + c + 1))
                for t in range(2):
                    mm = nc.tensor.matmul(k.psum[:, 2 * slot + 1, 2 * t:2 * t + 2], rows[slot][:, t * P:(t + 1) * P],
                                             k.const("ident")[0:2, 0:2], start=True, stop=True)
                mm.then_inc(turned.sem, 1)

            def unit(i, c):
                slot, weights = wait_parts(pe, i, c)
                for kc in range(KD):
                    mm = product_of_parts(k, k.psum[0:2, 2 * slot, 0:256], [x[:, kc, :] for x in cond_parts],
                                          [wide_tile(w)[:, kc, :] for w in weights], kc == 0, kc == KD - 1)
                mm.then_inc(k.unit_done, 1)
                if c > 0:
                    turn(i, c - 1)

            pe.wait_ge(cond_low.sem, cond_low.base + 1)
            unit(0, 0)
            each_unit(pe, 1, spec.n, unit)
            turn(0, spec.n - 1)

        @block.vector
        def _(dve):
            def place(i, c):
                slot = (spec.start + c) % RING
                dve.wait_ge(turned.sem, i * RING + (turned.base + c + 1))
                for t in range(2):
                    chunk = i * (RING * 2) + (c * 2 + t)
                    last = nc.vector.tensor_scalar(one(k.mod, chunk), k.psum[:, 2 * slot + 1, 2 * t:2 * t + 2],
                                                   column(k.vec, chunk + bias), None, ALU.add)
                last.then_inc(k.banks_free, 1)

            def unit(i, c):
                slot = wait_product(k, dve, spec, i, c)
                nc.vector.tensor_copy(rows[slot], k.psum[0:2, 2 * slot, 0:256]).then_inc(copied.sem, 1)
                if c > 0:
                    place(i, c - 1)
                split_low(dve, i, c + RING - 1)

            dve.wait_ge(cond_high.sem, cond_high.base + 1)
            nc.vector.tensor_tensor(cond_parts[1][:, :, :], k.cond[:, :, :], cond_parts[0][:, :, :].bitcast(F32), ALU.subtract)\
                .then_inc(cond_low.sem, 1)
            for c in range(RING - 1):
                split_low(dve, 0, c)
            unit(0, 0)
            each_unit(dve, 1, spec.n, unit)
            place(0, spec.n - 1)
            dve.wait_ge(k.banks_free, spec.start + spec.n + RING)
            for m, name in enumerate(("ffn1", "mix", "ffn2")):
                gain = k.vec_at[f"{name}_{l}"]
                for cond in range(2):
                    nc.vector.scalar_tensor_tensor(k.gain[:, m, :, cond], k.mod[:, (3 * m + 1) * KD:(3 * m + 2) * KD, cond],
                                                   1.0, k.vec[:, gain:gain + KD], ALU.add, ALU.mult).then_inc(derived.sem, 1)
            for m, at in ((0, 2), (1, 8)):
                nc.vector.tensor_scalar(k.gate[:, m], k.mod[:, at * KD:(at + 1) * KD, :], 0.5, None, ALU.mult)\
                    .then_inc(derived.sem, 1)
    cond_high.close(1), cond_low.close(1)
    derived.close(8), copied.close(spec.n), turned.close(spec.n)
    if l == 0:
        close_squares(k)


def modulated(k, m):
    return (lambda c, cond: k.gain[:, m, c, cond:cond + 1],
            lambda c, cond: k.mod[:, 3 * m * KD + c, cond:cond + 1])


def half_gate(k, m):
    def gate(chunk, cond):
        if isinstance(chunk, int):
            return k.gate[:, m, chunk, cond:cond + 1]
        return k.gate[:, m, bass.ds(chunk, 1), cond]
    return gate


def mix_gate(k):
    def gate(chunk, cond):
        if isinstance(chunk, int):
            return k.mod[:, 5 * KD + chunk, cond:cond + 1]
        return k.mod[:, bass.ds(chunk + 5 * KD, 1), cond]
    return gate


def ending(k, out):
    nc = k.nc
    turned, placed, stored = (k.tally(n) for n in ("tokens_turned", "tokens_placed", "stored"))
    rows = k.arena[:, 0:2 * D].rearrange("p (t n) -> p t n", t=2)
    with nc.Block() as block:
        @block.tensor
        def _(pe):
            for tt in range(2):
                for c in range(KD):
                    mm = nc.tensor.transpose(k.psum[:, 2 * tt + c // 4, (c % 4) * P:(c % 4 + 1) * P],
                                             k.h[:, c, tt * P:(tt + 1) * P], k.const("ident"))
                    if c % 4 == 3:
                        mm.then_inc(turned.sem, 1)

        @block.vector
        def _(dve):
            for n in range(4):
                dve.wait_ge(turned.sem, turned.base + n + 1)
                nc.vector.tensor_copy(rows[:, n // 2, (n % 2) * BANK:(n % 2 + 1) * BANK], k.psum[:, n, :])\
                    .then_inc(placed.sem, 1)

        @block.sync
        def _(sp):
            for n in range(4):
                sp.wait_ge(placed.sem, placed.base + n + 1)
                sp.dma_start(out[0][(n // 2) * P:(n // 2 + 1) * P, (n % 2) * BANK:(n % 2 + 1) * BANK],
                             rows[:, n // 2, (n % 2) * BANK:(n % 2 + 1) * BANK]).then_inc(stored.sem, 16)
            sp.wait_ge(stored.sem, 64)



def even_mixer(k):
    nc = k.nc
    qn, kn = (k.arena[:, n * HEADS * TOK:(n + 1) * HEADS * TOK].rearrange("p (h t) -> p h t", h=HEADS) for n in range(2))
    width = HD + MLA_ROPE
    ypad = k.side[:, 0:4 * 2 * (LAT + 2 * PAD)].rearrange("p (c s t) -> p c s t", c=4, s=2)

    spec = k.spec("in0")
    first, cleared, taps = k.tally("first_bank_out"), k.tally("cleared"), k.tally("tap_done")
    sums = [k.side[:, at:at + TOK] for at in (4 * 2 * (LAT + 2 * PAD), 4 * 2 * (LAT + 2 * PAD) + TOK)]
    sums += [k.mix[:, c, :] for c in (6, 7)]
    n_conv = 4
    with nc.Block() as block:
        stream_ahead(k, block, spec)

        @block.gpsimd
        def _(pool):
            nc.gpsimd.memset(ypad[:, :, :, 0:PAD], 0.0).then_inc(cleared.sem, 1)
            nc.gpsimd.memset(ypad[:, :, :, PAD + LAT:], 0.0).then_inc(cleared.sem, 1)
            pool.wait_ge(cleared.sem, cleared.base + 2)
            nc.gpsimd.memset(k.arena[width:P, 0:2 * HEADS * TOK], 0.0)

        @block.tensor
        def _(pe):
            for c in range(spec.n):
                slot = wait_weights(k, pe, spec, 0, c)
                for t in range(2):
                    m = MLA_ROPE if (c, t) == (n_conv + 2, 1) else P
                    for kc in range(KD):
                        lhs = wide_lhs(k.slots[slot], kc, t) if c in (n_conv, n_conv + 1) else \
                            pair_tiles(k.slots[slot])[:, t, kc, 0:m]
                        mm = nc.tensor.matmul(k.psum[0:m, 2 * slot + t, :], lhs, k.h[:, kc, :], start=kc == 0, stop=kc == KD - 1)
                mm.then_inc(k.unit_done, 1)

        @block.scalar
        def _(act):
            for c in range(spec.n):
                slot = wait_product(k, act, spec, 0, c)
                if c >= n_conv:
                    last = nc.scalar.activation(k.mix[:, 2 * (c - n_conv), :], k.psum[:, 2 * slot, :], ACT.Copy)
                else:
                    if c >= 2:
                        act.wait_ge(k.banks_free, RING + spec.start + c - 1)
                    last = nc.scalar.activation(k.square[:, c % 2, :], k.psum[:, 2 * slot + 1, :], ACT.Sigmoid,
                                                bias=column(k.vec, k.vec_at["glu_b"] + 4 + c))
                last.then_inc(first.sem, 1)

        @block.vector
        def _(dve):
            dve.wait_ge(cleared.sem, cleared.base + 2)
            for c in range(spec.n):
                slot = wait_product(k, dve, spec, 0, c)
                dve.wait_ge(first.sem, first.base + c + 1)
                if c >= n_conv:
                    m = MLA_ROPE if c == n_conv + 2 else P
                    nc.vector.tensor_copy(k.mix[0:m, 2 * (c - n_conv) + 1, :], k.psum[0:m, 2 * slot + 1, :])\
                        .then_inc(k.banks_free, 1)
                    continue
                nc.vector.scalar_tensor_tensor(
                    ypad[:, c, :, PAD:PAD + LAT], k.psum[:, 2 * slot, :].rearrange("p (s t) -> p s t", s=2),
                    column(k.vec, k.vec_at["glu_b"] + c), k.square[:, c % 2, :].rearrange("p (s t) -> p s t", s=2),
                    ALU.add, ALU.mult).then_inc(k.banks_free, 1)
                if c % 2 == 0:
                    continue
                dve.wait_ge(k.banks_free, RING + spec.start + c + 1)
                two = [(sums[n].rearrange("p (s t) -> p s t", s=2), ypad[:, n], n, k.vec_at["dw_w"] + n) for n in (c - 1, c)]
                base = taps.base + (c - 1) * CONV_W
                for total, y, n, w in two:
                    nc.vector.tensor_scalar(total, y[:, :, 0:LAT], column(k.vec, w), column(k.vec, k.vec_at["dw_b"] + n),
                                            ALU.mult, ALU.add).then_inc(taps.sem, 1)
                per_round = 5
                with dve.Fori(0, (CONV_W - 1) // per_round) as i:
                    for u in range(1, per_round + 1):
                        for m, (total, y, n, w) in enumerate(two):
                            dve.wait_ge(taps.sem, i * (2 * per_round) + (base + 2 * u + m - 1))
                            nc.vector.scalar_tensor_tensor(total, y[:, :, bass.ds(i * per_round + u, LAT)],
                                                           column(k.vec, i * (per_round * n_conv) + (w + u * n_conv)), total,
                                                           ALU.mult, ALU.add).then_inc(taps.sem, 1)
    first.close(spec.n)
    cleared.close(2)
    taps.close(n_conv * CONV_W)

    squared, mean, root, inv = (k.tally(n) for n in ("squared", "mean_done", "root_done", "inverse_done"))
    groups = [([0, 1], P, "kv_norm"), ([2, 3, 4], P, "q_norm")]
    with nc.Block() as block:
        @block.scalar
        def _(act):
            for chunks, rows, _ in groups:
                for c in chunks:
                    nc.scalar.activation(k.h[0:rows, c, :], k.mix[0:rows, c, :], ACT.Square).then_inc(squared.sem, 1)
            for g, (chunks, rows, _) in enumerate(groups):
                act.wait_ge(mean.sem, mean.base + g + 1)
                if g == 2:
                    act.wait_ge(inv.sem, inv.base + 1)
                nc.scalar.activation(k.roots[0:rows, g % 2, :], k.psum[0:rows, g, :], ACT.Sqrt, bias=k.eps[0:rows, 0:1],
                                     scale=1.0 / (rows * len(chunks)))\
                    .then_inc(root.sem, 1)

        @block.tensor
        def _(pe):
            done = 0
            for g, (chunks, rows, _) in enumerate(groups):
                for n, c in enumerate(chunks):
                    done += 1
                    pe.wait_ge(squared.sem, squared.base + done)
                    mm = nc.tensor.matmul(k.psum[0:rows, g, :], k.const("ones")[0:rows, 0:rows], k.h[0:rows, c, :],
                                          start=n == 0, stop=n == len(chunks) - 1)
                mm.then_inc(mean.sem, 1)

        @block.vector
        def _(dve):
            for g, (chunks, rows, gain) in enumerate(groups):
                dve.wait_ge(root.sem, root.base + g + 1)
                nc.vector.reciprocal(k.rinvs[0:rows, g % 2, :], k.roots[0:rows, g % 2, :]).then_inc(inv.sem, 1)
                dve.wait_ge(inv.sem, inv.base + g + 1)
                for n, c in enumerate(chunks):
                    nc.vector.scalar_tensor_tensor(k.mix[0:rows, c, :], k.mix[0:rows, c, :], column(k.vec, k.vec_at[gain] + n, slice(0, rows)),
                                                   k.rinvs[0:rows, g % 2, :], ALU.mult, ALU.mult)
    squared.close(5), mean.close(2), root.close(2), inv.close(2)

    spec = k.spec("heads0")
    item, out = k.tally("item_done"), k.tally("item_out")
    with nc.Block() as block:
        stream_ahead(k, block, spec)
        slots = [(spec.start + c) % RING for c in range(2)]
        uk, uv = (k.slots[slots[0]][:, n * 1024:(n + 1) * 1024].rearrange("p (k n) -> p k n", k=2) for n in range(2))
        uq = k.slots[slots[1]][:, 0:2304].rearrange("p (k h e) -> p k h e", k=3, h=HEADS)

        @block.scalar
        def _(act):
            for h in range(HEADS):
                nc.scalar.activation(kn[HD:width, h, :], k.mix[0:MLA_ROPE, 5, :], ACT.Copy)

        @block.tensor
        def _(pe):
            n = 0

            def free_bank():
                if n >= 8:
                    pe.wait_ge(out.sem, out.base + n - 7)
                return n % 8

            wait_weights(k, pe, spec, 0, 0)
            for pair in range(HEADS // 2):
                bank = free_bank()
                for kc in range(2):
                    mm = nc.tensor.matmul(k.psum[:, bank, :], uk[:, kc, pair * P:(pair + 1) * P], k.mix[:, kc, :],
                                          start=kc == 0, stop=kc == 1)
                mm.then_inc(item.sem, 1)
                n += 1
            for tt in range(4):
                bank = free_bank()
                for kc in range(2):
                    mm = nc.tensor.matmul(k.psum[:, bank, :], k.mix[:, kc, tt * P:(tt + 1) * P], uv[:, kc, :],
                                          start=kc == 0, stop=kc == 1)
                mm.then_inc(item.sem, 1)
                n += 1
            wait_weights(k, pe, spec, 0, 1)
            for h in range(HEADS):
                bank = free_bank()
                for kc in range(3):
                    mm = nc.tensor.matmul(k.psum[0:HD + MLA_ROPE, bank, :], uq[:, kc, h, :], k.mix[:, 2 + kc, :],
                                          start=kc == 0, stop=kc == 2)
                mm.then_inc(item.sem, 1)
                n += 1

        @block.vector
        def _(dve):
            for n in range(HEADS // 2 + 4 + HEADS):
                dve.wait_ge(item.sem, item.base + n + 1)
                bank = k.psum[:, n % 8, :]
                if n < 4:
                    for hh in range(2):
                        last = nc.vector.tensor_copy(kn[0:HD, 2 * n + hh, :], bank[hh * HD:(hh + 1) * HD])
                elif n < 8:
                    last = nc.vector.tensor_copy(k.v[:, n - 4, :], bank)
                else:
                    last = nc.vector.tensor_copy(qn[0:width, n - 8, :], bank[0:width])
                last.then_inc(out.sem, 1)
            dve.sem_inc(k.unit_done, 2)
            dve.sem_inc(k.banks_free, 2)
    item.close(16), out.close(16)

    scaled_gains(k, width ** -0.5, ["mla_q"])
    norm_all_heads(k, [(kn, HEADS, "mla_k"), (qn, HEADS, "mla_q")])
    both = k.arena[:, 0:2 * HEADS * TOK].rearrange("p (h t) -> p h t", h=2 * HEADS)
    rotate_heads(k, both, P, 2 * HEADS, k.const("turn96"), k.const("cos96"), k.const("sin96"))

    convolution(k, sums)
    for queries, keys, tile0, tiles in ((slice(0, LAT), slice(0, TOK), 0, 4), (slice(LAT, TOK), slice(LAT, TOK), 2, 2)):
        def score(ps, b, hh, qt, keys=keys):
            tile = slice(qt * P, (qt + 1) * P)
            return nc.tensor.matmul(ps, k.q_stage[:, hh, tile], one(kn, b * 2 + hh, col=keys), start=True, stop=True)

        attention(k, HEADS // 2, tiles, lambda b: [(k.q_stage[:, :, :], qn[:, bass.ds(b * 2, 2), queries])],
                  score, lambda b, hh, kt: k.v[:, tile0 + kt, bass.ds(b * P + hh * HD, HD)], HD,
                  lambda b: one(k.mix, b, col=queries))


def scaled_gains(k, scale, names):
    done = k.tally("derived")
    with k.nc.Block() as block:
        @block.vector
        def _(dve):
            for name in names:
                c = column(k.vec, k.vec_at[name])
                k.nc.vector.tensor_scalar(c, c, scale, None, ALU.mult).then_inc(done.sem, 1)
    done.close(len(names))


def convolution(k, acc):
    nc, C = k.nc, 4
    t = {n: k.tally(n) for n in ("mean_done", "centred", "squared", "root_done", "inverse_done", "normed")}
    dst = [k.mix[:, 4 + c, :] for c in range(C)]
    with nc.Block() as block:
        @block.vector
        def _(dve):
            dve.wait_ge(t["mean_done"].sem, t["mean_done"].base + 1)
            for c in range(C):
                nc.vector.tensor_tensor(acc[c], acc[c], k.psum[:, 0, :], ALU.subtract).then_inc(t["centred"].sem, 1)
            dve.wait_ge(t["root_done"].sem, t["root_done"].base + 1)
            nc.vector.reciprocal(k.rinv[:, :], k.root[:, :]).then_inc(t["inverse_done"].sem, 1)
            dve.wait_ge(t["inverse_done"].sem, t["inverse_done"].base + 1)
            for c in range(C):
                nc.vector.scalar_tensor_tensor(dst[c], acc[c], column(k.vec, k.vec_at["ln_g"] + c), k.rinv[:, :],
                                               ALU.mult, ALU.mult).then_inc(t["normed"].sem, 1)

        @block.tensor
        def _(pe):
            for c in range(C):
                mm = nc.tensor.matmul(k.psum[:, 0, :], k.const("mean512"), acc[c], start=c == 0, stop=c == C - 1)
            mm.then_inc(t["mean_done"].sem, 1)
            for c in range(C):
                pe.wait_ge(t["squared"].sem, t["squared"].base + c + 1)
                mm = nc.tensor.matmul(k.psum[:, 1, :], k.const("mean512"), k.h[:, c, :], start=c == 0, stop=c == C - 1)
            mm.then_inc(t["mean_done"].sem, 1)

        @block.scalar
        def _(act):
            for c in range(C):
                act.wait_ge(t["centred"].sem, t["centred"].base + c + 1)
                nc.scalar.activation(k.h[:, c, :], acc[c], ACT.Square).then_inc(t["squared"].sem, 1)
            act.wait_ge(t["mean_done"].sem, t["mean_done"].base + 2)
            nc.scalar.activation(k.root[:, :], k.psum[:, 1, :], ACT.Sqrt, bias=k.eps[:, 0:1]).then_inc(t["root_done"].sem, 1)
            for c in range(C):
                act.wait_ge(t["normed"].sem, t["normed"].base + c + 1)
                nc.scalar.activation(dst[c], dst[c], ACT.Silu, bias=column(k.vec, k.vec_at["ln_b"] + c))
    for name, n in dict(mean_done=2, centred=C, squared=C, root_done=1, inverse_done=1, normed=C).items():
        t[name].close(n)



def odd_mixer(k, w):
    nc = k.nc
    A = k.arena

    def heads(at, n, t):
        return A[:, at:at + n * t].rearrange("p (h t) -> p h t", h=n)

    ck, nk = heads(0, 2, TOK), heads(2 * TOK, HEADS, TOK)
    cq, nq = heads(10 * TOK, HEADS, LAT), heads(14 * TOK, HEADS, LAT)
    bias = k.side[:, 0:2 * HEADS * LAT].rearrange("p (q h k) -> p q h k", q=2, h=HEADS)

    spec = k.spec("in1")
    first, landed, masked = k.tally("first_bank_out"), k.tally("bias_landed"), k.tally("bias_masked")
    rows = LAT // GRID_W
    with nc.Block() as block:
        stream_ahead(k, block, spec)

        @block.gpsimd
        def _(pool):
            nc.gpsimd.memset(A[HD:P, 0:18 * TOK], 0.0)

        @block.tensor
        def _(pe):
            for c in range(spec.n):
                slot = wait_weights(k, pe, spec, 0, c)
                W = wide_tile(k.slots[slot])
                T = slice(0, TOK if c < 5 else LAT)
                if c in (0, 1, 2, 5, 6, 7, 8):
                    for t in range(1 if c == 0 else 2):
                        for kc in range(KD):
                            mm = nc.tensor.matmul(k.psum[:, 2 * slot + t, T], W[:, kc, t * P:(t + 1) * P], k.h[:, kc, T],
                                                  start=kc == 0, stop=kc == KD - 1)
                if c in (0, 3, 4):
                    n = P if c == 0 else 256
                    for tt in range(4):
                        at = k.psum[:, 2 * slot + 1, tt * P:(tt + 1) * P] if c == 0 else \
                            k.psum[:, 2 * slot + tt // 2, (tt % 2) * n:(tt % 2 + 1) * n]
                        for kc in range(KD):
                            mm = nc.tensor.matmul(at, k.h[:, kc, tt * P:(tt + 1) * P], W[:, kc, 256 - n:256],
                                                  start=kc == 0, stop=kc == KD - 1)
                mm.then_inc(k.unit_done, 1)

        def place(engine, copy, bank, c):
            slot = (spec.start + c) % RING
            src = k.psum[:, 2 * slot + bank, :]
            if c == 0 and bank == 1:
                return copy(k.v_shared[:, :, :], src.rearrange("p (t e) -> p t e", t=4))
            if c in (3, 4):
                return copy(k.v[:, 2 * bank:2 * bank + 2, (c - 3) * 256:(c - 2) * 256], src.rearrange("p (t e) -> p t e", t=2))
            to, h, T = {0: (ck, 0, TOK), 1: (nk, 0, TOK), 2: (nk, 4, TOK), 5: (cq, 0, LAT), 6: (cq, 4, LAT),
                        7: (nq, 0, LAT), 8: (nq, 4, LAT)}[c]
            for hh in range(2):
                last = copy(to[0:HD, h + 2 * bank + hh, :], src[hh * HD:(hh + 1) * HD, 0:T])
            return last

        @block.scalar
        def _(act):
            for r in range(rows):
                for j in range(rows):
                    src = bass.AP(w["l1_na_rpb"].tensor, (j - r + RPB_H // 2) * RPB_W + RPB_W // 2 - GRID_W + 1,
                                  [[1, GRID_W], [RPB_H * RPB_W, HEADS], [1, GRID_W]])
                    dst = bias[(r % 2) * GRID_W:(r % 2 + 1) * GRID_W, r // 2, :, j * GRID_W:(j + 1) * GRID_W]
                    act.dma_start(dst, src).then_inc(landed.sem, 16)
            for c in range(spec.n):
                wait_product(k, act, spec, 0, c)
                place(act, lambda o, i: nc.scalar.activation(o, i, ACT.Copy), 0, c).then_inc(first.sem, 1)

        @block.vector
        def _(dve):
            for c in range(spec.n):
                wait_product(k, dve, spec, 0, c)
                dve.wait_ge(first.sem, first.base + c + 1)
                place(dve, nc.vector.tensor_copy, 1, c).then_inc(k.banks_free, 1)
            dve.wait_ge(landed.sem, landed.base + 16 * rows * rows)
            for qt in range(2):
                for h in range(HEADS):
                    nc.vector.tensor_tensor(bias[:, qt, h, :], bias[:, qt, h, :], k.const("window"), ALU.add)\
                        .then_inc(masked.sem, 1)
    first.close(spec.n), landed.close(16 * rows * rows), masked.close(2 * HEADS)

    scaled_gains(k, HD ** -0.5, ["gqa_q", "na_q"])
    two = lambda heads: heads.rearrange("p (a b) t -> p a (b t)", b=2)
    norm_all_heads(k, [(ck, 2, "gqa_k"), (nk, HEADS, "na_k"), (two(cq), HEADS // 2, "gqa_q"), (two(nq), HEADS // 2, "na_q")])
    rotate_heads(k, ck, P, 2, k.full("turn64"), k.const("cos64"), k.const("sin64"))
    rotate_heads(k, cq, P, HEADS, k.full("turn64"), k.const("cos64"), k.const("sin64"))

    for g in range(2):
        def score(ps, b, hh, qt, g=g):
            return nc.tensor.matmul(ps, k.q_stage[:, hh, qt * P:(qt + 1) * P], ck[:, g, :], start=True, stop=True)

        attention(k, 2, 4, lambda b: [(k.q_stage[:, :, :], cq[:, bass.ds(b * 2 + 4 * g, 2), :])], score,
                  lambda b, hh, kt: k.v_shared[:, kt, g * HD:(g + 1) * HD], HD, lambda b: one(k.mix, b + 2 * g, col=slice(0, LAT)))

    def score(ps, b, hh, qt):
        nc.tensor.matmul(ps, k.q_stage[:, hh, qt * P:(qt + 1) * P], one(nk, b * 2 + hh), start=True, stop=False)
        return nc.tensor.matmul(ps[:, 0:LAT], k.const("flip"), one(bias[:, qt], b * 2 + hh), start=False, stop=True)

    attention(k, HEADS // 2, 4, lambda b: [(k.q_stage[:, :, :], nq[:, bass.ds(b * 2, 2), :])], score,
              lambda b, hh, kt: k.v[:, kt, bass.ds(b * P + hh * HD, HD)], HD, lambda b: one(k.mix, b + 4, col=slice(0, LAT)))



def rope_tables(k):
    nc = k.nc
    step, done = k.tally("angle_step"), k.tally("table_done")
    R = slice(0, ROPE2)
    ang, turns, low = k.rinvs[R, 0, 0:LAT], k.roots[R, 1, 0:LAT], k.roots[R, 0, 0:LAT]
    magic = 1.5 * 2.0 ** 23
    two_pi = 2 * np.pi
    c1 = 6.28125
    c2 = float(np.float32(two_pi - c1))
    c3 = float(two_pi - c1 - c2)
    with nc.Block() as block:
        @block.vector
        def _(dve):
            n = [0]

            def chained(ins):
                n[0] += 1
                ins.then_inc(step.sem, 1)
                dve.wait_ge(step.sem, step.base + n[0])

            nc.vector.memset(k.r_stage[:, 0, :], 1.0)
            nc.vector.memset(k.r_stage[:, 1, :], 0.0)
            chained(nc.vector.tensor_copy(ang, k.positions[:, :]))
            chained(nc.vector.tensor_scalar(ang, ang, k.const("freq")[:, 0:1], None, ALU.mult))
            chained(nc.vector.tensor_scalar(turns, ang, float(1 / two_pi), magic, ALU.mult, ALU.add))
            chained(nc.vector.tensor_scalar(turns, turns, -magic, None, ALU.add))
            for c in (c1, c2, c3):
                chained(nc.vector.scalar_tensor_tensor(ang, turns, -c, ang, ALU.mult, ALU.add))
            top = float(np.nextafter(np.float32(np.pi), np.float32(0)))
            chained(nc.vector.tensor_scalar(ang, ang, top, -top, ALU.min, ALU.max))

        @block.scalar
        def _(act):
            act.wait_ge(step.sem, step.base + 8)
            nc.scalar.activation(low, ang, ACT.Abs).then_inc(done.sem, 1)
            nc.scalar.activation(k.sin2, ang, ACT.Sin).then_inc(done.sem, 1)
            act.wait_ge(done.sem, done.base + 1)
            nc.scalar.activation(k.cos2, low, ACT.Sin, scale=-1.0, bias=k.half_pi[R, 0:1]).then_inc(done.sem, 1)
    step.close(8), done.close(3)


def lambda_init(l):
    return 0.8 - 0.6 * float(np.exp(-0.3 * l))


HEAD_AT = dict(aq=0, ak=8, dq=16, dk=20, iq=24, ik=32, bq=33, bk=37, cq=41, ck=45)
N_HEADS2 = 49
SCALED_UNITS = (0, 1, 4, 8, 10)


def project_heads(k, l, splits):
    nc, spec = k.nc, k.spec(f"in_b{l}")
    first = k.tally("first_bank_out")
    T = slice(0, LAT)
    n_qk, n_v = len(QK_COLUMNS), len(V_COLUMNS)
    values = [k.va[:, :, 0:256], k.va[:, :, 256:512], k.bv, k.cv, k.dv]
    split_high, split_low, wait_parts = splits
    with nc.Block() as block:
        stream_ahead(k, block, spec)

        @block.gpsimd
        def _(pool):
            nc.gpsimd.memset(k.heads[HD:P, :, :], 0.0)

        @block.tensor
        def _(pe):
            def rows(kc):
                return [x[:, kc, :] for x in k.normed]

            def tile(kc, t):
                return [x[:, kc, t * P:(t + 1) * P] for x in k.normed]

            for c in range(spec.n):
                slot, parts = wait_parts(pe, 0, c)
                b0, b1 = k.psum[:, 2 * slot], k.psum[:, 2 * slot + 1]

                def weights(kc, at, n, parts=parts):
                    return [wide_tile(w)[:, kc, at:at + n] for w in parts]

                if c < n_qk:
                    products = [(bank[:, T], lambda kc, t=t: weights(kc, t * P, P), rows) for t, bank in enumerate((b0, b1))]
                elif c < n_qk + n_v:
                    products = [(bank[:, T], lambda kc, t=t: tile(kc, t), lambda kc: weights(kc, 0, 256))
                                for t, bank in enumerate((b0, b1))]
                else:
                    products = [(b0[0:HD, T], lambda kc: weights(kc, 0, HD), rows),
                                (b0[0:4, LAT:TOK], lambda kc: weights(kc, 72, 4), rows)]
                    products += [(b1[:, t * 8:(t + 1) * 8], lambda kc, t=t: tile(kc, t), lambda kc: weights(kc, HD, 8))
                                 for t in range(2)]
                for to, left, right in products:
                    for kc in range(KD):
                        mm = product_of_parts(k, to, left(kc), right(kc), kc == 0, kc == KD - 1)
                mm.then_inc(k.unit_done, 1)

        def head_of(c):
            return 4 * c if c < 8 else HEAD_AT["bq"] + 4 * (c - 8)

        @block.scalar
        def _(act):
            split_high(act, 0, 1)
            for c in range(spec.n):
                slot = wait_product(k, act, spec, 0, c)
                split_high(act, 0, c + 2)
                bank = k.psum[:, 2 * slot]
                if c < n_qk:
                    for hh in range(2):
                        last = nc.scalar.activation(k.heads[0:HD, head_of(c) + hh, :], bank[hh * HD:(hh + 1) * HD, T], ACT.Copy,
                                                    scale=HD ** -0.5 if c in SCALED_UNITS else 1.0)
                elif c < n_qk + n_v:
                    last = nc.scalar.activation(values[c - n_qk][:, 0], bank[:, T], ACT.Copy)
                else:
                    nc.scalar.activation(k.heads[0:HD, HEAD_AT["ik"], :], bank[0:HD, T], ACT.Copy)
                    last = nc.scalar.activation(k.forget, bank[0:4, LAT:TOK], ACT.Identity,
                                                bias=column(k.vec, k.vec_at[f"fgt{l}"], slice(0, 4)))
                last.then_inc(first.sem, 1)

        @block.vector
        def _(dve):
            split_low(dve, 0, 1)
            for c in range(spec.n):
                slot = wait_product(k, dve, spec, 0, c)
                split_low(dve, 0, c + 2)
                dve.wait_ge(first.sem, first.base + c + 1)
                bank = k.psum[:, 2 * slot + 1]
                if c < n_qk:
                    for hh in range(2):
                        last = nc.vector.tensor_scalar(k.heads[0:HD, head_of(c) + 2 + hh, :], bank[hh * HD:(hh + 1) * HD, T],
                                                       HD ** -0.5 if c in SCALED_UNITS else 1.0, None, ALU.mult)
                elif c < n_qk + n_v:
                    last = nc.vector.tensor_copy(values[c - n_qk][:, 1], bank[:, T])
                else:
                    last = nc.vector.tensor_copy(k.index_weight, bank[:, 0:16])
                last.then_inc(k.banks_free, 1)
    first.close(spec.n)


def log_sigmoids(k, l):
    nc = k.nc
    t = {n: k.tally(n) for n in ("magnitude", "exp_done", "log_done", "sum_step", "dots", "lambda_exp", "selector_landed")}
    mag, low = k.square[0:4, 0, 0:LAT], k.square[0:4, 1, 0:LAT]
    with nc.Block() as block:
        @block.vector
        def _(dve):
            nc.vector.memset(k.ones_row, 1.0).then_inc(t["sum_step"].sem, 1)
            for v in range(2):
                nc.vector.scalar_tensor_tensor(k.roots[:, v, 0:HD], k.lam[:, l, 2 * v, :], 1.0, k.lam[:, l, 2 * v + 1, :],
                                               ALU.mult, ALU.mult, accum_out=k.lam_exp[:, v:v + 1]).then_inc(t["dots"].sem, 1)
            dve.wait_ge(t["log_done"].sem, t["log_done"].base + 1)
            nc.vector.scalar_tensor_tensor(low, k.forget, 0.0, mag, ALU.min, ALU.subtract).then_inc(t["sum_step"].sem, 1)
            dve.wait_ge(t["sum_step"].sem, t["sum_step"].base + 2)
            nc.vector.tensor_tensor_scan(k.cum, k.ones_row, low, 0.0, ALU.mult, ALU.add).then_inc(t["sum_step"].sem, 1)
            dve.wait_ge(t["sum_step"].sem, t["sum_step"].base + 3)
            for h in range(4):
                nc.vector.tensor_copy(k.heads[HD:HD + 4, HEAD_AT["bq"] + h, :], k.cum).then_inc(t["sum_step"].sem, 1)
                nc.vector.tensor_scalar(k.heads[HD + 32:HD + 36, HEAD_AT["bk"] + h, :], k.cum, -1.0, None, ALU.mult)\
                    .then_inc(t["sum_step"].sem, 1)
            dve.wait_ge(t["lambda_exp"].sem, t["lambda_exp"].base + 1)
            nc.vector.tensor_scalar(k.lam_exp[:, 1:2], k.lam_exp[:, 1:2], -lambda_init(l), None, ALU.add)\
                .then_inc(t["sum_step"].sem, 1)
            dve.wait_ge(t["sum_step"].sem, t["sum_step"].base + 12)
            nc.vector.tensor_tensor(k.minus_lam, k.lam_exp[:, 1:2], k.lam_exp[:, 0:1], ALU.subtract).then_inc(t["sum_step"].sem, 1)

        @block.scalar
        def _(act):
            nc.scalar.activation(mag, k.forget, ACT.Abs).then_inc(t["magnitude"].sem, 1)
            act.wait_ge(t["magnitude"].sem, t["magnitude"].base + 1)
            nc.scalar.activation(mag, mag, ACT.Exp, scale=-1.0).then_inc(t["exp_done"].sem, 1)
            act.wait_ge(t["dots"].sem, t["dots"].base + 2)
            nc.scalar.activation(k.lam_exp[:, 0:2], k.lam_exp[:, 0:2], ACT.Exp).then_inc(t["lambda_exp"].sem, 1)
            act.wait_ge(t["exp_done"].sem, t["exp_done"].base + 1)
            nc.scalar.activation(mag, mag, ACT.Ln, bias=1.0).then_inc(t["log_done"].sem, 1)

        @block.sync
        def _(sp):
            for row, name in ((HD, "bk"), (HD + 32, "bq")):
                sp.dma_start(k.heads[row:row + 4, HEAD_AT[name]:HEAD_AT[name] + 4, :], k.selector)\
                    .then_inc(t["selector_landed"].sem, 16)
            sp.wait_ge(t["selector_landed"].sem, t["selector_landed"].base + 32)
    for name, n in dict(magnitude=1, exp_done=1, log_done=1, sum_step=13, dots=2, lambda_exp=1, selector_landed=32).items():
        t[name].close(n)


def score_keys(k):
    nc = k.nc
    t = {n: k.tally(n) for n in ("scored", "rectified", "summed")}
    n_pairs = 4
    with nc.Block() as block:
        @block.tensor
        def _(pe):
            for qt in range(2):
                for j in range(n_pairs):
                    n = qt * n_pairs + j
                    for jj in range(2):
                        mm = nc.tensor.matmul(k.psum[:, n, jj * LAT:(jj + 1) * LAT],
                                              k.heads[:, HEAD_AT["iq"] + 2 * j + jj, qt * P:(qt + 1) * P],
                                              k.heads[:, HEAD_AT["ik"], :], start=True, stop=True)
                    mm.then_inc(t["scored"].sem, 1)

        @block.scalar
        def _(act):
            for n in range(2 * n_pairs):
                act.wait_ge(t["scored"].sem, t["scored"].base + n + 1)
                if n >= 2:
                    act.wait_ge(t["summed"].sem, t["summed"].base + 2 * (n - 1))
                nc.scalar.activation(k.square[:, n % 2, :], k.psum[:, n, :], ACT.Relu).then_inc(t["rectified"].sem, 1)

        @block.vector
        def _(dve):
            for n in range(2 * n_pairs):
                qt, j = n // n_pairs, n % n_pairs
                dve.wait_ge(t["rectified"].sem, t["rectified"].base + n + 1)
                for jj in range(2):
                    if (j, jj) == (0, 0):
                        before = k.const("causal")[:, qt * LAT:(qt + 1) * LAT]
                    else:
                        before = k.score[:, qt, :]
                        dve.wait_ge(t["summed"].sem, t["summed"].base + 2 * n + jj)
                    nc.vector.scalar_tensor_tensor(k.score[:, qt, :], k.square[:, n % 2, jj * LAT:(jj + 1) * LAT],
                                                   k.index_weight[:, qt * 8 + 2 * j + jj:qt * 8 + 2 * j + jj + 1], before,
                                                   ALU.mult, ALU.add).then_inc(t["summed"].sem, 1)
    for name, n in dict(scored=2 * n_pairs, rectified=2 * n_pairs, summed=4 * n_pairs).items():
        t[name].close(n)


BEST_ROUNDS = TOPK // 8


def take_best(k, dve, r):
    found, taken = k.tally("best_found"), k.tally("taken")
    for qt in range(2):
        if r:
            dve.wait_ge(taken.sem, taken.base + 2 * (r - 1) + qt + 1)
        k.nc.vector.max(k.best[:, qt, :], k.score[:, qt, :]).then_inc(found.sem, 1)
    for qt in range(2):
        dve.wait_ge(found.sem, found.base + 2 * r + qt + 1)
        k.nc.vector.match_replace(k.score[:, qt, :], k.best[:, qt, :], k.score[:, qt, :], TAKEN).then_inc(taken.sem, 1)


def mask_others(k, dve):
    taken = k.tally("taken")
    for qt in range(2):
        dve.wait_ge(taken.sem, taken.base + 2 * BEST_ROUNDS + qt - 1)
        k.nc.vector.tensor_scalar(k.chosen[:, qt, :], k.score[:, qt, :], TAKEN / 2, MASKED, ALU.is_gt, ALU.mult)\
            .then_inc(taken.sem, 1)
    for qt in range(2):
        dve.wait_ge(taken.sem, taken.base + 2 * BEST_ROUNDS + qt + 1)
        k.nc.vector.tensor_tensor(k.chosen[:, qt, :], k.chosen[:, qt, :], k.const("causal")[:, qt * LAT:(qt + 1) * LAT], ALU.add)\
            .then_inc(taken.sem, 1)


def stick_breaking(k):
    nc, N = k.nc, 4
    names = ("logits", "magnitude", "exp_done", "log_done", "softplus", "kept", "summed_later", "in_exponent", "exponent",
             "weight_exp", "masked", "weighted", "placed")
    t = {n: k.tally("sb_" + n) for n in names}
    strict = k.const("strict")

    def buf(h):
        return k.square[:, h % 2, :], k.roots[:, h % 2, :], k.rinvs[:, h % 2, :]

    def weigh(pe, h):
        _, _, weights = buf(h)
        pe.wait_ge(t["masked"].sem, t["masked"].base + h + 1)
        if h >= 2:
            pe.wait_ge(t["placed"].sem, t["placed"].base + h - 1)
        for kt in range(2):
            mm = nc.tensor.matmul(k.psum[0:HD, 6 + h % 2, 0:LAT], k.cv[:, kt, h * HD:(h + 1) * HD],
                                  weights[:, kt * LAT:(kt + 1) * LAT], start=kt == 0, stop=kt == 1)
        mm.then_inc(t["weighted"].sem, 1)

    with nc.Block() as block:
        @block.tensor
        def _(pe):
            for h in range(N):
                for kt in range(2):
                    mm = nc.tensor.matmul(k.psum[:, h, kt * LAT:(kt + 1) * LAT],
                                          k.heads[:, HEAD_AT["ck"] + h, kt * P:(kt + 1) * P],
                                          k.heads[:, HEAD_AT["cq"] + h, :], start=True, stop=True)
                mm.then_inc(t["logits"].sem, 1)
            for h in range(N):
                _, _, kept = buf(h)
                pe.wait_ge(t["kept"].sem, t["kept"].base + h + 1)
                if h >= 2:
                    pe.wait_ge(t["exponent"].sem, t["exponent"].base + h - 1)
                bank = k.psum[:, 4 + h % 2, :]
                nc.tensor.matmul(bank[:, 0:LAT], k.const("later"), kept[:, 0:LAT], start=True, stop=False)
                nc.tensor.matmul(bank[:, 0:LAT], k.const("ones"), kept[:, LAT:TOK], start=False, stop=True)
                nc.tensor.matmul(bank[:, LAT:TOK], k.const("later"), kept[:, LAT:TOK], start=True, stop=True)\
                    .then_inc(t["summed_later"].sem, 1)
                if h >= 1:
                    weigh(pe, h - 1)
            weigh(pe, N - 1)

        @block.vector
        def _(dve):
            def middle(h):
                low, soft, kept = buf(h)
                dve.wait_ge(t["log_done"].sem, t["log_done"].base + h + 1)
                if h >= 2:
                    dve.wait_ge(t["masked"].sem, t["masked"].base + h - 1)
                nc.vector.scalar_tensor_tensor(soft, k.psum[:, h, :], 0.0, low, ALU.max, ALU.add).then_inc(t["softplus"].sem, 1)
                dve.wait_ge(t["softplus"].sem, t["softplus"].base + h + 1)
                if h >= 2:
                    dve.wait_ge(t["weighted"].sem, t["weighted"].base + h - 1)
                nc.vector.scalar_tensor_tensor(kept, soft, -1.0, strict, ALU.mult, ALU.mult).then_inc(t["kept"].sem, 1)
                nc.vector.tensor_tensor(low, k.psum[:, h, :], soft, ALU.subtract).then_inc(t["in_exponent"].sem, 1)
                dve.wait_ge(t["in_exponent"].sem, t["in_exponent"].base + h + 1)
                dve.wait_ge(t["summed_later"].sem, t["summed_later"].base + h + 1)
                nc.vector.tensor_tensor(soft, low, k.psum[:, 4 + h % 2, :], ALU.add).then_inc(t["exponent"].sem, 1)

            def end(h):
                low, soft, kept = buf(h)
                dve.wait_ge(t["weight_exp"].sem, t["weight_exp"].base + h + 1)
                nc.vector.tensor_tensor(kept, soft, strict, ALU.mult).then_inc(t["masked"].sem, 1)

            rounds = BEST_ROUNDS // (2 * N)
            for h in range(2):
                for r in range(rounds):
                    take_best(k, dve, h * rounds + r)
                middle(h)
            done = 2 * rounds
            for h in range(N):
                for r in range(rounds):
                    take_best(k, dve, done + r)
                done += rounds
                end(h)
                if h >= 1 and h + 1 < N:
                    for r in range(rounds):
                        take_best(k, dve, done + r)
                    done += rounds
                    middle(h + 1)
            for r in range(done, BEST_ROUNDS):
                take_best(k, dve, r)
            mask_others(k, dve)

        @block.scalar
        def _(act):
            def begin(h):
                low, soft, kept = buf(h)
                act.wait_ge(t["logits"].sem, t["logits"].base + h + 1)
                if h >= 2:
                    act.wait_ge(t["exponent"].sem, t["exponent"].base + h - 1)
                nc.scalar.activation(low, k.psum[:, h, :], ACT.Abs).then_inc(t["magnitude"].sem, 1)
                act.wait_ge(t["magnitude"].sem, t["magnitude"].base + h + 1)
                nc.scalar.activation(low, low, ACT.Exp, scale=-1.0).then_inc(t["exp_done"].sem, 1)
                act.wait_ge(t["exp_done"].sem, t["exp_done"].base + h + 1)
                nc.scalar.activation(low, low, ACT.Ln, bias=1.0).then_inc(t["log_done"].sem, 1)

            def end(h):
                low, soft, kept = buf(h)
                act.wait_ge(t["exponent"].sem, t["exponent"].base + h + 1)
                nc.scalar.activation(soft, soft, ACT.Exp).then_inc(t["weight_exp"].sem, 1)

            def place(h):
                act.wait_ge(t["weighted"].sem, t["weighted"].base + h + 1)
                nc.scalar.activation(k.y[(h % 2) * HD:(h % 2 + 1) * HD, 6 + h // 2, :], k.psum[0:HD, 6 + h % 2, 0:LAT],
                                     ACT.Copy).then_inc(t["placed"].sem, 1)

            begin(0), begin(1)
            for h in range(N):
                end(h)
                if h + 2 < N:
                    begin(h + 2)
                if h >= 1:
                    place(h - 1)
            place(N - 1)
    for name in names:
        t[name].close(N)
    k.tally("best_found").close(2 * BEST_ROUNDS), k.tally("taken").close(2 * BEST_ROUNDS + 4)


def merge_branches(k, l, splits):
    nc, spec = k.nc, k.spec(f"merge_b{l}")
    T = slice(0, LAT)
    opened, product, summed = (k.tally(n) for n in ("gates_open", "gated", "gated_sum"))
    bias = k.vec_at[f"gate_b{l}"]
    y = dict(a=[k.y[:, c, :] for c in range(4)], b=[k.y[:, c, :] for c in (4, 5)],
             c=[k.y[:, c, :] for c in (6, 7)], d=[k.selected[:, c, :] for c in range(2)])
    parts = [[(0, 16, y["a"]), (3, 20, y["d"])], [(1, 16, y["b"]), (2, 18, y["c"])]]
    split_high, split_low, wait_parts = splits

    def all_units(engine, unit):
        for first, last in ((0, 2), (2, spec.n - 2), (spec.n - 2, spec.n)):
            each_unit(engine, first, last, unit)

    with nc.Block() as block:
        stream_ahead(k, block, spec)

        @block.tensor
        def _(pe):
            def unit(i, c):
                slot, weights = wait_parts(pe, i, c)
                W = tall_tile(k.slots[slot])
                for n, (_, row, chunks) in enumerate(parts[c % 2]):
                    half = slice(n * LAT, (n + 1) * LAT)
                    for kc in range(KD):
                        at = (n * KD + kc) * P
                        product_of_parts(k, k.psum[:, 2 * slot, half], [w[:, at:at + P] for w in weights],
                                         [x[:, kc, :] for x in k.normed], kc == 0, kc == KD - 1)
                    for kc, chunk in enumerate(chunks):
                        mm = nc.tensor.matmul(k.psum[:, 2 * slot + 1, half], W[:, row + kc, :], chunk,
                                              start=kc == 0, stop=kc == len(chunks) - 1)
                mm.then_inc(k.unit_done, 1)
            all_units(pe, unit)

        @block.scalar
        def _(act):
            def unit(i, c):
                slot = wait_product(k, act, spec, i, c)
                split_high(act, i, c + 2)
                act.wait_ge(k.banks_free, i * RING + (RING + spec.start + c - 1))
                for n, (gate, _, _) in enumerate(parts[c % 2]):
                    at = i * (RING // 2) + (bias + gate * KD + c // 2)
                    last = nc.scalar.activation(k.square[:, c % 2, n * LAT:(n + 1) * LAT],
                                                k.psum[:, 2 * slot, n * LAT:(n + 1) * LAT], ACT.Sigmoid,
                                                bias=column(k.vec, at))
                last.then_inc(opened.sem, 1)
            split_high(act, 0, 0), split_high(act, 0, 1)
            all_units(act, unit)

        @block.vector
        def _(dve):
            def unit(i, c):
                slot = wait_product(k, dve, spec, i, c)
                split_low(dve, i, c + 2)
                dve.wait_ge(opened.sem, i * RING + (opened.base + c + 1))
                tmp = k.roots[:, c % 2, :]
                nc.vector.tensor_tensor(tmp, k.square[:, c % 2, :], k.psum[:, 2 * slot + 1, :], ALU.mult).then_inc(product.sem, 1)
                dve.wait_ge(product.sem, i * RING + (product.base + c + 1))
                row = one(k.merged, i * (RING // 2) + c // 2)
                if c % 2 == 0:
                    nc.vector.tensor_tensor(row, tmp[:, 0:LAT], tmp[:, LAT:TOK], ALU.add).then_inc(k.banks_free, 1)
                else:
                    nc.vector.tensor_tensor(row, row, tmp[:, 0:LAT], ALU.add).then_inc(summed.sem, 1)
                    dve.wait_ge(summed.sem, i * (RING // 2) + (summed.base + c // 2 + 1))
                    nc.vector.tensor_tensor(row, row, tmp[:, LAT:TOK], ALU.add).then_inc(k.banks_free, 1)
            split_low(dve, 0, 0), split_low(dve, 0, 1)
            all_units(dve, unit)
    opened.close(spec.n), product.close(spec.n), summed.close(spec.n // 2)


def second_attentions(k, l):
    nc = k.nc
    causal = [k.const("causal")[:, qt * LAT:(qt + 1) * LAT] for qt in range(2)]
    rotate_heads(k, k.heads, P, HEAD_AT["ik"] + 1, k.full("turn16"), k.r_stage[:, 0, :], k.r_stage[:, 1, :])
    log_sigmoids(k, l)

    def logits(ps, q, hh, qt, key_head, last=False):
        return nc.tensor.matmul(ps, k.q_stage[:, hh, qt * P:(qt + 1) * P], one(k.heads, key_head), start=True, stop=last)

    def queries(name):
        return lambda b: [(k.q_stage[:, :, :], k.heads[:, bass.ds(b * 2 + HEAD_AT[name], 2), :])]

    def score(ps, b, hh, qt):
        logits(ps, "aq", hh, qt, b * 2 + (HEAD_AT["ak"] + hh))
        return nc.tensor.matmul(ps, k.const("ident"), causal[qt], start=False, stop=True)

    attention(k, 4, 2, queries("aq"), score, lambda b, hh, kt: k.va[:, kt, bass.ds(b * P, P)], P,
              lambda b: one(k.y, b), difference=k.minus_lam)
    scaled_gains(k, 1.0 - lambda_init(l), [f"diff{l}"])
    norm_heads(k, k.y, P, 4, LAT, k.const("ones"), column(k.vec, k.vec_at[f"diff{l}"]), scale=1.0 / P, eps=k.eps5)

    def score(ps, b, hh, qt):
        logits(ps, "bq", hh, qt, b * 2 + (HEAD_AT["bk"] + hh))
        return nc.tensor.matmul(ps, k.const("ident"), causal[qt], start=False, stop=True)

    attention(k, 2, 2, queries("bq"), score, lambda b, hh, kt: k.bv[:, kt, bass.ds(b * P + hh * HD, HD)], HD,
              lambda b: one(k.y, b + 4))

    score_keys(k)
    stick_breaking(k)


    def score(ps, b, hh, qt):
        logits(ps, "dq", hh, qt, b * 2 + (HEAD_AT["dk"] + hh))
        return nc.tensor.matmul(ps, k.const("ident"), k.chosen[:, qt, :], start=False, stop=True)

    attention(k, 2, 2, queries("dq"), score, lambda b, hh, kt: k.dv[:, kt, bass.ds(b * P + hh * HD, HD)], HD,
              lambda b: one(k.selected, b))


def hybrid_mixer(k, l, gain):
    stack, sb = scoped(k, F32)
    with stack:
        k.normed = [sb(f"normed{n}", [P, KD, LAT], F32R) for n in range(2)]
        k.va = sb("values_a", [P, 2, 512])
        k.bv, k.cv, k.dv = (sb(f"values_{n}", [P, 2, 256]) for n in "bcd")
        k.y, k.selected = k.x[:, :, LAT:TOK], sb("selected", [P, 2, LAT])
        k.best, k.index_weight = sb("best", [P, 2, 8]), sb("index_weight", [P, 16])
        k.lam_exp, k.minus_lam, k.forget = sb("lam_exp", [P, 2]), sb("minus_lam", [P, 1]), sb("forget", [4, LAT])

        heads, sb = scoped(k, F32)
        with heads:
            k.heads = sb("heads", [P, N_HEADS2, LAT])
            projection, sb = scoped(k, F32R)
            with projection:
                part_buffers(k, sb, 2)
                splits = weight_parts(k, [k.spec(f"in_b{l}")], 2)
                norm_tokens(k, LAT, gain, dst=k.heads, parts=k.normed, splits=splits)
                project_heads(k, l, splits)
            inner, sb = scoped(k, F32)
            with inner:
                k.cum, k.ones_row = sb("cum", [4, LAT]), sb("ones_row", [4, LAT])
                k.chosen, k.score = sb("chosen", [P, 2, LAT]), sb("score", [P, 2, LAT])
                tiles = sb("probabilities", [P, 7, LAT])
                k.prob, k.prob_t = (lambda j, keys: tiles[:, j, 0:keys]), (lambda u, keys: tiles[:, 4 + u, 0:keys])
                k.out_rows = tiles[:, 6, :].rearrange("p (q e) -> p q e", q=2)
                second_attentions(k, l)

        products, sb = scoped(k, F32R)
        with products:
            part_buffers(k, sb, 2)
            k.merged = sb("merged", [P, KD, LAT], F32)
            merged_parts = [sb(f"merged_part{n}", [P, KD, LAT]) for n in range(2)]
            merge, out = k.spec(f"merge_b{l}"), k.spec(f"out_b{l}")
            splits = weight_parts(k, [merge, out], 2)
            merge_branches(k, l, splits)
            add_product_of_parts(k, out, LAT, k.merged, merged_parts, None, splits, merge.n)


def second_block(k, w):
    k.cos2, k.sin2 = k.r_stage[0:ROPE2, 0, :], k.r_stage[0:ROPE2, 1, :]
    k.selector = w["selector"].rearrange("j (h t) -> j h t", h=4)
    rope_tables(k)
    for l in (0, 1):
        for m in ("ffn1", "mix", "ffn2"):
            at_gain = k.vec_at[f"{m}_b{l}"]
            gain = lambda c, cond, at_gain=at_gain: column(k.vec, at_gain + c)
            if m == "mix":
                hybrid_mixer(k, l, gain)
            else:
                half_ffn(k, LAT, m, f"_b{l}", gain, None, 0.5)



def mixer_buffers(k):
    stack, sb = scoped(k, F32)
    k.mix = sb("mix", [P, KD, TOK])
    k.side = sb("side", [P, 4096])
    k.v, k.v_shared = sb("v", [P, 4, 512]), sb("v_shared", [P, 4, P])
    return stack


def head_buffers(k):
    stack, sb = scoped(k, F32)
    k.h, k.arena = sb("h", [P, KD, TOK]), sb("arena", [P, 12800])
    k.prob = lambda j, keys: k.h[:, j, TOK - keys:TOK]
    k.prob_t = lambda u, keys: k.h[:, 4 + u, TOK - keys:TOK]
    k.out_rows = k.h[:, 6, LAT:TOK].rearrange("p (q e) -> p q e", q=2)
    return stack


def program(nc, w, out):
    rows, vec_at = vector_rows()
    _, const_at = constant_table()
    with ExitStack() as ctx:
        def sb(name, shape, dt=F32):
            return ctx.enter_context(nc.sbuf_tensor(name, shape, dt))

        tallies = {}

        def tally(name):
            if name not in tallies:
                tallies[name] = Tally(ctx.enter_context(nc.semaphore(name)))
            return tallies[name]

        k = Shared()
        k.nc, k.tally = nc, tally
        k.vec_rows, k.vec_at, k.n_rows = rows, vec_at, sum(r[2] for r in rows)
        n_const = sum(n for _, _, n in const_at.values())
        k.consts = sb("consts", [P, n_const])
        k.const = lambda name: k.consts[0:const_at[name][0], const_at[name][1]:const_at[name][1] + const_at[name][2]]
        k.full = lambda name: k.consts[:, const_at[name][1]:const_at[name][1] + const_at[name][2]]
        k.vec = sb("vec", [P, 4 * P])
        k.eps, k.eps5, k.half_pi = sb("eps", [P, 1]), sb("eps5", [P, 1]), sb("half_pi", [P, 1])
        k.cond = sb("cond", [P, KD, 2])
        k.mod = sb("mod", [P, N_MOD * KD, 2])
        k.gain, k.gate = sb("gain", [P, 3, KD, 2]), sb("gate", [P, 2, KD, 2])
        k.lam = sb("lam", [P, 2, 4, HD])
        k.positions = sb("positions", [ROPE2, LAT], mybir.dt.int32)
        k.x = sb("x", [P, KD, TOK])
        k.slots = [sb(f"weights{s}", [P, SLOT]) for s in range(RING)]
        k.q_stage, k.r_stage = sb("q_stage", [P, 2, LAT]), sb("r_stage", [P, 2, LAT])
        k.negmax, k.rowsum, k.inverse = sb("negmax", [P, 4]), sb("rowsum", [P, 4]), sb("inverse", [P, 8])
        k.square, k.roots, k.rinvs = sb("square", [P, 2, TOK]), sb("roots", [P, 2, TOK]), sb("rinvs", [P, 2, TOK])
        k.root, k.rinv = k.roots[:, 0, :], k.rinvs[:, 0, :]
        k.psum = ctx.enter_context(nc.psum_tensor("psum", [P, 8, BANK], F32))
        k.weights_ready = [ctx.enter_context(nc.semaphore(f"weights_ready{s}")) for s in range(RING)]
        k.unit_done = ctx.enter_context(nc.semaphore("unit_done"))
        k.banks_free = ctx.enter_context(nc.semaphore("banks_free"))
        k.plan = weight_plan(w)
        k.spec = lambda name: next(s for s in k.plan if s.name == name)

        k.scope = 0
        with head_buffers(k):
            opening(k, w)
        for l in (0, 1):
            conditioning(k, l)
            tokens = TOK
            half_ffn(k, tokens, "ffn1", l, *modulated(k, 0), half_gate(k, 0))
            with mixer_buffers(k):
                with head_buffers(k):
                    norm_tokens(k, tokens, *modulated(k, 1))
                    if l == 0:
                        even_mixer(k)
                    else:
                        odd_mixer(k, w)
                        tokens = LAT
                products, sb = scoped(k, F32R)
                with products:
                    part_buffers(k, sb, 2)
                    parts = [sb(f"mixed_part{n}", [P, KD, tokens]) for n in range(2)]
                    add_product_of_parts(k, k.spec(f"out{l}"), tokens, k.mix, parts, mix_gate(k))
            half_ffn(k, tokens, "ffn2", l, *modulated(k, 2), half_gate(k, 1))
        second_block(k, w)
        with head_buffers(k):
            norm_tokens(k, LAT, lambda c, cond: column(k.vec, vec_at["final"] + c))
            ending(k, out)



def kernel(**inputs):
    import concourse.bacc as bacc
    from concourse.bass_utils import run_bass_kernel_spmd

    nc = bacc.Bacc("TRN2", target_bir_lowering=False, num_devices=1)
    arrays, w = {}, {}
    for name, value in {**inputs, "constants": constant_table()[0], "selector": selector()}.items():
        a = np.ascontiguousarray(value)
        arrays["in_" + name] = a
        w[name] = nc.dram_tensor("in_" + name, a.shape, mybir.dt.from_np(a.dtype), kind="ExternalInput").ap()
    out = nc.dram_tensor("out", (1, LAT, D), F32, kind="ExternalOutput").ap()
    program(nc, w, out)
    return run_bass_kernel_spmd(nc, [arrays], core_ids=[0]).results[0]["out"]
```
